# Optimizing a Trainium2 kernel written in Bass

```python
import math
import jax, jax.numpy as jnp
from jax import lax
import numpy as np

D_MODEL = 2048
BATCH = 1
SEQ = 256
DEPTH = 2

N_MEM = 256
N_MIXERS = 2
HEAD_DIM = 128
EPS = 1e-6
X_HEADS = 4
X_WIDTH = X_HEADS * HEAD_DIM
BRANCH_WIDTH = D_MODEL - X_WIDTH
MIX_WIDTH = BRANCH_WIDTH + X_WIDTH
GLA_HEADS = 4
GLA_DV = BRANCH_WIDTH // GLA_HEADS
GLA_DK = GLA_DV // 2
GLA_KEY_WIDTH = GLA_HEADS * GLA_DK
GLA_GATE_RANK = 16
GLA_GATE_TEMP = 16.0
GLA_CHUNK = 64
NSA_HEADS = BRANCH_WIDTH // HEAD_DIM
NSA_GROUPS = 2
NSA_HPG = NSA_HEADS // NSA_GROUPS
NSA_KV_WIDTH = NSA_GROUPS * HEAD_DIM
N_BRANCH = 3
CMP_LEN = 32
CMP_STRIDE = 16
CMP_HIDDEN = 256
SLC_LEN = 64
SLC_TOPN = 16
WINDOW = 512
Q_BLOCK = 128
FORCED = 1e4

GLA_SIZES = [GLA_KEY_WIDTH, GLA_KEY_WIDTH, BRANCH_WIDTH, GLA_GATE_RANK, BRANCH_WIDTH, X_WIDTH, X_WIDTH]
NSA_SIZES = [BRANCH_WIDTH] + [NSA_KV_WIDTH] * 6 + [NSA_HEADS * N_BRANCH, BRANCH_WIDTH, X_WIDTH, X_WIDTH]
GLA_IN = sum(GLA_SIZES)
NSA_IN = sum(NSA_SIZES)
N_GLA_LAYERS = (DEPTH + 1) // 2
N_NSA_LAYERS = DEPTH // 2

kernel_name = 'hybrid_gla_nsa_memxattn'

def rmsnorm(x, g):
    xf = x.astype(jnp.float32)
    y = xf * lax.rsqrt(jnp.mean(xf * xf, axis=-1, keepdims=True) + EPS)
    return (y * g.astype(jnp.float32)).astype(x.dtype)

def split_cols(a, sizes):
    return jnp.split(a, np.cumsum(sizes)[:-1].tolist(), axis=-1)

def masked_softmax(s, mask):
    p = jax.nn.softmax(jnp.where(mask, s, -1e30), axis=-1)
    return jnp.where(mask, p, 0.0)

def mem_cross_attention(xq, mem_n, w_kv):
    B, T, _ = xq.shape
    M = mem_n.shape[1]
    k, v = jnp.split(mem_n @ w_kv, 2, axis=-1)
    q = xq.reshape(B, T, X_HEADS, HEAD_DIM)
    k = k.reshape(B, M, X_HEADS, HEAD_DIM)
    v = v.reshape(B, M, X_HEADS, HEAD_DIM)
    s = jnp.einsum('bthd,bmhd->bhtm', q, k).astype(jnp.float32) * HEAD_DIM ** -0.5
    p = jax.nn.softmax(s, axis=-1).astype(v.dtype)
    return jnp.einsum('bhtm,bmhd->bthd', p, v).reshape(B, T, X_WIDTH)

def gla_chunk_scan(q, k, v, logg):
    B, T, H, DK = q.shape
    DV = v.shape[-1]
    C = GLA_CHUNK
    N = T // C

    def to_chunks(a):
        return a.reshape(B, N, C, H, a.shape[-1]).transpose(1, 0, 3, 2, 4)

    qc, kc, vc, gc = to_chunks(q), to_chunks(k), to_chunks(v), to_chunks(logg)
    causal = jnp.tril(jnp.ones((C, C), dtype=bool))[:, :, None]

    def step(S, inp):
        qi, ki, vi, gi = inp
        b = jnp.cumsum(gi, axis=2)
        b_last = b[:, :, -1:, :]
        diff = b[:, :, :, None, :] - b[:, :, None, :, :]
        decay = jnp.exp(jnp.where(causal, diff, -jnp.inf))
        attn = jnp.einsum('bhcd,bhsd,bhcsd->bhcs', qi, ki, decay)
        o = jnp.einsum('bhcd,bhde->bhce', qi * jnp.exp(b), S) + jnp.einsum('bhcs,bhse->bhce', attn, vi)
        S = jnp.exp(b_last[:, :, 0, :])[..., None] * S + jnp.einsum('bhsd,bhse->bhde', ki * jnp.exp(b_last - b), vi)
        return S, o

    S0 = jnp.zeros((B, H, DK, DV), jnp.float32)
    _, o = lax.scan(step, S0, (qc, kc, vc, gc))
    return o.transpose(1, 0, 3, 2, 4).reshape(B, T, H, DV)

def gla_mixer(h, mem_n, w_in, w_gate_lr, b_gate, g_norm, w_kv, w_out):
    B, T, _ = h.shape
    f32 = jnp.float32
    q, k, v, glr, r, xq, xg = split_cols(h @ w_in, GLA_SIZES)
    q = q.reshape(B, T, GLA_HEADS, GLA_DK).astype(f32) * GLA_DK ** -0.5
    k = k.reshape(B, T, GLA_HEADS, GLA_DK).astype(f32)
    v = v.reshape(B, T, GLA_HEADS, GLA_DV).astype(f32)
    logg = jax.nn.log_sigmoid((glr @ w_gate_lr + b_gate).astype(f32)) / GLA_GATE_TEMP
    logg = logg.reshape(B, T, GLA_HEADS, GLA_DK)
    o = gla_chunk_scan(q, k, v, logg)
    o = rmsnorm(o, g_norm).reshape(B, T, BRANCH_WIDTH).astype(h.dtype)
    y_seq = o * jax.nn.silu(r)
    y_mem = mem_cross_attention(xq, mem_n, w_kv) * jax.nn.silu(xg)
    return jnp.concatenate([y_seq, y_mem], axis=-1) @ w_out

def nsa_mixer(h, mem_n, w_in, pe_k, pe_v, wk1, wk2, wv1, wv2, w_kv, w_out):
    B, T, _ = h.shape
    dt = h.dtype
    f32 = jnp.float32
    G, HPG, HD = NSA_GROUPS, NSA_HPG, HEAD_DIM
    scale = HD ** -0.5
    q, kc, vc, ks, vs, kw, vw, gl, r, xq, xg = split_cols(h @ w_in, NSA_SIZES)
    q = q.reshape(B, T, G, HPG, HD)
    gates = jax.nn.sigmoid(gl.astype(f32)).reshape(B, T, G, HPG, N_BRANCH)
    kc, vc, ks, vs, kw, vw = [a.reshape(B, T, G, HD) for a in (kc, vc, ks, vs, kw, vw)]

    n_cmp = (T - CMP_LEN) // CMP_STRIDE + 1
    cidx = np.arange(n_cmp)[:, None] * CMP_STRIDE + np.arange(CMP_LEN)[None, :]

    def compress(a, pe, w1, w2):
        blocks = a[:, cidx] + pe[None, None, :, None, :]
        blocks = blocks.transpose(0, 1, 3, 2, 4).reshape(B, n_cmp, G, CMP_LEN * HD)
        return jax.nn.silu(blocks @ w1) @ w2

    k_cmp = compress(kc, pe_k, wk1, wk2)
    v_cmp = compress(vc, pe_v, wv1, wv2)
    cmp_end = jnp.asarray(cidx[:, -1])

    n_slc = T // SLC_LEN
    top_n = min(SLC_TOPN, n_slc)
    cstart = np.arange(n_cmp) * CMP_STRIDE
    sstart = np.arange(n_slc) * SLC_LEN
    overlap = jnp.asarray(((cstart[:, None] < sstart[None, :] + SLC_LEN) &
                           (cstart[:, None] + CMP_LEN > sstart[None, :])).astype(np.float32))
    k_sb = ks.reshape(B, n_slc, SLC_LEN, G, HD).transpose(0, 3, 1, 2, 4)
    v_sb = vs.reshape(B, n_slc, SLC_LEN, G, HD).transpose(0, 3, 1, 2, 4)

    kw_pad = jnp.pad(kw, ((0, 0), (WINDOW, 0), (0, 0), (0, 0)))
    vw_pad = jnp.pad(vw, ((0, 0), (WINDOW, 0), (0, 0), (0, 0)))

    n_qb = T // Q_BLOCK
    q_blocks = q.reshape(B, n_qb, Q_BLOCK, G, HPG, HD).transpose(1, 0, 2, 3, 4, 5)
    g_blocks = gates.reshape(B, n_qb, Q_BLOCK, G, HPG, N_BRANCH).transpose(1, 0, 2, 3, 4, 5)
    bi = jnp.arange(B)[:, None, None, None]
    gi = jnp.arange(G)[None, :, None, None]
    jblk = jnp.arange(n_slc)

    def block_fn(args):
        qb_idx, qb, gb = args
        start = qb_idx * Q_BLOCK
        t = start + jnp.arange(Q_BLOCK)
        s = jnp.einsum('bqghd,bngd->bghqn', qb, k_cmp).astype(f32) * scale
        p_cmp = masked_softmax(s, cmp_end[None, :] <= t[:, None])
        o_cmp = jnp.einsum('bghqn,bngd->bqghd', p_cmp.astype(dt), v_cmp)
        imp = jnp.einsum('bghqn,nj->bgqj', p_cmp, overlap)
        cur = t // SLC_LEN
        forced = (jblk[None, :] == 0) | (jblk[None, :] == cur[:, None]) | (jblk[None, :] == cur[:, None] - 1)
        imp = jnp.where(forced, FORCED, imp)
        imp = jnp.where(jblk[None, :] > cur[:, None], -FORCED, imp)
        _, sel = lax.top_k(imp, top_n)
        ksel = k_sb[bi, gi, sel].reshape(B, G, Q_BLOCK, top_n * SLC_LEN, HD)
        vsel = v_sb[bi, gi, sel].reshape(B, G, Q_BLOCK, top_n * SLC_LEN, HD)
        pos = (sel[..., None] * SLC_LEN + jnp.arange(SLC_LEN)).reshape(B, G, Q_BLOCK, top_n * SLC_LEN)
        s = jnp.einsum('bqghd,bgqkd->bghqk', qb, ksel).astype(f32) * scale
        p = masked_softmax(s, (pos <= t[None, None, :, None])[:, :, None])
        o_slc = jnp.einsum('bghqk,bgqkd->bqghd', p.astype(dt), vsel)
        kwin = lax.dynamic_slice_in_dim(kw_pad, start, Q_BLOCK + WINDOW, axis=1)
        vwin = lax.dynamic_slice_in_dim(vw_pad, start, Q_BLOCK + WINDOW, axis=1)
        wpos = start - WINDOW + jnp.arange(Q_BLOCK + WINDOW)
        m_win = (wpos[None, :] <= t[:, None]) & (wpos[None, :] > t[:, None] - WINDOW) & (wpos[None, :] >= 0)
        s = jnp.einsum('bqghd,bkgd->bghqk', qb, kwin).astype(f32) * scale
        p = masked_softmax(s, m_win)
        o_win = jnp.einsum('bghqk,bkgd->bqghd', p.astype(dt), vwin)
        o = gb[..., 0:1] * o_cmp + gb[..., 1:2] * o_slc + gb[..., 2:3] * o_win
        return o.astype(dt)

    o = lax.map(block_fn, (jnp.arange(n_qb), q_blocks, g_blocks))
    o = o.transpose(1, 0, 2, 3, 4, 5).reshape(B, T, BRANCH_WIDTH)
    y_seq = o * jax.nn.silu(r)
    y_mem = mem_cross_attention(xq, mem_n, w_kv) * jax.nn.silu(xg)
    return jnp.concatenate([y_seq, y_mem], axis=-1) @ w_out

def setup_inputs(seed: int = 0) -> dict:
    key = jax.random.key(seed)
    ks = jax.random.split(key, 20)
    f32 = jnp.float32

    def nrm(k, shape, scale):
        return jax.random.normal(k, shape, f32) * scale

    nA, nB = N_GLA_LAYERS, N_NSA_LAYERS
    return {
        'x': nrm(ks[0], (BATCH, SEQ, D_MODEL), 1.0),
        'mem': nrm(ks[1], (BATCH, N_MEM, D_MODEL), 1.0),
        'ln_pre': 1.0 + nrm(ks[2], (DEPTH, D_MODEL), 0.02),
        'ln_post': 1.0 + nrm(ks[3], (DEPTH, D_MODEL), 0.02),
        'ln_mem': 1.0 + nrm(ks[4], (DEPTH, D_MODEL), 0.02),
        'w_mem_kv': nrm(ks[5], (DEPTH, D_MODEL, 2 * X_WIDTH), D_MODEL ** -0.5),
        'gla_w_in': nrm(ks[6], (nA, D_MODEL, GLA_IN), D_MODEL ** -0.5),
        'gla_w_gate_lr': nrm(ks[7], (nA, GLA_GATE_RANK, GLA_KEY_WIDTH), GLA_GATE_RANK ** -0.5),
        'gla_b_gate': nrm(ks[8], (nA, GLA_KEY_WIDTH), 0.1),
        'gla_norm': 1.0 + nrm(ks[9], (nA, GLA_DV), 0.02),
        'gla_w_out': nrm(ks[10], (nA, MIX_WIDTH, D_MODEL), MIX_WIDTH ** -0.5),
        'nsa_w_in': nrm(ks[11], (nB, D_MODEL, NSA_IN), D_MODEL ** -0.5),
        'nsa_pe_k': nrm(ks[12], (nB, CMP_LEN, HEAD_DIM), 0.1),
        'nsa_pe_v': nrm(ks[13], (nB, CMP_LEN, HEAD_DIM), 0.1),
        'nsa_wk1': nrm(ks[14], (nB, CMP_LEN * HEAD_DIM, CMP_HIDDEN), (CMP_LEN * HEAD_DIM) ** -0.5),
        'nsa_wk2': nrm(ks[15], (nB, CMP_HIDDEN, HEAD_DIM), CMP_HIDDEN ** -0.5),
        'nsa_wv1': nrm(ks[16], (nB, CMP_LEN * HEAD_DIM, CMP_HIDDEN), (CMP_LEN * HEAD_DIM) ** -0.5),
        'nsa_wv2': nrm(ks[17], (nB, CMP_HIDDEN, HEAD_DIM), CMP_HIDDEN ** -0.5),
        'nsa_w_out': nrm(ks[18], (nB, MIX_WIDTH, D_MODEL), MIX_WIDTH ** -0.5),
    }

def reference(x, mem, ln_pre, ln_post, ln_mem, w_mem_kv, gla_w_in, gla_w_gate_lr, gla_b_gate, gla_norm, gla_w_out,
              nsa_w_in, nsa_pe_k, nsa_pe_v, nsa_wk1, nsa_wk2, nsa_wv1, nsa_wv2, nsa_w_out):
    h = x
    for i in range(DEPTH):
        xn = rmsnorm(h, ln_pre[i])
        mem_n = rmsnorm(mem, ln_mem[i])
        a = i // N_MIXERS
        if i % N_MIXERS == 0:
            y = gla_mixer(xn, mem_n, gla_w_in[a], gla_w_gate_lr[a], gla_b_gate[a], gla_norm[a], w_mem_kv[i], gla_w_out[a])
        else:
            y = nsa_mixer(xn, mem_n, nsa_w_in[a], nsa_pe_k[a], nsa_pe_v[a], nsa_wk1[a], nsa_wk2[a], nsa_wv1[a], nsa_wv2[a],
                          w_mem_kv[i], nsa_w_out[a])
        h = h + rmsnorm(y, ln_post[i])
    return h


_drawn_inputs = setup_inputs


def setup_inputs(seed=0):
    import zlib

    import numpy as np

    out = dict(_drawn_inputs(seed))
    spreads = {}
    factors = {'ln_post': 2.717,
     'ln_mem': 8.0,
     'gla_norm': 3.292,
     'nsa_pe_k': 48.144,
     'nsa_pe_v': 8.0,
     'nsa_wk1': 5.462,
     'nsa_wk2': 5.313}
    for name, (base, spread) in spreads.items():
        noise = np.random.default_rng([zlib.crc32(name.encode()), seed]).standard_normal(out[name].shape)
        drawn = base * np.exp(spread * noise) if base else spread * noise
        out[name] = __import__('jax').numpy.asarray(drawn.astype(out[name].dtype))
    for name, factor in factors.items():
        out[name] = (out[name] * factor).astype(out[name].dtype)
    return out
```

```python
import concourse.bass as bass
from concourse import mybir
from contextlib import ExitStack

P = 128
D_MODEL, SEQ, N_MEM = 2048, 256, 256
KT = D_MODEL // P
TT = SEQ // P
HD = 128
X_HEADS = 4
XW = X_HEADS * HD
BW = D_MODEL - XW
GLA_HEADS, GLA_DV = 4, BW // 4
GLA_DK = GLA_DV // 2
KEYW = GLA_HEADS * GLA_DK
FT = KEYW // P
RANK = 16
GATE_TEMP = 16.0
NSA_HEADS, NSA_GROUPS = BW // HD, 2
HPG = NSA_HEADS // NSA_GROUPS
KVW = NSA_GROUPS * HD
N_BRANCH = 3
CMP_LEN, CMP_STRIDE, CMP_HIDDEN = 32, 16, 256
N_CMP = (SEQ - CMP_LEN) // CMP_STRIDE + 1
NB = NSA_GROUPS * N_CMP
EPS = 1e-6
LEVELS = 8
MASKED = -1e30
ATT_SCALE = float(HD) ** -0.5
GLA_SCALE = float(GLA_DK) ** -0.5

RING = 4
PIECE = 1024
LEAD = RING - 1

TM, FM, MIX, NARROW, CMP = "token-major", "feature-major", "both", "narrow", "compress"


class Chunk:

    def __init__(self, name, kind, w, col, width, lhs):
        self.name, self.kind, self.w, self.col, self.width, self.lhs = name, kind, w, col, width, lhs
        self.tiles = {NARROW: KT, CMP: PIECE // CMP_HIDDEN}.get(kind, PIECE // 512)
        self.n = {CMP: CMP_LEN}.get(kind, KT) // self.tiles


def chunk_list():
    g, n = "gla_w_in", "nsa_w_in"
    gq, gv, gl = 0, 2 * KEYW, 2 * KEYW + BW
    gr = gl + RANK
    nk = BW
    ng = BW + 6 * KVW
    nr = ng + NSA_HEADS * N_BRANCH
    out = []
    for i, act in ((0, "A"), (1, "B")):
        out.append(Chunk(f"mem_k{i}", FM, f"kv{i}", 0, XW, act))
        out.append(Chunk(f"mem_v{i}", TM, f"kv{i}", XW, XW, act))
    out.append(Chunk("g_lr", NARROW, g, gl, RANK, "A"))
    out += [Chunk(f"g_qk{j}", FM, g, gq + 512 * j, 512, "A") for j in range(3)]
    out += [Chunk(f"g_v{j}", TM, g, gv + 512 * j, 512, "A") for j in range(3)]
    out.append(Chunk("g_xq", FM, g, gr + BW, XW, "A"))
    out.append(Chunk("g_r0", TM, g, gr, 512, "A"))
    out.append(Chunk("g_xg", TM, g, gr + BW + XW, XW, "A"))
    out += [Chunk(f"g_r{j}", TM, g, gr + 512 * j, 512, "A") for j in (1, 2)]
    out += [Chunk(f"g_out{j}", TM, "gla_w_out", 512 * j, 512, "B") for j in range(4)]
    out.append(Chunk("n_gl", NARROW, n, ng, NSA_HEADS * N_BRANCH, "A"))
    out.append(Chunk("n_cmp", FM, n, nk, 2 * KVW, "A"))
    out.append(Chunk("n_slc", MIX, n, nk + 2 * KVW, 2 * KVW, "A"))
    out.append(Chunk("n_win", MIX, n, nk + 4 * KVW, 2 * KVW, "A"))
    out.append(Chunk("n_wk1", CMP, "nsa_wk1", 0, CMP_HIDDEN, "K"))
    out.append(Chunk("n_wv1", CMP, "nsa_wv1", 0, CMP_HIDDEN, "V"))
    out += [Chunk(f"n_q{j}", FM, n, 512 * j, 512, "A") for j in range(3)]
    out.append(Chunk("n_xq", FM, n, nr + BW, XW, "A"))
    out.append(Chunk("n_xg", TM, n, nr + BW + XW, XW, "A"))
    out += [Chunk(f"n_r{j}", TM, n, nr + 512 * j, 512, "A") for j in range(3)]
    out += [Chunk(f"n_out{j}", TM, "nsa_w_out", 512 * j, 512, "B") for j in range(4)]
    n0 = 0
    for c, ch in enumerate(out):
        ch.c, ch.first, ch.last = c, n0, n0 + ch.n - 1
        n0 += ch.n
    return out, n0


def hybrid_trunk(nc, a, out):
    f32, f32r, bf16, i32 = mybir.dt.float32, mybir.dt.float32r, mybir.dt.bfloat16, mybir.dt.int32
    ALU, ACT, AX = mybir.AluOpType, mybir.ActivationFunctionType, mybir.AxisListType

    chunks, pieces = chunk_list()
    C = {ch.name: ch for ch in chunks}
    piece_of = [(ch, j) for ch in chunks for j in range(ch.n)]
    weights = {"kv0": a["w_mem_kv"][0], "kv1": a["w_mem_kv"][1], "gla_w_in": a["gla_w_in"][0],
               "gla_w_out": a["gla_w_out"][0], "nsa_w_in": a["nsa_w_in"][0], "nsa_w_out": a["nsa_w_out"][0],
               "nsa_wk1": a["nsa_wk1"][0], "nsa_wv1": a["nsa_wv1"][0]}

    base = (nc.sbuf_base + 31) // 32 * 32
    top = [0]

    def at(name, shape, dt, off):
        return nc.alloc_sbuf_tensor_at(name, [shape[0], *shape[1:]], dt, offset=base + off)

    def region(size):
        off = top[0]
        top[0] += (size + 31) // 32 * 32
        assert base + top[0] <= nc.sbuf_usable_end, top[0]
        return off

    def new(name, shape, dt):
        n = 4 if dt != bf16 else 2
        for s in shape[1:]:
            n *= s
        return at(name, shape, dt, region(n))

    RAW = new("weights_raw", [P, RING, PIECE], f32)
    WHI = new("weights_high", [P, RING, PIECE], f32r)
    WLO = new("weights_low", [P, RING, PIECE], f32r)
    AHI = new("act_a_high", [P, KT, SEQ], f32r)
    ALO = new("act_a_low", [P, KT, SEQ], f32r)
    b_off = region(2 * KT * SEQ * 4)
    BHI = at("act_b_high", [P, KT, SEQ], f32r, b_off)
    BLO = at("act_b_low", [P, KT, SEQ], f32r, b_off + KT * SEQ * 4)
    h_off = region(TT * D_MODEL * 4)
    H = at("stream", [P, TT, D_MODEL], f32, h_off)
    m_off = region(2 * TT * BW * 4)
    y_off = region(TT * D_MODEL * 4)
    Y = at("mixed", [P, TT, D_MODEL], f32, y_off)
    XQT = new("xattn_q", [P, X_HEADS, SEQ], f32)
    KX = [new(f"xattn_k{i}", [P, X_HEADS, N_MEM], f32) for i in range(2)]
    VX = [new(f"xattn_v{i}", [P, TT, XW], f32) for i in range(2)]
    SG = new("gate_sigmoid", [P, TT, 512], f32)
    IDENT = new("identity", [P, P], f32)
    GT = new("gains_transposed", [P, 4 * KT], f32)
    gla_off = region(9 * P * 4 + 7 * 64 * 4 + 2 * 3 * P * 4 + GLA_DV * 4)
    ST = new("stats", [P, 192], f32)

    LGH = at("log_gate_high", [P, TT, KEYW], f32r, h_off)
    LGL = at("log_gate_low", [P, TT, KEYW], f32r, h_off + TT * KEYW * 4)
    PX = at("xattn_probs", [P, 2, 512], f32, h_off + 2 * TT * KEYW * 4)
    QK = at("gla_qk", [P, 2 * FT, SEQ], f32, m_off)
    V = at("gla_v", [P, TT, BW], f32, m_off + 2 * FT * SEQ * 4)
    E = at("gla_decayed", [P, LEVELS, 3, SEQ], f32, b_off)
    QKP = at("gla_qk_product", [P, FT, SEQ], f32, b_off + LEVELS * 3 * SEQ * 4)
    WG = at("gate_weights", [RANK + 1, KEYW], f32, y_off)
    GLT = at("gate_rank_t", [RANK + 1, SEQ], f32, y_off + KEYW * 4)
    GLR = at("gate_rank", [P, TT, 64], f32, y_off + KEYW * 4 + 1024)
    ZA = at("gate_abs", [P, KEYW], f32, y_off + KEYW * 4 + 1536)
    ZL = at("gate_log", [P, KEYW], f32, y_off + 2 * KEYW * 4 + 1536)
    ZG = at("gate_sum", [P, KEYW], f32, y_off + 3 * KEYW * 4 + 1536)
    PATTERN = at("decay_patterns", [P, 9, P], f32r, gla_off)
    LMASK = at("level_masks", [P, 7, 64], i32, gla_off + 9 * P * 4)
    AT = at("gla_attn_t", [P, 2, 3, P], f32, gla_off + 9 * P * 4 + 7 * 64 * 4)
    GN = at("gla_norm_rows", [P, GLA_DV], f32, gla_off + 9 * P * 4 + 7 * 64 * 4 + 2 * 3 * P * 4)
    PT0 = at("xattn_probs_t", [P, 2, 512], f32, m_off)
    PAT0 = at("pattern_scratch", [P, 9, P], f32, b_off)
    MSK0 = at("mask_scratch", [P, 7, 64], f32, b_off + 9 * P * 4)

    NQT = at("nsa_q", [P, NSA_HEADS, SEQ], f32, m_off)
    NKT = at("nsa_k", [P, 2, NSA_GROUPS, SEQ], f32, m_off + NSA_HEADS * SEQ * 4)
    NV = at("nsa_v", [P, 2, TT, KVW], f32, m_off + NSA_HEADS * SEQ * 4 + 4096)
    KVC = at("nsa_cmp_kv", [P, 2, NSA_GROUPS, SEQ], f32, m_off + NSA_HEADS * SEQ * 4 + 8192)
    BKH = at("cmp_blocks_high", [P, 2, CMP_LEN, NB], f32r, b_off)
    BKL = at("cmp_blocks_low", [P, 2, CMP_LEN, NB], f32r, b_off + 7680)
    BKT = at("cmp_blocks", [P, CMP_LEN, NB], f32, b_off + 15360)
    W2 = at("cmp_w2", [P, 2, 2, HD], f32, b_off + 19200)
    HID = at("cmp_hidden", [P, 2, 2, 32], f32, b_off + 21248)
    HSG = at("cmp_hidden_sigmoid", [P, 2, 2, 32], f32, b_off + 21760)
    KC = at("cmp_k", [P, 32], f32, b_off + 22272)
    VC = at("cmp_v", [N_CMP, NSA_GROUPS, HD], f32, b_off + 22400)
    PC = at("cmp_probs", [P, 3, 8, 16], f32, b_off + 23424)
    PTC = at("cmp_probs_t", [16, 2, 256], f32, b_off + 24960)
    GATES = at("nsa_gates", [P, TT, 64], f32, b_off + 27008)
    PE0 = at("cmp_pe", [CMP_LEN, 2, HD], f32, b_off + 27520)
    PET = at("cmp_pe_t", [P, 2, CMP_LEN], f32, b_off + 28544)
    CB = at("causal_bias", [P, P], bf16, gla_off)
    IDB = at("identity_bf16", [P, P], bf16, gla_off + 256)
    CMB = at("cmp_bias", [P, TT, 16], bf16, gla_off + 512)
    ROWOK = at("cmp_row_visible", [P, TT], f32, gla_off + 576)
    PN = at("nsa_probs", [P, 2, 512], f32, gla_off + 608)
    PT1 = at("nsa_probs_t", [P, 2, 512], f32, gla_off + 608 + 4096)
    GPOST = [at(f"post_gain{i}", [P, D_MODEL], f32, m_off + 4096) for i in range(2)]
    G0 = at("gains_raw", [4 * KT, P], f32, m_off)
    JUNK = at("squares", [P, D_MODEL], f32, m_off + 12288 + 2048)

    SS = ST[:, 0:16]
    RSTD = ST[:, 16:32]
    NM = ST[:, 32:36]
    RS = ST[:, 36:40]
    RI = ST[:, 40:44]
    MX = ST[:, 44:48]
    SSG = ST[:, 48:56]
    RG = ST[:, 56:64]
    DQ = ST[:, 64:72]
    MC = ST[:, 72:96]
    SC = ST[:, 96:120]
    FC = ST[:, 120:144]
    ONES = ST[:, 144:145]
    HALF = ST[:, 160:168]

    ctx = ExitStack()
    with ctx:
        PS = [ctx.enter_context(nc.psum_tensor(f"bank{i}", [P, 512], f32)) for i in range(8)]

        def sem(name):
            return ctx.enter_context(nc.semaphore(name))

        raw_in = [sem(f"raw_piece_in{i}") for i in range(RING)]
        hi_ready, lo_ready, piece_used = sem("high_ready"), sem("low_ready"), sem("piece_used")
        act_drained, dve_drained = sem("drained_by_scalar"), sem("drained_by_vector")
        mem_in = [sem(f"mem_in{i}") for i in range(2)]
        x_in = [sem(f"x_in{i}") for i in range(2)]
        gains_in, wg_in, gn_in, res_in = sem("gains_in"), sem("gate_weights_in"), sem("gla_norm_in"), sem("residual_in")
        w2_in, pe_in = sem("cmp_w2_in"), sem("cmp_pe_in")
        post_in = [sem(f"post_gain_in{i}") for i in range(2)]
        stored = sem("stored")
        consts, consts2 = sem("constants_ready"), sem("nsa_constants_ready")
        pool_step, dve_step, act_step = sem("pool_step"), sem("vector_step"), sem("scalar_step")
        squared, normed = sem("squared"), sem("normed")
        mean_ready, rstd_ready = sem("mean_square"), sem("reciprocal_root")
        small_t, small_c = sem("small_transposed"), sem("small_copied")
        tr_ready, tr_hi, tr_lo = sem("transposed"), sem("transposed_high"), sem("transposed_low")
        z_ready, z_exp, lg_ready = sem("gate_logits"), sem("gate_ln"), sem("log_gates")
        d_ready, e_ready, qk_ready = sem("decay_logs"), sem("decays"), sem("decayed")
        qkp_ready, dq_ready, dq_kept = sem("qk_products"), sem("qk_sums"), sem("qk_sums_kept")
        s_ready, at_ready = sem("gla_scores"), sem("gla_attn")
        o_ready, o_kept, o_sq, o_norm = sem("gla_out"), sem("gla_out_kept"), sem("gla_out_squared"), sem("gla_out_normed")
        sc_ready, mx_ready, pr_ready, pn_ready = sem("scores"), sem("maxima"), sem("probs"), sem("probs_scaled")
        pt_ready, pt_kept, pv_ready, head_kept = sem("probs_t"), sem("probs_t_kept"), sem("pv_done"), sem("head_kept")
        cs_ready, cs_shift, cs_exp, cs_done = sem("cmp_scores"), sem("cmp_shifted"), sem("cmp_exps"), sem("cmp_probs_done")
        blk_ready, hid_exp, hid_ready = sem("cmp_blocks_ready"), sem("hidden_exps"), sem("hidden_ready")
        kvc_ready, kvc_kept = sem("cmp_kv_ready"), sem("cmp_kv_kept")
        gate_exp, gate_ready, mixed_gated = sem("gate_exps"), sem("gates_ready"), sem("mixed_gated")
        sg_exp = sem("sigmoid_exps")
        y_sq, res_ready = sem("projected_squared"), sem("residual_ready")

        steps = {}

        def put(slot, *step):
            steps.setdefault(slot, []).append(step)

        t_base = {"mem": 0, "x0": KT, "y0": 2 * KT, "x1": 3 * KT, "y1": 4 * KT}

        for ch in chunks:
            if ch.name[2:4] in ("r0", "r1", "r2", "xg"):
                put(ch.last, "gated_drain", ch)
            elif ch.kind == CMP:
                put(ch.last, "hidden_drain", ch)
            else:
                put(ch.last, "drain", ch)
        put(4, "square", 1)
        for kt in range(KT):
            put(C["mem_k1"].first + 2 + kt // 2, "transpose", "x0", kt)
        q0 = C["g_lr"].last
        put(q0, "rank_t")
        put(q0 + 1, "gate", 0)
        put(q0 + 2, "gate", 1)
        for d in range(12):
            put(q0 + 4 + d, "decay", 0, d)
        k0 = C["g_qk2"].last
        put(k0, "qk_sums")
        for l in range(LEVELS):
            put(k0 + 1 + l, "decayed", 0, l)
        s0 = k0 + LEVELS + 1
        for h in (0, 1):
            put(s0 + 2 * h, "gla_scores", h, 0)
            put(s0 + 2 * h + 1, "gla_scores", h, 1)
            o0 = max(s0 + 2 * h + 2, C[f"g_v{(384 * h + 383) // 512}"].last + 1)
            put(o0, "gla_out", h)
        s1 = max(s0 + 4, o0 + 1)
        for d in range(12):
            put(s1 + d, "decay", 1, d)
        for l in range(LEVELS):
            put(s1 + 6 + l + (1 if l >= 4 else 0), "decayed", 1, l)
        s2 = s1 + 15
        for h in (2, 3):
            put(s2 + 2 * (h - 2), "gla_scores", h, 0)
            put(s2 + 2 * (h - 2) + 1, "gla_scores", h, 1)
            o0 = max(s2 + 2 * (h - 2) + 2, C[f"g_v{(384 * h + 383) // 512}"].last + 1)
            put(o0, "gla_out", h)
        put(o0 + 1, "gla_norm")
        ax = o0 + 2
        t_unit = 0
        s_uses = []
        tables = dict(units=[], attn=[])
        for h in range(X_HEADS):
            put(ax + h, "scores", ("x", 0, h), len(tables["attn"]))
            s_uses.append(("attn", len(tables["attn"])))
            put(ax + h + 1, "probs_t", ("x", 0, h), t_unit, len(tables["attn"]))
            put(ax + h + 2, "pv", ("x", 0, h), t_unit, len(tables["attn"]))
            tables["attn"].append(t_unit)
            t_unit += 1
        put(C["g_out0"].first - 1, "y_order")
        for kt in list(range(12, 16)) + list(range(0, 12)):
            put(C["g_out0"].first - 1, "transpose", "y0", kt)
        put(C["g_out3"].last, "residual", 0)
        for kt in range(KT):
            put(C["g_out3"].last, "transpose", "x1", kt)
        put(C["n_gl"].last, "nsa_gates")
        put(C["n_gl"].last, "pe_t")
        put(C["n_cmp"].last + 1, "blocks", 0)
        put(C["n_cmp"].last + 3, "blocks", 1)
        put(C["n_wk1"].last + 1, "cmp_kv", 0)
        put(C["n_wv1"].last + 1, "cmp_kv", 1)
        for j in range(3):
            u0 = C[f"n_q{j}"].last + 1
            put(u0, "cmp_scores", j)
            s_uses.append(("cmp", j))
            u = u0 + 1
            for h in range(4 * j, 4 * j + 4):
                for br in (0, 1, 2):
                    unit = ("cmp", 1, h) if br == 0 else ("nsa", br - 1, h)
                    at_i = len(tables["attn"])
                    if br:
                        put(u, "scores", unit, at_i)
                        s_uses.append(("attn", at_i))
                        tables["attn"].append(t_unit)
                        put(u + 1, "probs_t", unit, t_unit, at_i)
                        put(u + 2, "pv", unit, t_unit, at_i)
                        u += 1
                    else:
                        put(u + 1, "probs_t", unit, t_unit, None)
                        put(u + 2, "pv", unit, t_unit, None)
                    t_unit += 1
        ux = max(u + 1, C["n_xq"].last + 1)
        for h in range(X_HEADS):
            at_i = len(tables["attn"])
            put(ux + h, "scores", ("x", 1, h), at_i)
            s_uses.append(("attn", at_i))
            tables["attn"].append(t_unit)
            put(ux + h + 1, "probs_t", ("x", 1, h), t_unit, at_i)
            put(ux + h + 2, "pv", ("x", 1, h), t_unit, at_i)
            t_unit += 1
        for kt in list(range(12, 16)) + list(range(0, 12)):
            put(C["n_out0"].first - 1, "transpose", "y1", kt)
        put(C["n_out3"].last, "residual", 1)

        def last_slot(kind, test):
            return max(s for s, l in steps.items() for st in l if st[0] == kind and test(st))

        ready0 = last_slot("pv", lambda st: st[1][0] == "x" and st[1][1] == 0)
        ready1 = last_slot("pv", lambda st: st[1][1] == 1 and st[1][0] == "x")
        assert ready0 <= C["g_xg"].last and ready1 <= C["n_xg"].last, (ready0, C["g_xg"].last, ready1, C["n_xg"].last)

        slots = list(range(-1, pieces))
        seq = [st for s in slots for st in steps.get(s, ())]
        drained_at = {}
        for st in seq:
            if "drain" in st[0]:
                assert st[1].c == len(drained_at)
                drained_at[st[1].c] = True
        t_order = {}
        for st in seq:
            if st[0] == "transpose":
                t_order[st[1:]] = len(t_order) + KT
        units = [st for st in seq if st[0] == "probs_t"]
        assert [u[2] for u in units] == list(range(t_unit))
        heads = []
        for u in units:
            key = (u[1][0] == "x", u[1][1] if u[1][0] == "x" else 1, u[1][2])
            if key not in heads:
                heads.append(key)

        def head_no(unit):
            return heads.index((unit[0] == "x", unit[1] if unit[0] == "x" else 1, unit[2]))

        def t_source(stage):
            return {"mem": Y, "x0": H, "y0": Y, "x1": Y, "y1": Y}[stage]

        def t_dest(stage):
            return {"mem": [(AHI, ALO, 2 * KT), (BHI, BLO, 3 * KT)], "x0": [(AHI, ALO, 0)], "y0": [(BHI, BLO, None)],
                    "x1": [(AHI, ALO, KT)], "y1": [(BHI, BLO, None)]}[stage]

        def lhs_ready(ch):
            return {"m": KT, "g": 2 * KT, "n": 4 * KT}[ch.name[0]] + (KT if "out" in ch.name else 0)

        def lhs_free(stage):
            return {"x0": "mem_v0", "y0": "mem_v1", "x1": "g_r2", "y1": "g_out3"}[stage]

        def piece_view(buf, n):
            ch, j = piece_of[n]
            return buf[:, n % RING, 0:ch.tiles * ch.width].rearrange("p (t w) -> p t w", t=ch.tiles)

        def acc_bank(ch, i):
            return PS[2 * (ch.c % 2) + i]

        def unit_probs(unit):
            return (PX, PT0) if unit[:2] == ("x", 0) else (PN, PT1)

        def decay_unit(p, d):
            g, rest = divmod(d, 6)
            ft, i = divmod(rest, 2)
            return g, ft, i

        def head_rows(h):
            t0 = 3 * (h // 2)
            return [(t0, 0, P), (t0 + 1, 0, 64)] if h % 2 == 0 else [(t0 + 2, 0, P), (t0 + 1, 64, P)]

        JUNK2 = at("squares2", [P, D_MODEL], f32, m_off + 12288 + 64)

        gated_names = ["g_r0", "g_xg", "g_r1", "g_r2", "n_xg", "n_r0", "n_r1", "n_r2"]

        def gated_no(ch):
            return gated_names.index(ch.name)

        block = ctx.enter_context(nc.Block())

        @block.sync
        def _(sp):
            def piece_in(n):
                ch, j = piece_of[n]
                if n >= RING:
                    sp.wait_ge(lo_ready, n - RING + 1)
                rows = weights[ch.w][j * ch.tiles * P:(j + 1) * ch.tiles * P, ch.col:ch.col + ch.width]
                sp.dma_start(piece_view(RAW, n), rows.rearrange("(t p) w -> p t w", p=P)).then_inc(raw_in[n % RING], 16)

            for i in range(TT):
                sp.dma_start(Y[:, i, :], a["mem"][0, i * P:(i + 1) * P, :]).then_inc(mem_in[i], 16)
            for g, name in enumerate(("ln_pre", "ln_mem")):
                sp.dma_start(G0[2 * KT * g:2 * KT * (g + 1), :],
                             a[name].rearrange("l (t p) -> (l t) p", p=P)).then_inc(gains_in, 16)
            for n in range(LEAD):
                piece_in(n)
            for i in range(TT):
                sp.dma_start(H[:, i, :], a["x"][0, i * P:(i + 1) * P, :]).then_inc(x_in[i], 16)
            sp.dma_start(GN[:, :], a["gla_norm"][0:1, :].to_broadcast([P, GLA_DV])).then_inc(gn_in, 16)
            for s in range(0, pieces):
                if s + LEAD < pieces:
                    piece_in(s + LEAD)
                for st in steps.get(s - LEAD, ()) if s >= LEAD else ():
                    pass
                if s == 2:
                    sp.wait_ge(tr_lo, KT)
                    sp.dma_start(WG[0:RANK, :], a["gla_w_gate_lr"][0]).then_inc(wg_in, 16)
                    sp.dma_start(WG[RANK:RANK + 1, :], a["gla_b_gate"][0:1, :]).then_inc(wg_in, 16)
                if s == C["g_out0"].first + RING + 1:
                    sp.wait_ge(pt_ready, X_HEADS)
                    sp.wait_ge(pv_ready, X_HEADS)
                    sp.wait_ge(o_norm, GLA_HEADS)
                    for i in range(TT):
                        sp.dma_start(H[:, i, :], a["x"][0, i * P:(i + 1) * P, :]).then_inc(res_in, 16)
                    sp.dma_start(GPOST[0][:, :], a["ln_post"][0:1, :].to_broadcast([P, D_MODEL])).then_inc(post_in[0], 16)
                if s == C["n_gl"].first + RING:
                    sp.wait_ge(tr_lo, 4 * KT)
                    for g, w in enumerate(("nsa_wk2", "nsa_wv2")):
                        sp.dma_start(W2[:, g], a[w][0].rearrange("(t p) d -> p t d", p=P)).then_inc(w2_in, 16)
                    for g, w in enumerate(("nsa_pe_k", "nsa_pe_v")):
                        sp.dma_start(PE0[:, g, :], a[w][0]).then_inc(pe_in, 16)
                if s == C["n_out0"].first + RING + 1:
                    sp.wait_ge(pv_ready, t_unit)
                    sp.dma_start(GPOST[1][:, :], a["ln_post"][1:2, :].to_broadcast([P, D_MODEL])).then_inc(post_in[1], 16)
            for i in range(TT):
                sp.wait_ge(res_ready, TT + i + 1)
                sp.dma_start(out[0, i * P:(i + 1) * P, :], H[:, i, :]).then_inc(stored, 16)
            sp.wait_ge(stored, 16 * TT)

        @block.gpsimd
        def _(pool):
            count = [0]

            def step(ins):
                count[0] += 1
                ins.then_inc(pool_step, 1)
                pool.wait_ge(pool_step, count[0])

            def keep_where(view, value_of, pattern, base_, mult, fill):
                step(nc.gpsimd.affine_select(out=view, in_=view, compare_op=ALU.is_ge, fill=fill, base=base_,
                                             pattern=pattern, channel_multiplier=mult))

            powers = [0]

            def rstd(v):
                pool.wait_ge(mean_ready, powers[0] + 1)
                nc.gpsimd.tensor_tensor(v, v, HALF[:, 0:v.shape[1]], ALU.pow).then_inc(rstd_ready, 1)
                powers[0] += 1

            step(nc.gpsimd.memset(IDENT[:, :], 0.0))
            step(nc.gpsimd.affine_select(out=IDENT[:, :], in_=IDENT[:, :], compare_op=ALU.not_equal, fill=1.0, base=0,
                                         pattern=[[-1, P]], channel_multiplier=1))
            step(nc.gpsimd.memset(HALF, -0.5))
            nc.gpsimd.memset(ONES, 1.0).then_inc(consts, 1)
            for c in range(2 * TT):
                rstd(RSTD[:, c:c + 1])
            pool.wait_ge(tr_lo, KT + 0)
            pool.wait_ge(piece_used, C["mem_v1"].last + 1)
            step(nc.gpsimd.memset(PAT0[:, :, :], 1.0))
            step(nc.gpsimd.memset(MSK0[:, :, :], 1.0))
            for l in range(7):
                h = 1 << l
                v = PAT0[:, l, :].rearrange("p (b w o) -> p b w o", w=2, o=h)
                nb = P // (2 * h)
                keep_where(v[:, :, 0, :], None, [[-2 * h, nb], [-1, h]], -1, 1, 0.0)
                keep_where(v[:, :, 0, :], None, [[2 * h, nb], [0, h]], h - 1, -1, 0.0)
                keep_where(v[:, :, 1, :], None, [[-2 * h, nb], [0, h]], -h, 1, 0.0)
                keep_where(v[:, :, 1, :], None, [[2 * h, nb], [1, h]], h, -1, 0.0)
                m = MSK0[:, l, :].rearrange("p (b o) -> p b o", o=h)
                keep_where(m, None, [[-2 * h, nb], [0, h]], 0, 1, 0.0)
                keep_where(m, None, [[2 * h, nb], [0, h]], h - 1, -1, 0.0)
            keep_where(PAT0[:, 7, :], None, [[-1, P]], -1, 1, 0.0)
            keep_where(PAT0[:, 8, :], None, [[1, P]], 0, -1, 0.0)
            nc.gpsimd.tensor_copy(PATTERN[:, :, :], PAT0[:, :, :]).then_inc(consts, 1)
            nc.gpsimd.tensor_copy(LMASK[:, :, :], MSK0[:, :, :]).then_inc(consts, 1)
            nc.gpsimd.memset(AT[:, :, :, :], 0.0).then_inc(consts, 1)
            rstd(RG)
            pool.wait_ge(pv_ready, X_HEADS)
            pool.wait_ge(o_norm, GLA_HEADS)
            step(nc.gpsimd.memset(CB[:, :], 0.0))
            step(nc.gpsimd.memset(IDB[:, :], 0.0))
            step(nc.gpsimd.memset(CMB[:, :, :], 0.0))
            step(nc.gpsimd.memset(ROWOK[:, :], 1.0))
            keep_where(CB[:, :], None, [[-1, P]], 0, 1, MASKED)
            step(nc.gpsimd.affine_select(out=IDB[:, :], in_=IDB[:, :], compare_op=ALU.not_equal, fill=1.0, base=0,
                                         pattern=[[-1, P]], channel_multiplier=1))
            keep_where(CMB[:, :, :], None, [[P, TT], [-CMP_STRIDE, 16]], -(CMP_LEN - 1), 1, MASKED)
            keep_where(ROWOK[:, :], None, [[P, TT]], -(CMP_LEN - 1), 1, 0.0)
            nc.gpsimd.memset(ST[:, 153:154], 1.0).then_inc(consts2, 1)
            for c in (4, 5, 6, 7, 8, 9):
                rstd(RSTD[:, c:c + 1])

        @block.tensor
        def _(pe):
            def transpose(stage, kt, n):
                if n >= 4:
                    pe.wait_ge(tr_lo, n - 3)
                src = t_source(stage)
                for i in range(TT):
                    last = nc.tensor.transpose(PS[4 + n % 4][:, i * P:(i + 1) * P], src[:, i, kt * P:(kt + 1) * P], IDENT[:, :])
                last.then_inc(tr_ready, 1)

            def products(n):
                ch, j = piece_of[n]
                if j == 0:
                    if ch.c >= 2:
                        pe.wait_ge(act_drained, ch.c - 1)
                        pe.wait_ge(dve_drained, ch.c - 1)
                    if ch.kind == CMP:
                        pe.wait_ge(blk_ready, 1 if ch.lhs == "K" else 2)
                    else:
                        pe.wait_ge(tr_lo, lhs_ready(ch))
                pe.wait_ge(lo_ready, n + 1)
                hi, lo = piece_view(WHI, n), piece_view(WLO, n)
                last = None
                for t in range(ch.tiles):
                    kt = j * ch.tiles + t
                    first, end = kt == 0, j == ch.n - 1 and t == ch.tiles - 1
                    if ch.kind == CMP:
                        g = "KV".index(ch.lhs)
                        for half in range(2):
                            o = acc_bank(ch, 0)[:, 32 * half:32 * half + NB]
                            w = slice(half * P, (half + 1) * P)
                            for q, (wt, bt) in enumerate(((hi, BKH), (lo, BKH), (hi, BKL))):
                                last = nc.tensor.matmul(o, wt[:, t, w], bt[:, g, kt, :], start=first and half == 0 and q == 0,
                                                        stop=end and q == 2, skip_group_check=True)
                        continue
                    xh, xl = (AHI, ALO) if ch.lhs == "A" else (BHI, BLO)
                    outs = []
                    if ch.kind == TM:
                        outs = [(acc_bank(ch, i)[:, 0:ch.width], True, slice(0, ch.width), i) for i in range(TT)]
                    if ch.kind == NARROW:
                        outs = [(acc_bank(ch, 0)[:, 64 * i:64 * i + ch.width], i == 0, slice(0, ch.width), i) for i in range(TT)]
                    if ch.kind == FM:
                        outs = [(acc_bank(ch, b // 2)[:, b % 2 * SEQ:(b % 2 + 1) * SEQ], b % 2 == 0, slice(b * P, (b + 1) * P), None)
                                for b in range(4)]
                    if ch.kind == MIX:
                        outs = [(acc_bank(ch, 0)[:, b * SEQ:(b + 1) * SEQ], b == 0, slice(b * P, (b + 1) * P), None)
                                for b in range(2)]
                        outs += [(acc_bank(ch, 1)[:, i * KVW:(i + 1) * KVW], i == 0, slice(KVW, 2 * KVW), i) for i in range(TT)]
                    for o, opens, w, i in outs:
                        for q, (wt, xt) in enumerate(((hi, xh), (lo, xh), (hi, xl))):
                            ww = wt[:, t, w]
                            if i is None:
                                args = (ww, xt[:, kt, :])
                            else:
                                args = (xt[:, kt, i * P:(i + 1) * P], ww)
                            last = nc.tensor.matmul(o, *args, start=first and opens and q == 0, stop=end and q == 2,
                                                    skip_group_check=True)
                last.then_inc(piece_used, 1)

            def score_bank_free(s):
                if s >= 2:
                    kind, k = s_uses[s - 2]
                    if kind == "attn":
                        pe.wait_ge(pr_ready, k + 1)
                    else:
                        pe.wait_ge(cs_shift, k + 1)

            pe.wait_ge(consts, 1)
            pe.wait_ge(gains_in, 32)
            nc.tensor.transpose(PS[0][:, 0:4 * KT], G0[:, :], IDENT[0:4 * KT, 0:4 * KT]).then_inc(small_t, 1)
            pe.wait_ge(normed, TT)
            for kt in range(KT):
                transpose("mem", kt, kt)
            d_no = s_no = 0
            for s in slots:
                if s >= 0:
                    products(s)
                for st in steps.get(s, ()):
                    what = st[0]
                    if what == "transpose":
                        stage, kt = st[1:]
                        n = t_order[stage, kt]
                        if stage == "x0" and kt == 0:
                            pe.wait_ge(normed, 2 * TT)
                        if stage in ("y0", "y1") and kt == 12:
                            pe.wait_ge(mixed_gated, 4 * TT * (1 if stage == "y0" else 2))
                            pe.wait_ge(pv_ready, X_HEADS if stage == "y0" else t_unit)
                            pe.wait_ge(head_kept, X_HEADS if stage == "y0" else len(heads))
                        if stage == "x1" and kt == 0:
                            pe.wait_ge(normed, 3 * TT)
                        transpose(stage, kt, n)
                    elif what == "rank_t":
                        pe.wait_ge(act_drained, C["g_lr"].c + 1)
                        pe.wait_ge(tr_lo, 2 * KT)
                        for i in range(TT):
                            last = nc.tensor.transpose(PS[4][0:RANK, i * P:(i + 1) * P], GLR[:, i, 0:RANK], IDENT[:, :])
                        last.then_inc(small_t, 1)
                    elif what == "gate":
                        i, = st[1:]
                        pe.wait_ge(small_c, 2)
                        pe.wait_ge(wg_in, 32)
                        if i == 1:
                            pe.wait_ge(lg_ready, 1)
                        for k, (c0, w) in enumerate(((0, 512), (512, KEYW - 512))):
                            last = nc.tensor.matmul(PS[6 + k][:, 0:w], GLT[:, i * P:(i + 1) * P], WG[:, c0:c0 + w],
                                                    start=True, stop=True)
                        last.then_inc(z_ready, 1)
                    elif what == "decay":
                        p, d = st[1:]
                        g, ft, i = decay_unit(p, d)
                        if d_no == 0:
                            pe.wait_ge(lg_ready, TT)
                            pe.wait_ge(consts, 4)
                        if d_no >= 2:
                            pe.wait_ge(e_ready, d_no - 1)
                        if p == 1 and d == 0:
                            pe.wait_ge(o_kept, 2)
                        o = PS[4 + d_no % 2]
                        parts = [(0, 4 * g, 4)] if g == 0 or i == 0 else [(0, 4, 3), (3, 8, 1)]
                        for k, (c0, m, w) in enumerate(parts):
                            for q, lg in enumerate((LGH, LGL)):
                                last = nc.tensor.matmul(o[:, c0 * P:(c0 + w) * P],
                                                        lg[:, i, (3 * p + ft) * P:(3 * p + ft + 1) * P],
                                                        PATTERN[:, m:m + w, :].rearrange("p l t -> p (l t)"),
                                                        start=k == 0 and q == 0, stop=q == 1, skip_group_check=True)
                        last.then_inc(d_ready, 1)
                        d_no += 1
                    elif what == "qk_sums":
                        pe.wait_ge(qkp_ready, 1)
                        for i in range(TT):
                            for h in range(GLA_HEADS):
                                for k, (ft, r0, r1) in enumerate(head_rows(h)):
                                    last = nc.tensor.matmul(PS[7 - h % 2][:, h + i - h % 2:h + i - h % 2 + 1],
                                                            QKP[r0:r1, ft, i * P:(i + 1) * P], ONES[r0:r1, :],
                                                            start=i == 0 and h < 2 and k == 0, stop=k == 1,
                                                            skip_group_check=True)
                        last.then_inc(dq_ready, 1)
                    elif what == "gla_scores":
                        h, i = st[1:]
                        pe.wait_ge(qk_ready, LEVELS * (h // 2 + 1))
                        if h >= 1:
                            pe.wait_ge(at_ready, 2 * (h - 1) + i + 1)
                        else:
                            pe.wait_ge(dq_kept, 1)
                        o = PS[6 + i]
                        for l in range(LEVELS):
                            hf = 1 << l
                            for k, (ft, r0, r1) in enumerate(head_rows(h)):
                                ft -= 3 * (h // 2)
                                if l < 7:
                                    lhs = E[r0:r1, l, ft, i * P:(i + 1) * P]
                                    rhs = E[r0:r1, l, ft, i * P:(i + 1) * P].rearrange("p (b w o) -> p b w o", w=2, o=hf)[:, :, 1, :]
                                    dst = o[:, 64 * l:64 * (l + 1)].rearrange("p (b o) -> p b o", o=hf)
                                else:
                                    lhs = E[r0:r1, l, ft, 0:P]
                                    rhs = E[r0:r1, l, ft, P + 64 * i:P + 64 * (i + 1)]
                                    dst = o[:, 448:512]
                                last = nc.tensor.matmul(dst, lhs, rhs, start=l == 0 and k == 0, stop=k == 1,
                                                        skip_group_check=True)
                        last.then_inc(s_ready, 1)
                    elif what == "gla_out":
                        h, = st[1:]
                        pe.wait_ge(at_ready, 2 * h + 2)
                        pe.wait_ge(e_ready, 12 * (h // 2 + 1))
                        pe.wait_ge(act_drained, C[f"g_v{(384 * h + 383) // 512}"].c + 1)
                        pe.wait_ge(dve_drained, C[f"g_v{(384 * h + 383) // 512}"].c + 1)
                        if h >= 1:
                            pe.wait_ge(o_kept, h)
                        v = slice(h * GLA_DV, (h + 1) * GLA_DV)
                        nc.tensor.matmul(PS[4][:, 0:GLA_DV], AT[:, h % 2, 0, :], V[:, 0, v], start=True, stop=True)
                        nc.tensor.matmul(PS[5][:, 0:GLA_DV], AT[:, h % 2, 2, :], V[:, 0, v], start=True, stop=False)
                        nc.tensor.matmul(PS[5][:, 0:GLA_DV], AT[:, h % 2, 1, :], V[:, 1, v], start=False, stop=True)\
                            .then_inc(o_ready, 1)
                    elif what == "scores":
                        unit, at_i = st[1:]
                        kind, which, h = unit
                        if at_i == 0:
                            pe.wait_ge(o_kept, GLA_HEADS)
                            pe.wait_ge(at_ready, 2 * GLA_HEADS)
                        score_bank_free(s_no)
                        bank = PS[4 + s_no % 2]
                        if kind == "x":
                            ch = C["g_xq" if which == 0 else "n_xq"]
                            pe.wait_ge(act_drained, ch.c + 1)
                            pe.wait_ge(dve_drained, ch.c + 1)
                            for i in range(TT):
                                last = nc.tensor.matmul(bank[:, i * SEQ:(i + 1) * SEQ], XQT[:, h, i * P:(i + 1) * P],
                                                        KX[which][:, h, :], start=i == 0, stop=True, skip_group_check=True)
                        else:
                            ch = C[f"n_q{h // 4}"]
                            pe.wait_ge(act_drained, ch.c + 1)
                            pe.wait_ge(dve_drained, ch.c + 1)
                            g = h // HPG
                            nc.tensor.matmul(bank[:, 0:P], NQT[:, h, 0:P], NKT[:, which, g, 0:P],
                                             start=True, stop=False, skip_group_check=True)
                            nc.tensor.matmul(bank[:, P:P + SEQ], NQT[:, h, P:SEQ], NKT[:, which, g, :],
                                             start=False, stop=False, skip_group_check=True)
                            nc.tensor.matmul(bank[:, 0:P], IDB[:, :], CB[:, :], start=False, stop=True, skip_group_check=True)
                            last = nc.tensor.matmul(bank[:, SEQ:SEQ + P], IDB[:, :], CB[:, :], start=False, stop=True,
                                                    skip_group_check=True)
                        last.then_inc(sc_ready, 1)
                        s_no += 1
                    elif what == "probs_t":
                        unit, t, at_i = st[1:]
                        kind, which, h = unit
                        if t >= 1:
                            pe.wait_ge(pt_kept, t)
                        if kind == "cmp":
                            pe.wait_ge(cs_done, h // 4 + 1)
                            for i in range(TT):
                                last = nc.tensor.transpose(PS[6][0:16, i * P:(i + 1) * P], PC[:, h // 4, 2 * (h % 4) + i, :],
                                                           IDENT[:, :])
                        else:
                            pe.wait_ge(pn_ready, at_i + 1)
                            pr = unit_probs(unit)[0]
                            for k in range(4 if kind == "x" else 3):
                                last = nc.tensor.transpose(PS[6][:, k * P:(k + 1) * P], pr[:, at_i % 2, k * P:(k + 1) * P],
                                                           IDENT[:, :])
                        last.then_inc(pt_ready, 1)
                    elif what == "pv":
                        unit, t, at_i = st[1:]
                        kind, which, h = unit
                        pe.wait_ge(pt_kept, t + 1)
                        e = head_no(unit)
                        o = [PS[7][:, i * P:(i + 1) * P] for i in range(TT)]
                        if kind in ("x", "cmp"):
                            if e >= 1:
                                pe.wait_ge(head_kept, e)
                        if kind == "x":
                            pt = unit_probs(unit)[1]
                            for i in range(TT):
                                for m in range(TT):
                                    last = nc.tensor.matmul(o[i], pt[:, t % 2, (2 * i + m) * P:(2 * i + m + 1) * P],
                                                            VX[which][:, m, h * HD:(h + 1) * HD], start=i == 0 and m == 0,
                                                            stop=m == 1, skip_group_check=True)
                        elif kind == "cmp":
                            for i in range(TT):
                                last = nc.tensor.matmul(o[i], PTC[0:N_CMP, t % 2, i * P:(i + 1) * P], VC[:, h // HPG, :],
                                                        start=i == 0, stop=False, skip_group_check=True)
                        else:
                            g = slice(h // HPG * HD, (h // HPG + 1) * HD)
                            pt = PT1
                            for i, blk, m in ((0, 0, 0), (1, 1, 0), (1, 2, 1)):
                                last = nc.tensor.matmul(o[i], pt[:, t % 2, blk * P:(blk + 1) * P], NV[:, which, m, g],
                                                        start=False, stop=which == 1 and blk != 1, skip_group_check=True)
                        last.then_inc(pv_ready, 1)
                    elif what == "pe_t":
                        pe.wait_ge(pe_in, 32)
                        pe.wait_ge(tr_lo, 4 * KT)
                        for g in range(2):
                            last = nc.tensor.transpose(PS[4][:, g * CMP_LEN:(g + 1) * CMP_LEN], PE0[:, g, :],
                                                       IDENT[0:CMP_LEN, 0:CMP_LEN])
                        last.then_inc(small_t, 1)
                    elif what == "cmp_kv":
                        g, = st[1:]
                        pe.wait_ge(hid_ready, g + 1)
                        pe.wait_ge(w2_in, 32)
                        if g == 0:
                            for t in range(2):
                                last = nc.tensor.matmul(PS[6][:, 0:NB], W2[:, 0, t, :], HID[:, 0, t, 0:NB], start=t == 0, stop=t == 1)
                        else:
                            pe.wait_ge(kvc_kept, 1)
                            for gr in range(NSA_GROUPS):
                                for t in range(2):
                                    last = nc.tensor.matmul(PS[6][0:N_CMP, gr * HD:(gr + 1) * HD],
                                                            HID[:, 1, t, gr * N_CMP:(gr + 1) * N_CMP], W2[:, 1, t, :],
                                                            start=gr == 0 and t == 0, stop=t == 1, skip_group_check=True)
                        last.then_inc(kvc_ready, 1)
                    elif what == "cmp_scores":
                        j, = st[1:]
                        if j == 0:
                            pe.wait_ge(kvc_kept, 2)
                            pe.wait_ge(consts2, 1)
                        ch = C[f"n_q{j}"]
                        pe.wait_ge(act_drained, ch.c + 1)
                        pe.wait_ge(dve_drained, ch.c + 1)
                        score_bank_free(s_no)
                        bank = PS[4 + s_no % 2]
                        for hh in range(4):
                            h = 4 * j + hh
                            for i in range(TT):
                                o = bank[:, (2 * hh + i) * 16:(2 * hh + i) * 16 + N_CMP]
                                g = h // HPG
                                nc.tensor.matmul(o, NQT[:, h, i * P:(i + 1) * P], KC[:, g * N_CMP:(g + 1) * N_CMP],
                                                 start=hh == 0 and i == 0, stop=False, skip_group_check=True)
                                last = nc.tensor.matmul(o, IDB[:, :], CMB[:, i, 0:N_CMP], start=False, stop=True,
                                                        skip_group_check=True)
                        last.then_inc(cs_ready, 1)
                        s_no += 1

        @block.scalar
        def _(act):
            count = [0]

            def step(ins):
                count[0] += 1
                ins.then_inc(act_step, 1)
                act.wait_ge(act_step, count[0])

            def split_high(n):
                act.wait_ge(raw_in[n % RING], 16 * (n // RING + 1))
                if n >= RING:
                    act.wait_ge(piece_used, n - RING + 1)
                ch, j = piece_of[n]
                w = slice(0, ch.tiles * ch.width)
                nc.scalar.activation(WHI[:, n % RING, w], RAW[:, n % RING, w], ACT.Copy).then_inc(hi_ready, 1)

            def transposed_high(stage, kt, n):
                act.wait_ge(tr_ready, n + 1)
                if n == KT or n == 2 * KT or n == 3 * KT or n == 4 * KT:
                    act.wait_ge(piece_used, C[lhs_free(stage)].last + 1)
                if n == 0:
                    act.wait_ge(small_c, 1)
                src = PS[4 + n % 4][:, 0:SEQ]
                for hi, lo, gain in t_dest(stage):
                    if gain is None:
                        last = nc.scalar.activation(hi[:, kt, :], src, ACT.Copy)
                    else:
                        last = nc.scalar.activation(hi[:, kt, :], src, ACT.Copy, scale=GT[:, gain + kt:gain + kt + 1])
                last.then_inc(tr_hi, 1)

            def square(stage, i, src):
                nc.scalar.activation(JUNK[:, 0:D_MODEL], src, ACT.Square, accum_out=SS[:, 2 * stage + i:2 * stage + i + 1])\
                    .then_inc(squared, 1)

            for i in range(TT):
                act.wait_ge(mem_in[i], 16)
                if i:
                    act.wait_ge(squared, i)
                square(0, i, Y[:, i, :])
            for n in range(LEAD):
                split_high(n)
            for kt in range(KT):
                transposed_high("mem", kt, kt)
            s_no = d_no = 0
            for s in slots:
                if s >= 0 and s + LEAD < pieces:
                    split_high(s + LEAD)
                for st in steps.get(s, ()):
                    what = st[0]
                    if what == "square":
                        for i in range(TT):
                            act.wait_ge(x_in[i], 16)
                            act.wait_ge(squared, TT + i)
                            square(1, i, H[:, i, :])
                    elif what == "transpose":
                        transposed_high(*st[1:], t_order[st[1:]])
                    elif what == "drain":
                        ch, = st[1:]
                        act.wait_ge(piece_used, ch.last + 1)
                        src, scale = acc_bank(ch, 0), 1.0
                        if ch.name.startswith("mem_k"):
                            dst = KX[int(ch.name[-1])][:, 0:2, :].rearrange("p b t -> p (b t)")
                        elif ch.name.startswith("mem_v"):
                            dst = VX[int(ch.name[-1])][:, 0, :]
                        elif ch.name == "g_lr":
                            act.wait_ge(tr_lo, KT)
                            dst, src = GLR[:, :, 0:RANK], src[:, 0:128].rearrange("p (i w) -> p i w", i=TT)[:, :, 0:RANK]
                        elif ch.name.startswith("g_qk"):
                            j = int(ch.name[-1])
                            dst = QK[:, 4 * j:4 * j + 2, :].rearrange("p b t -> p (b t)")
                            scale = GLA_SCALE if 4 * j < FT else 1.0
                        elif ch.name.startswith("g_v"):
                            j = int(ch.name[-1])
                            dst = V[:, 0, 512 * j:512 * (j + 1)]
                        elif ch.name in ("g_xq", "n_xq"):
                            if ch.name == "n_xq":
                                act.wait_ge(sc_ready, X_HEADS)
                            dst = XQT[:, 0:2, :].rearrange("p b t -> p (b t)")
                        elif "out" in ch.name:
                            j = int(ch.name[-1])
                            if j == 0:
                                act.wait_ge(tr_lo, (3 if ch.name[0] == "g" else 5) * KT)
                            dst = Y[:, 0, 512 * j:512 * (j + 1)]
                        elif ch.name == "n_gl":
                            nc.scalar.activation(GATES[:, :, 0:36], src[:, 0:128].rearrange("p (i w) -> p i w", i=TT)[:, :, 0:36],
                                                 ACT.Exp, scale=-1.0).then_inc(act_drained, 1)
                            continue
                        elif ch.name == "n_cmp":
                            dst = KVC[:, 0].rearrange("p g t -> p (g t)")
                        elif ch.name in ("n_slc", "n_win"):
                            dst = NKT[:, 0 if ch.name == "n_slc" else 1].rearrange("p g t -> p (g t)")
                        elif ch.name.startswith("n_q"):
                            j = int(ch.name[-1])
                            dst = NQT[:, 4 * j:4 * j + 2, :].rearrange("p b t -> p (b t)")
                        nc.scalar.activation(dst, src if ch.kind == NARROW else src[:, 0:512], ACT.Copy, scale=scale)\
                            .then_inc(act_drained, 1)
                    elif what == "gated_drain":
                        ch, = st[1:]
                        act.wait_ge(piece_used, ch.last + 1)
                        for i in range(TT):
                            if gated_no(ch):
                                act.wait_ge(mixed_gated, TT * (gated_no(ch) - 1) + i + 1)
                            ins = nc.scalar.activation(SG[:, i, :], acc_bank(ch, i)[:, :], ACT.Exp, scale=-1.0)
                            if i == 0:
                                ins.then_inc(sg_exp, 1)
                            else:
                                ins.then_inc(sg_exp, 1)
                        act.wait_ge(sg_exp, TT * (gated_no(ch) + 1))
                        nc.scalar.activation(ST[:, 150:151], ST[:, 144:145], ACT.Copy).then_inc(act_drained, 1)
                    elif what == "hidden_drain":
                        ch, = st[1:]
                        g = "KV".index(ch.lhs)
                        act.wait_ge(piece_used, ch.last + 1)
                        nc.scalar.activation(HSG[:, g, :, 0:NB], acc_bank(ch, 0)[:, 0:64].rearrange("p (t n) -> p t n", t=2)[:, :, 0:NB],
                                             ACT.Exp, scale=-1.0).then_inc(act_drained, 1)
                    elif what == "gate":
                        i, = st[1:]
                        act.wait_ge(z_ready, i + 1)
                        step(nc.scalar.activation(ZA[:, 0:512], PS[6][:, :], ACT.Abs))
                        step(nc.scalar.activation(ZA[:, 512:KEYW], PS[7][:, 0:KEYW - 512], ACT.Abs))
                        step(nc.scalar.activation(ZA[:, :], ZA[:, :], ACT.Exp, scale=-1.0))
                        nc.scalar.activation(ZL[:, :], ZA[:, :], ACT.Ln, bias=1.0).then_inc(z_exp, 1)
                    elif what == "decay":
                        p, d = st[1:]
                        g, ft, i = decay_unit(p, d)
                        act.wait_ge(d_ready, d_no + 1)
                        if d == 0 and p == 1:
                            act.wait_ge(s_ready, 4)
                        nc.scalar.activation(E[:, 4 * g:4 * g + 4, ft, i * P:(i + 1) * P],
                                             PS[4 + d_no % 2][:, :].rearrange("p (l t) -> p l t", l=4), ACT.Exp,
                                             scale=1.0 / GATE_TEMP).then_inc(e_ready, 1)
                        d_no += 1
                    elif what == "gla_out":
                        h, = st[1:]
                        act.wait_ge(o_kept, h + 1)
                        for i in range(TT):
                            nc.scalar.activation(SG[:, i, 0:GLA_DV], V[:, i, h * GLA_DV:(h + 1) * GLA_DV], ACT.Square,
                                                 accum_out=SSG[:, 2 * h + i:2 * h + i + 1]).then_inc(o_sq, 1)
                            act.wait_ge(o_sq, 2 * h + i + 1)
                    elif what == "scores":
                        unit, at_i = st[1:]
                        kind, which, h = unit
                        act.wait_ge(mx_ready, at_i + 1)
                        if at_i >= 2:
                            act.wait_ge(pt_ready, tables["attn"][at_i - 2] + 1)
                        pr = unit_probs(unit)[0]
                        bank, b = PS[4 + s_no % 2], at_i % 2
                        spans = ((0, SEQ), (SEQ, 2 * SEQ)) if kind == "x" else ((0, P), (P, P + SEQ))
                        if kind == "nsa" and at_i == X_HEADS:
                            act.wait_ge(consts2, 1)
                        for i, (c0, c1) in enumerate(spans):
                            ins = nc.scalar.activation(pr[:, b, c0:c1], bank[:, c0:c1], ACT.Exp, scale=ATT_SCALE,
                                                       bias=NM[:, 2 * b + i:2 * b + i + 1], accum_out=RS[:, 2 * b + i:2 * b + i + 1])
                        ins.then_inc(pr_ready, 1)
                        s_no += 1
                    elif what == "probs_t":
                        unit, t, at_i = st[1:]
                        act.wait_ge(pt_ready, t + 1)
                        if t >= 2:
                            act.wait_ge(pv_ready, t - 1)
                        if unit[0] == "cmp":
                            nc.scalar.activation(PTC[:, t % 2, :], PS[6][0:16, 0:SEQ], ACT.Copy).then_inc(pt_kept, 1)
                        else:
                            w = 512 if unit[0] == "x" else 384
                            nc.scalar.activation(unit_probs(unit)[1][:, t % 2, 0:w], PS[6][:, 0:w], ACT.Copy).then_inc(pt_kept, 1)
                    elif what == "pv":
                        unit, t, at_i = st[1:]
                        kind, which, h = unit
                        if kind == "x":
                            act.wait_ge(pv_ready, t + 1)
                            act.wait_ge(pn_ready, at_i + 1)
                            for i in range(TT):
                                ins = nc.scalar.activation(Y[:, i, BW + h * HD:BW + (h + 1) * HD], PS[7][:, i * P:(i + 1) * P],
                                                           ACT.Copy, scale=RI[:, 2 * (at_i % 2) + i:2 * (at_i % 2) + i + 1])
                            ins.then_inc(head_kept, 1)
                        elif kind == "nsa" and which == 1:
                            act.wait_ge(pv_ready, t + 1)
                            nc.scalar.activation(Y[:, :, h * HD:(h + 1) * HD], PS[7][:, 0:SEQ].rearrange("p (i d) -> p i d", i=TT),
                                                 ACT.Copy).then_inc(head_kept, 1)
                    elif what == "cmp_scores":
                        j, = st[1:]
                        act.wait_ge(cs_shift, j + 1)
                        nc.scalar.activation(PC[:, j, :, 0:N_CMP], PC[:, j, :, 0:N_CMP], ACT.Exp, scale=ATT_SCALE).then_inc(cs_exp, 1)
                        s_no += 1
                    elif what == "residual":
                        l, = st[1:]
                        for i in range(TT):
                            act.wait_ge(dve_drained, C["g_out3" if l == 0 else "n_out3"].c + 1)
                            act.wait_ge(act_drained, C["g_out3" if l == 0 else "n_out3"].c + 1)
                            act.wait_ge(post_in[l], 16)
                            nc.scalar.activation(JUNK2[:, :], Y[:, i, :], ACT.Square,
                                                 accum_out=SS[:, 4 + 4 * l + i:5 + 4 * l + i]).then_inc(y_sq, 1)
                            act.wait_ge(y_sq, 2 * l + i + 1)
                        if l == 0:
                            for i in range(TT):
                                act.wait_ge(res_ready, i + 1)
                                nc.scalar.activation(JUNK2[:, :], H[:, i, :], ACT.Square,
                                                     accum_out=SS[:, 6 + i:7 + i]).then_inc(squared, 1)
                                act.wait_ge(squared, 2 * TT + i + 1)

        @block.vector
        def _(dve):
            count = [0]

            def step(ins):
                count[0] += 1
                ins.then_inc(dve_step, 1)
                dve.wait_ge(dve_step, count[0])

            def split_low(n):
                dve.wait_ge(hi_ready, n + 1)
                ch, j = piece_of[n]
                w = slice(0, ch.tiles * ch.width)
                nc.vector.tensor_tensor(WLO[:, n % RING, w], RAW[:, n % RING, w], WHI[:, n % RING, w].bitcast(f32), ALU.subtract)\
                    .then_inc(lo_ready, 1)

            rstds = [0]

            def rstd(dst, src, n):
                nc.vector.tensor_scalar(dst, src, 1.0 / n, EPS, ALU.mult, ALU.add).then_inc(mean_ready, 1)
                rstds[0] += 1
                dve.wait_ge(rstd_ready, rstds[0])

            def transposed_low(stage, kt, n):
                dve.wait_ge(tr_hi, n + 1)
                src = PS[4 + n % 4][:, 0:SEQ]
                for hi, lo, gain in t_dest(stage):
                    if gain is None:
                        last = nc.vector.tensor_tensor(lo[:, kt, :], src, hi[:, kt, :].bitcast(f32), ALU.subtract)
                    else:
                        last = nc.vector.scalar_tensor_tensor(lo[:, kt, :], src, GT[:, gain + kt:gain + kt + 1],
                                                              hi[:, kt, :].bitcast(f32), ALU.mult, ALU.subtract)
                last.then_inc(tr_lo, 1)

            dve.wait_ge(small_t, 1)
            nc.vector.tensor_copy(GT[:, :], PS[0][:, 0:4 * KT]).then_inc(small_c, 1)
            for i in range(TT):
                dve.wait_ge(squared, i + 1)
                rstd(RSTD[:, i:i + 1], SS[:, i:i + 1], D_MODEL)
                nc.vector.tensor_scalar(Y[:, i, :], Y[:, i, :], RSTD[:, i:i + 1], None, ALU.mult).then_inc(normed, 1)
            for n in range(LEAD):
                split_low(n)
            for kt in range(KT):
                transposed_low("mem", kt, kt)
            s_no = 0
            for s in slots:
                if s >= 0 and s + LEAD < pieces:
                    split_low(s + LEAD)
                for st in steps.get(s, ()):
                    what = st[0]
                    if what == "square":
                        for i in range(TT):
                            dve.wait_ge(squared, TT + i + 1)
                            rstd(RSTD[:, 2 + i:3 + i], SS[:, 2 + i:3 + i], D_MODEL)
                            nc.vector.tensor_scalar(H[:, i, :], H[:, i, :], RSTD[:, 2 + i:3 + i], None, ALU.mult).then_inc(normed, 1)
                    elif what == "transpose":
                        transposed_low(*st[1:], t_order[st[1:]])
                    elif what == "drain":
                        ch, = st[1:]
                        src, scale = acc_bank(ch, 1), None
                        if ch.kind == NARROW:
                            if ch.name == "n_gl":
                                dve.wait_ge(act_drained, ch.c + 1)
                                step(nc.vector.tensor_scalar(GATES[:, :, 0:36], GATES[:, :, 0:36], 1.0, None, ALU.add))
                                nc.vector.reciprocal(GATES[:, :, 0:36], GATES[:, :, 0:36]).then_inc(dve_drained, 1)
                            else:
                                dve.wait_ge(wg_in, 32)
                                dve.wait_ge(tr_lo, KT)
                                nc.vector.memset(GLT[:, :], 1.0).then_inc(dve_drained, 1)
                            continue
                        dve.wait_ge(piece_used, ch.last + 1)
                        if ch.name.startswith("mem_k"):
                            dst = KX[int(ch.name[-1])][:, 2:4, :].rearrange("p b t -> p (b t)")
                        elif ch.name.startswith("mem_v"):
                            dst = VX[int(ch.name[-1])][:, 1, :]
                        elif ch.name.startswith("g_qk"):
                            j = int(ch.name[-1])
                            dst = QK[:, 4 * j + 2:4 * j + 4, :].rearrange("p b t -> p (b t)")
                            scale = GLA_SCALE if 4 * j + 2 < FT else None
                        elif ch.name.startswith("g_v"):
                            j = int(ch.name[-1])
                            dst = V[:, 1, 512 * j:512 * (j + 1)]
                        elif ch.name in ("g_xq", "n_xq"):
                            if ch.name == "n_xq":
                                dve.wait_ge(sc_ready, X_HEADS)
                            dst = XQT[:, 2:4, :].rearrange("p b t -> p (b t)")
                        elif "out" in ch.name:
                            j = int(ch.name[-1])
                            dst = Y[:, 1, 512 * j:512 * (j + 1)]
                        elif ch.name == "n_cmp":
                            dst = KVC[:, 1].rearrange("p g t -> p (g t)")
                        elif ch.name in ("n_slc", "n_win"):
                            dst = NV[:, 0 if ch.name == "n_slc" else 1].rearrange("p i w -> p (i w)")
                        elif ch.name.startswith("n_q"):
                            j = int(ch.name[-1])
                            dst = NQT[:, 4 * j + 2:4 * j + 4, :].rearrange("p b t -> p (b t)")
                        if scale is None:
                            nc.vector.tensor_copy(dst, src[:, 0:512]).then_inc(dve_drained, 1)
                        else:
                            nc.vector.tensor_scalar(dst, src[:, 0:512], scale, None, ALU.mult).then_inc(dve_drained, 1)
                    elif what == "gated_drain":
                        ch, = st[1:]
                        k = gated_no(ch)
                        c0 = BW if "xg" in ch.name else 512 * int(ch.name[-1])
                        if k == 0:
                            dve.wait_ge(o_norm, GLA_HEADS)
                        if k == 1:
                            dve.wait_ge(head_kept, X_HEADS)
                        if k == 4:
                            dve.wait_ge(head_kept, len(heads))
                        for i in range(TT):
                            dve.wait_ge(sg_exp, TT * k + i + 1)
                            step(nc.vector.tensor_scalar(SG[:, i, :], SG[:, i, :], 1.0, None, ALU.add))
                            step(nc.vector.reciprocal(SG[:, i, :], SG[:, i, :]))
                            step(nc.vector.tensor_tensor(SG[:, i, :], SG[:, i, :], acc_bank(ch, i)[:, :], ALU.mult))
                            nc.vector.tensor_tensor(Y[:, i, c0:c0 + 512], Y[:, i, c0:c0 + 512], SG[:, i, :], ALU.mult)\
                                .then_inc(mixed_gated, 1)
                        dve.wait_ge(mixed_gated, TT * (k + 1))
                        nc.vector.memset(ST[:, 151:152], 0.0).then_inc(dve_drained, 1)
                    elif what == "hidden_drain":
                        ch, = st[1:]
                        g = "KV".index(ch.lhs)
                        dve.wait_ge(act_drained, ch.c + 1)
                        v = HSG[:, g, :, 0:NB]
                        step(nc.vector.tensor_scalar(v, v, 1.0, None, ALU.add))
                        step(nc.vector.reciprocal(v, v))
                        step(nc.vector.tensor_tensor(HID[:, g, :, 0:NB], v,
                                                     acc_bank(ch, 0)[:, 0:64].rearrange("p (t n) -> p t n", t=2)[:, :, 0:NB], ALU.mult))
                        nc.vector.memset(ST[:, 151:152], 0.0).then_inc(dve_drained, 1)
                        nc.vector.memset(ST[:, 152:153], 0.0).then_inc(hid_ready, 1)
                    elif what == "rank_t":
                        dve.wait_ge(small_t, 2)
                        dve.wait_ge(dve_drained, C["g_lr"].c + 1)
                        nc.vector.tensor_copy(GLT[0:RANK, :], PS[4][0:RANK, 0:SEQ]).then_inc(small_c, 1)
                    elif what == "gate":
                        i, = st[1:]
                        dve.wait_ge(z_exp, i + 1)
                        nc.vector.scalar_tensor_tensor(ZG[:, 0:512], PS[6][:, :], 0.0, ZL[:, 0:512], ALU.min, ALU.subtract)
                        step(nc.vector.scalar_tensor_tensor(ZG[:, 512:KEYW], PS[7][:, 0:KEYW - 512], 0.0, ZL[:, 512:KEYW],
                                                            ALU.min, ALU.subtract))
                        step(nc.vector.tensor_copy(LGH[:, i, :], ZG[:, :]))
                        nc.vector.tensor_tensor(LGL[:, i, :], ZG[:, :], LGH[:, i, :].bitcast(f32), ALU.subtract).then_inc(lg_ready, 1)
                    elif what == "qk_sums":
                        dve.wait_ge(act_drained, C["g_qk2"].c + 1)
                        dve.wait_ge(dve_drained, C["g_qk2"].c + 1)
                        nc.vector.tensor_tensor(QKP[:, :, :], QK[:, 0:FT, :], QK[:, FT:2 * FT, :], ALU.mult).then_inc(qkp_ready, 1)
                        dve.wait_ge(dq_ready, 1)
                        for par in range(2):
                            ins = nc.vector.tensor_copy(DQ.rearrange("p (g w i) -> p g w i", w=2, i=TT)[:, :, par, :],
                                                        PS[7 - par][:, 0:4].rearrange("p (g i) -> p g i", i=TT))
                        ins.then_inc(dq_kept, 1)
                    elif what == "decayed":
                        p, l = st[1:]
                        dve.wait_ge(e_ready, 12 * p + 6 * (l // 4 + 1))
                        hf = 1 << l

                        def halves(x, w):
                            return x.rearrange("p f t -> p (f t)").rearrange("p (b w o) -> p b w o", w=2, o=hf)[:, :, w, :]

                        e = E[:, l, :, :]
                        nc.vector.tensor_tensor(halves(e, 1), halves(e, 1), halves(QK[:, 3 * p:3 * p + 3, :], 1), ALU.mult)
                        nc.vector.tensor_tensor(halves(e, 0), halves(e, 0), halves(QK[:, FT + 3 * p:FT + 3 * p + 3, :], 0), ALU.mult)\
                            .then_inc(qk_ready, 1)
                    elif what == "gla_scores":
                        h, i = st[1:]
                        dve.wait_ge(s_ready, 2 * h + i + 1)
                        if h == 0 and i == 0:
                            dve.wait_ge(consts, 4)
                        if h >= 2:
                            dve.wait_ge(o_ready, h - 1)
                        for l in range(7):
                            hf = 1 << l
                            dst = AT[:, h % 2, i, :].rearrange("p (b w o) -> p b w o", w=2, o=hf)[:, :, 1, :]
                            src = PS[6 + i][:, 64 * l:64 * (l + 1)].rearrange("p (b o) -> p b o", o=hf)
                            msk = LMASK[:, l, :].rearrange("p (b o) -> p b o", o=hf)
                            step(nc.vector.copy_predicated(dst, msk, src))
                        nc.vector.tensor_copy(AT[:, h % 2, 2, 64 * i:64 * (i + 1)], PS[6 + i][:, 448:512]).then_inc(at_ready, 1)
                    elif what == "gla_out":
                        h, = st[1:]
                        dve.wait_ge(o_ready, h + 1)
                        v = slice(h * GLA_DV, (h + 1) * GLA_DV)
                        for i in range(TT):
                            ins = nc.vector.scalar_tensor_tensor(V[:, i, v], V[:, i, v], DQ[:, 2 * h + i:2 * h + i + 1],
                                                                 PS[4 + i][:, 0:GLA_DV], ALU.mult, ALU.add)
                        ins.then_inc(o_kept, 1)
                    elif what == "gla_norm":
                        dve.wait_ge(o_sq, 2 * GLA_HEADS)
                        dve.wait_ge(gn_in, 16)
                        rstd(RG, SSG, GLA_DV)
                        for h in range(GLA_HEADS):
                            v = slice(h * GLA_DV, (h + 1) * GLA_DV)
                            for i in range(TT):
                                ins = nc.vector.scalar_tensor_tensor(Y[:, i, v], V[:, i, v], RG[:, 2 * h + i:2 * h + i + 1],
                                                                     GN[:, :], ALU.mult, ALU.mult)
                            ins.then_inc(o_norm, 1)
                    elif what == "scores":
                        unit, at_i = st[1:]
                        kind, which, h = unit
                        dve.wait_ge(sc_ready, at_i + 1)
                        bank, b = PS[4 + s_no % 2], at_i % 2
                        m = MX[:, 2 * b:2 * b + 2]
                        if kind == "x":
                            step(nc.vector.tensor_reduce(m, bank[:, :].rearrange("p (i k) -> p i k", i=TT), AX.X, ALU.max))
                        else:
                            nc.vector.tensor_reduce(m[:, 0:1], bank[:, 0:P], AX.X, ALU.max)
                            step(nc.vector.tensor_reduce(m[:, 1:2], bank[:, P:P + SEQ], AX.X, ALU.max))
                        nc.vector.tensor_scalar(NM[:, 2 * b:2 * b + 2], m, -ATT_SCALE, None, ALU.mult).then_inc(mx_ready, 1)
                        s_no += 1
                    elif what == "probs_t":
                        unit, t, at_i = st[1:]
                        kind, which, h = unit
                        if kind == "cmp":
                            continue
                        b = at_i % 2
                        dve.wait_ge(pr_ready, at_i + 1)
                        ri = RI[:, 2 * b:2 * b + 2]
                        if kind == "x":
                            if at_i % X_HEADS >= 2:
                                dve.wait_ge(head_kept, head_no(unit) - 1)
                            nc.vector.reciprocal(ri, RS[:, 2 * b:2 * b + 2]).then_inc(pn_ready, 1)
                        else:
                            step(nc.vector.reciprocal(ri, RS[:, 2 * b:2 * b + 2]))
                            step(nc.vector.tensor_tensor(ri, ri, GATES[:, :, N_BRANCH * h + 1 + which], ALU.mult))
                            nc.vector.tensor_scalar(PN[:, b, 0:P], PN[:, b, 0:P], ri[:, 0:1], None, ALU.mult)
                            nc.vector.tensor_scalar(PN[:, b, P:P + SEQ], PN[:, b, P:P + SEQ], ri[:, 1:2], None, ALU.mult)\
                                .then_inc(pn_ready, 1)
                    elif what == "pe_t":
                        dve.wait_ge(small_t, 3)
                        nc.vector.tensor_copy(PET[:, :, :].rearrange("p g j -> p (g j)"), PS[4][:, 0:2 * CMP_LEN]).then_inc(small_c, 1)
                    elif what == "blocks":
                        g, = st[1:]
                        dve.wait_ge(act_drained, C["n_cmp"].c + 1)
                        dve.wait_ge(dve_drained, C["n_cmp"].c + 1)
                        dve.wait_ge(small_c, 3)
                        if g:
                            dve.wait_ge(blk_ready, g)
                        for half in range(2):
                            for gr in range(NSA_GROUPS):
                                src = KVC[:, g, gr, half * 16:half * 16 + 16 * N_CMP].rearrange("p (n j) -> p j n", j=16)
                                pe_b = PET[:, g, half * 16:(half + 1) * 16].unsqueeze(2).to_broadcast([P, 16, N_CMP])
                                dst = BKT[:, half * 16:(half + 1) * 16, gr * N_CMP:(gr + 1) * N_CMP]
                                last = nc.vector.tensor_tensor(dst, src, pe_b, ALU.add)
                        step(last)
                        flat = "p j n -> p (j n)"
                        step(nc.vector.tensor_copy(BKH[:, g].rearrange(flat), BKT[:, :, :].rearrange(flat)))
                        nc.vector.tensor_tensor(BKL[:, g].rearrange(flat), BKT[:, :, :].rearrange(flat),
                                                BKH[:, g].rearrange(flat).bitcast(f32), ALU.subtract).then_inc(blk_ready, 1)
                    elif what == "cmp_kv":
                        g, = st[1:]
                        dve.wait_ge(kvc_ready, g + 1)
                        if g == 0:
                            nc.vector.tensor_copy(KC[:, 0:NB], PS[6][:, 0:NB]).then_inc(kvc_kept, 1)
                            nc.vector.memset(PC[:, :, :, :], 0.0)
                        else:
                            nc.vector.tensor_copy(VC[:, :, :].rearrange("p g d -> p (g d)"), PS[6][0:N_CMP, 0:SEQ]).then_inc(kvc_kept, 1)
                    elif what == "cmp_scores":
                        j, = st[1:]
                        dve.wait_ge(cs_ready, j + 1)
                        bank = PS[4 + s_no % 2][:, 0:128].rearrange("p (u n) -> p u n", n=16)[:, :, 0:N_CMP]
                        m, sm, fc = MC[:, 8 * j:8 * j + 8], SC[:, 8 * j:8 * j + 8], FC[:, 8 * j:8 * j + 8]
                        pc = PC[:, j, :, 0:N_CMP]
                        step(nc.vector.tensor_reduce(m, bank, AX.X, ALU.max))
                        nc.vector.tensor_tensor(pc, bank, m.unsqueeze(2).to_broadcast([P, 8, N_CMP]), ALU.subtract).then_inc(cs_shift, 1)
                        dve.wait_ge(cs_exp, j + 1)
                        step(nc.vector.tensor_reduce(sm, pc, AX.X, ALU.add))
                        step(nc.vector.reciprocal(fc, sm))
                        fv = fc.rearrange("p (h i) -> p h i", i=TT)
                        step(nc.vector.tensor_tensor(fv, fv, ROWOK[:, :].unsqueeze(1).to_broadcast([P, 4, TT]), ALU.mult))
                        gv = GATES[:, :, 12 * j:12 * j + 12].rearrange("p i (h b) -> p h i b", b=N_BRANCH)[:, :, :, 0]
                        step(nc.vector.tensor_tensor(fv, fv, gv, ALU.mult))
                        nc.vector.tensor_tensor(pc, pc, fc.unsqueeze(2).to_broadcast([P, 8, N_CMP]), ALU.mult).then_inc(cs_done, 1)
                        s_no += 1
                    elif what == "residual":
                        l, = st[1:]
                        for i in range(TT):
                            dve.wait_ge(y_sq, 2 * l + i + 1)
                            c = 4 + 4 * l + i
                            rstd(RSTD[:, c:c + 1], SS[:, c:c + 1], D_MODEL)
                            step(nc.vector.scalar_tensor_tensor(Y[:, i, :], Y[:, i, :], RSTD[:, c:c + 1], GPOST[l][:, :],
                                                                ALU.mult, ALU.mult))
                            if l == 0:
                                dve.wait_ge(res_in, 16 * TT)
                            nc.vector.tensor_tensor(H[:, i, :], H[:, i, :], Y[:, i, :], ALU.add).then_inc(res_ready, 1)
                        if l == 0:
                            for i in range(TT):
                                dve.wait_ge(squared, 2 * TT + i + 1)
                                rstd(RSTD[:, 6 + i:7 + i], SS[:, 6 + i:7 + i], D_MODEL)
                                nc.vector.tensor_scalar(Y[:, i, :], H[:, i, :], RSTD[:, 6 + i:7 + i], None, ALU.mult)\
                                    .then_inc(normed, 1)


_INS = ["x", "mem", "ln_pre", "ln_post", "ln_mem", "w_mem_kv", "gla_w_in", "gla_w_gate_lr", "gla_b_gate", "gla_norm",
        "gla_w_out", "nsa_w_in", "nsa_pe_k", "nsa_pe_v", "nsa_wk1", "nsa_wk2", "nsa_wv1", "nsa_wv2", "nsa_w_out"]


def kernel(**inputs):
    import numpy as _np
    import concourse.bacc as _bacc
    from concourse import mybir as _mybir
    from concourse.bass_utils import run_bass_kernel_spmd as _run

    nc = _bacc.Bacc("TRN2", target_bir_lowering=False, num_devices=1)
    arrays, args = {}, {}
    for name in _INS:
        v = _np.ascontiguousarray(inputs[name])
        arrays[f"in_{name}_dram"] = v
        args[name] = nc.dram_tensor(f"in_{name}_dram", v.shape, _mybir.dt.from_np(v.dtype), kind="ExternalInput").ap()
    out = nc.dram_tensor("out_0_dram", (1, SEQ, D_MODEL), _mybir.dt.float32, kind="ExternalOutput").ap()
    hybrid_trunk(nc, args, out)
    r = _run(nc, [arrays], core_ids=[0])
    return r.results[0]["out_0_dram"]
```

```python
import concourse.bass as bass
from concourse import mybir
from contextlib import ExitStack

P = 128
D_MODEL, SEQ, N_MEM = 2048, 256, 256
KT = D_MODEL // P
TT = SEQ // P
HD = 128
X_HEADS = 4
XW = X_HEADS * HD
BW = D_MODEL - XW
GLA_HEADS, GLA_DV = 4, BW // 4
GLA_DK = GLA_DV // 2
KEYW = GLA_HEADS * GLA_DK
FT = KEYW // P
RANK = 16
GATE_TEMP = 16.0
NSA_HEADS, NSA_GROUPS = BW // HD, 2
HPG = NSA_HEADS // NSA_GROUPS
KVW = NSA_GROUPS * HD
N_BRANCH = 3
CMP_LEN, CMP_STRIDE, CMP_HIDDEN = 32, 16, 256
N_CMP = (SEQ - CMP_LEN) // CMP_STRIDE + 1
NB = NSA_GROUPS * N_CMP
EPS = 1e-6
LEVELS = 8
MASKED = -1e30
ATT_SCALE = float(HD) ** -0.5
GLA_SCALE = float(GLA_DK) ** -0.5

RING = 4
PIECE = 1024
LEAD = RING - 1

TM, FM, MIX, NARROW, CMP = "token-major", "feature-major", "both", "narrow", "compress"


class Chunk:

    def __init__(self, name, kind, w, col, width, lhs):
        self.name, self.kind, self.w, self.col, self.width, self.lhs = name, kind, w, col, width, lhs
        self.tiles = {NARROW: KT, CMP: PIECE // CMP_HIDDEN}.get(kind, PIECE // 512)
        self.n = {CMP: CMP_LEN}.get(kind, KT) // self.tiles
        self.order = list(range(12, KT)) + list(range(12)) if "out" in name else list(range(CMP_LEN if kind == CMP else KT))


def chunk_list():
    g, n = "gla_w_in", "nsa_w_in"
    gq, gv, gl = 0, 2 * KEYW, 2 * KEYW + BW
    gr = gl + RANK
    nk = BW
    ng = BW + 6 * KVW
    nr = ng + NSA_HEADS * N_BRANCH
    out = []
    def memory(i, act):
        return [Chunk(f"mem_v{i}", TM, f"kv{i}", XW, XW, act), Chunk(f"mem_k{i}", FM, f"kv{i}", 0, XW, act)]

    out += memory(0, "A")
    out.append(Chunk("g_qk0", FM, g, gq, 512, "B"))
    out.append(Chunk("g_lr", NARROW, g, gl, RANK, "B"))
    out += [Chunk(f"g_qk{j}", FM, g, gq + 512 * j, 512, "B") for j in (1, 2)]
    out += [Chunk(f"g_v{j}", TM, g, gv + 512 * j, 512, "B") for j in range(3)]
    out.append(Chunk("g_xq", FM, g, gr + BW, XW, "B"))
    out.append(Chunk("g_r0", TM, g, gr, 512, "B"))
    out.append(Chunk("g_xg", TM, g, gr + BW + XW, XW, "B"))
    out += [Chunk(f"g_r{j}", TM, g, gr + 512 * j, 512, "B") for j in (1, 2)]
    out += [Chunk(f"g_out{j}", TM, "gla_w_out", 512 * j, 512, "A") for j in range(4)]
    out += memory(1, "B")
    out.append(Chunk("n_cmp", FM, n, nk, 2 * KVW, "A"))
    out.append(Chunk("n_gl", NARROW, n, ng, NSA_HEADS * N_BRANCH, "A"))
    out.append(Chunk("n_slc", MIX, n, nk + 2 * KVW, 2 * KVW, "A"))
    out.append(Chunk("n_win", MIX, n, nk + 4 * KVW, 2 * KVW, "A"))
    out.append(Chunk("n_wk1", CMP, "nsa_wk1", 0, CMP_HIDDEN, "K"))
    out.append(Chunk("n_wv1", CMP, "nsa_wv1", 0, CMP_HIDDEN, "V"))
    out += [Chunk(f"n_q{j}", FM, n, 512 * j, 512, "A") for j in range(3)]
    out.append(Chunk("n_xq", FM, n, nr + BW, XW, "A"))
    out.append(Chunk("n_xg", TM, n, nr + BW + XW, XW, "A"))
    out += [Chunk(f"n_r{j}", TM, n, nr + 512 * j, 512, "A") for j in range(3)]
    out += [Chunk(f"n_out{j}", TM, "nsa_w_out", 512 * j, 512, "B") for j in range(4)]
    n0 = 0
    for c, ch in enumerate(out):
        ch.c, ch.first, ch.last = c, n0, n0 + ch.n - 1
        n0 += ch.n
    return out, n0


def hybrid_trunk(nc, a, out):
    f32, f32r, bf16, i32 = mybir.dt.float32, mybir.dt.float32r, mybir.dt.bfloat16, mybir.dt.int32
    ALU, ACT, AX = mybir.AluOpType, mybir.ActivationFunctionType, mybir.AxisListType

    chunks, pieces = chunk_list()
    C = {ch.name: ch for ch in chunks}
    piece_of = [(ch, j) for ch in chunks for j in range(ch.n)]
    weights = {"kv0": a["w_mem_kv"][0], "kv1": a["w_mem_kv"][1], "gla_w_in": a["gla_w_in"][0],
               "gla_w_out": a["gla_w_out"][0], "nsa_w_in": a["nsa_w_in"][0], "nsa_w_out": a["nsa_w_out"][0],
               "nsa_wk1": a["nsa_wk1"][0], "nsa_wv1": a["nsa_wv1"][0]}

    base = (nc.sbuf_base + 31) // 32 * 32
    top = [0]

    def at(name, shape, dt, off):
        return nc.alloc_sbuf_tensor_at(name, [shape[0], *shape[1:]], dt, offset=base + off)

    def region(size):
        off = top[0]
        top[0] += (size + 31) // 32 * 32
        assert base + top[0] <= nc.sbuf_usable_end, top[0]
        return off

    def new(name, shape, dt):
        n = 4 if dt != bf16 else 2
        for s in shape[1:]:
            n *= s
        return at(name, shape, dt, region(n))

    RAW = new("weights_raw", [P, RING, PIECE], f32)
    WHI = new("weights_high", [P, RING, PIECE], f32r)
    WLO = new("weights_low", [P, RING, PIECE], f32r)
    a_off = region(2 * KT * SEQ * 4)
    AHI = at("act_a_high", [P, KT, SEQ], f32r, a_off)
    ALO = at("act_a_low", [P, KT, SEQ], f32r, a_off + KT * SEQ * 4)
    b_off = region(2 * KT * SEQ * 4)
    BHI = at("act_b_high", [P, KT, SEQ], f32r, b_off)
    BLO = at("act_b_low", [P, KT, SEQ], f32r, b_off + KT * SEQ * 4)
    h_off = region(TT * D_MODEL * 4)
    H = at("stream", [P, TT, D_MODEL], f32, h_off)
    m_off = region(2 * TT * BW * 4)
    y_off = region(TT * D_MODEL * 4)
    Y = at("mixed", [P, TT, D_MODEL], f32, y_off)
    XQT = new("xattn_q", [P, X_HEADS, SEQ], f32)
    KX = [new(f"xattn_k{i}", [P, X_HEADS, N_MEM], f32) for i in range(2)]
    VX = [new(f"xattn_v{i}", [P, TT, XW], f32) for i in range(2)]
    SG = new("gate_sigmoid", [P, TT, 512], f32)
    IDENT = new("identity", [P, P], f32)
    GT = new("gains_transposed", [P, 4 * KT], f32)
    gla_off = region(12 * P * 4 + 7 * 64 * 4 + 2 * 3 * P * 4 + GLA_DV * 4)
    ST = new("stats", [P, 192], f32)

    ROW = SG[:, 0, 0:SEQ]
    DIAG = SG[:, 1, 0:SEQ]
    ONESQ = SG[:, 1, SEQ:SEQ + P]
    MQ = [at(f"mem_again{q}", [P, TT, 512], f32, m_off + o) for q, o in enumerate((12288, 16384, 20480, 0))]

    LGH = at("log_gate_high", [P, TT, KEYW], f32r, h_off)
    LGL = at("log_gate_low", [P, TT, KEYW], f32r, h_off + TT * KEYW * 4)
    PX = at("xattn_probs", [P, 2, 512], f32, h_off + 2 * TT * KEYW * 4)
    QK = at("gla_qk", [P, 2 * FT, SEQ], f32, m_off)
    V = at("gla_v", [P, TT, BW], f32, m_off + 2 * FT * SEQ * 4)
    E = at("gla_decayed", [P, LEVELS, 3, SEQ], f32, a_off)
    QKP = at("gla_qk_product", [P, FT, SEQ], f32, a_off + LEVELS * 3 * SEQ * 4)
    WG = at("gate_weights", [RANK + 1, KEYW], f32, y_off)
    GLT = at("gate_rank_t", [RANK + 1, SEQ], f32, y_off + KEYW * 4)
    ZA = at("gate_abs", [P, KEYW], f32, y_off + KEYW * 4 + 1536)
    ZL = at("gate_log", [P, KEYW], f32, y_off + 2 * KEYW * 4 + 1536)
    ZG = at("gate_sum", [P, KEYW], f32, y_off + 3 * KEYW * 4 + 1536)
    PATTERN = at("decay_patterns", [P, 12, P], f32r, gla_off)
    LMASK = at("level_masks", [P, 7, 64], i32, gla_off + 12 * P * 4)
    AT = at("gla_attn_t", [P, 2, 3, P], f32, gla_off + 12 * P * 4 + 7 * 64 * 4)
    GN = at("gla_norm_rows", [P, GLA_DV], f32, gla_off + 12 * P * 4 + 7 * 64 * 4 + 2 * 3 * P * 4)
    PT0 = at("xattn_probs_t", [P, 2, 512], f32, m_off)
    PAT0 = at("pattern_scratch", [P, 9, P], f32, a_off)
    MSK0 = at("mask_scratch", [P, 7, 64], f32, a_off + 9 * P * 4)

    NQT = at("nsa_q", [P, NSA_HEADS, SEQ], f32, m_off)
    NKT = at("nsa_k", [P, 2, NSA_GROUPS, SEQ], f32, m_off + NSA_HEADS * SEQ * 4)
    NV = at("nsa_v", [P, 2, TT, KVW], f32, m_off + NSA_HEADS * SEQ * 4 + 4096)
    KVC = at("nsa_cmp_kv", [P, 2, NSA_GROUPS, SEQ], f32, m_off + NSA_HEADS * SEQ * 4 + 8192)
    BK = at("cmp_blocks_split", [P, 2, CMP_LEN * 2 * NB + P], f32r, b_off)
    BKT = at("cmp_blocks", [P, CMP_LEN, NB], f32, b_off + 16384)
    W2 = at("cmp_w2", [P, 2, 2, HD], f32, b_off + 20224)
    HT = at("cmp_hidden_rows", [2 * NB, 2, CMP_HIDDEN], f32, b_off + 22272)
    HB = at("cmp_hidden_parts", [P, 2, 2, 64], f32, b_off + 24320)
    HID = at("cmp_hidden", [P, 2, 2, 32], f32, b_off + 25344)
    HSG = at("cmp_hidden_sigmoid", [P, 2, 2, 32], f32, b_off + 25856)
    KC = at("cmp_k", [P, 32], f32, b_off + 26368)
    VC = at("cmp_v", [N_CMP, NSA_GROUPS, HD], f32, b_off + 26496)
    PC = at("cmp_probs", [P, 3, 8, 16], f32, b_off + 27520)
    PTC = at("cmp_probs_t", [16, 2, 256], f32, b_off + 29056)
    GATES = at("nsa_gates", [P, TT, 64], f32, b_off + 31104)
    PE0 = at("cmp_pe", [CMP_LEN, 2, HD], f32, b_off + 31616)
    PET = at("cmp_pe_t", [P, 2, CMP_LEN], f32, y_off)
    GTR = at("nsa_gates_t", [NSA_HEADS * N_BRANCH, SEQ], f32, y_off + 1024)
    CB = at("causal_bias", [P, P], bf16, gla_off)
    IDB = at("identity_bf16", [P, P], bf16, gla_off + 256)
    CMB = at("cmp_bias", [P, TT, 16], bf16, gla_off + 512)
    ROWOK = at("cmp_row_visible", [P, TT], f32, gla_off + 576)
    PN = at("nsa_probs", [P, 2, 512], f32, gla_off + 608)
    PT1 = at("nsa_probs_t", [P, 2, 512], f32, gla_off + 608 + 4096)
    GPOST = [at(f"post_gain{i}", [P, D_MODEL], f32, m_off + 4096) for i in range(2)]
    YSS = [ST[:, 168 + 8 * l:176 + 8 * l].rearrange("p (i j) -> p i j", i=TT) for l in range(2)]
    HSS = ST[:, 184:192].rearrange("p (i j) -> p i j", i=TT)
    G0 = at("gains_raw", [4 * KT, P], f32, m_off)
    JUNK = at("squares", [P, D_MODEL], f32, m_off + 12288 + 2048)

    SS = ST[:, 0:16]
    RSTD = ST[:, 16:32]
    NM = ST[:, 32:36]
    RS = ST[:, 36:40]
    RI = ST[:, 40:44]
    MX = ST[:, 44:48]
    SSG = ST[:, 48:56]
    RG = ST[:, 56:64]
    DQ = ST[:, 64:72]
    MC = ST[:, 72:96]
    SC = ST[:, 96:120]
    FC = ST[:, 120:144]
    ONES = ST[:, 144:145]
    HALF = ST[:, 160:168]

    ctx = ExitStack()
    with ctx:
        PS = [ctx.enter_context(nc.psum_tensor(f"bank{i}", [P, 512], f32)) for i in range(8)]

        def sem(name):
            return ctx.enter_context(nc.semaphore(name))

        raw_in = [sem(f"raw_piece_in{i}") for i in range(RING)]
        hi_ready, lo_ready, piece_used = sem("high_ready"), sem("low_ready"), sem("piece_used")
        act_drained, dve_drained = sem("drained_by_scalar"), sem("drained_by_vector")
        mem_in = [sem(f"mem_in{q}") for q in range(4)]
        mem_again = [sem(f"mem_again_in{q}") for q in range(4)]
        diag_ready = sem("diagonal_ready")
        x_in = [sem(f"x_in{i}") for i in range(2)]
        gains_in, wg_in, gn_in, res_in = sem("gains_in"), sem("gate_weights_in"), sem("gla_norm_in"), sem("residual_in")
        w2_in, pe_in = sem("cmp_w2_in"), sem("cmp_pe_in")
        post_in = [sem(f"post_gain_in{i}") for i in range(2)]
        stored = sem("stored")
        consts, consts2 = sem("constants_ready"), sem("nsa_constants_ready")
        pool_step, dve_step, act_step = sem("pool_step"), sem("vector_step"), sem("scalar_step")
        squared, normed = sem("squared"), sem("normed")
        mean_ready, rstd_ready = sem("mean_square"), sem("reciprocal_root")
        small_t, small_c = sem("small_transposed"), sem("small_copied")
        tr_ready, tr_hi, tr_lo = sem("transposed"), sem("transposed_high"), sem("transposed_low")
        z_ready, z_exp, lg_ready = sem("gate_logits"), sem("gate_ln"), sem("log_gates")
        d_ready, e_ready, qk_ready = sem("decay_logs"), sem("decays"), sem("decayed")
        qkp_ready, dq_ready, dq_kept = sem("qk_products"), sem("qk_sums"), sem("qk_sums_kept")
        s_ready, at_ready = sem("gla_scores"), sem("gla_attn")
        o_ready, o_kept, o_sq, o_norm = sem("gla_out"), sem("gla_out_kept"), sem("gla_out_squared"), sem("gla_out_normed")
        sc_ready, mx_ready, pr_ready, pn_ready = sem("scores"), sem("maxima"), sem("probs"), sem("probs_scaled")
        pt_ready, pt_kept, pv_ready, head_kept = sem("probs_t"), sem("probs_t_kept"), sem("pv_done"), sem("head_kept")
        cs_ready, cs_shift, cs_exp, cs_done = sem("cmp_scores"), sem("cmp_shifted"), sem("cmp_exps"), sem("cmp_probs_done")
        blk_ready, hid_exp, hid_ready = sem("cmp_blocks_ready"), sem("hidden_exps"), sem("hidden_ready")
        kvc_ready, kvc_kept = sem("cmp_kv_ready"), sem("cmp_kv_kept")
        gate_exp, gate_ready, mixed_gated = sem("gate_exps"), sem("gates_ready"), sem("mixed_gated")
        sg_exp = sem("sigmoid_exps")
        y_sq, res_ready = sem("projected_squared"), sem("residual_ready")
        hid_rows, hid_t, hid_parts, hid_sum = sem("hidden_rows"), sem("hidden_transposed"), sem("hidden_parts"), sem("hidden_sums")
        gates_sig, gates_t = sem("gates_sigmoid"), sem("gates_transposed")

        steps = {}

        def put(slot, *step):
            steps.setdefault(slot, []).append(step)

        for ch in chunks:
            if ch.name[2:4] in ("r0", "r1", "r2", "xg"):
                late = 4 if ch.name == "g_r0" else 0
                put(ch.last + late, "gated_drain", ch, 0)
                put(ch.last + late + 1, "gated_drain", ch, 1)
            elif ch.kind == CMP:
                put(ch.last, "hidden_drain", ch)
            else:
                put(ch.last, "drain", ch)
        for kt in range(4):
            put(-1, "transpose", "mem0", kt)
        for kt in range(4, KT):
            put((kt - 4) // 2, "transpose", "mem0", kt)
        put(2, "square", 0, 0)
        put(3, "square", 0, 1)
        put(4, "diagonal", 0)
        put(5, "transpose", "row0", 0)
        for i in range(TT):
            put(6 + i, "square", 1, i)
            put(8 + i, "scale", i)
        for kt in range(KT):
            put(10 + kt // 2, "transpose", "x0", kt)
        q0 = C["g_lr"].last
        put(q0 + 1, "gate", 0)
        put(q0 + 4, "gate", 1)
        for d in range(12):
            put(q0 + 8 + d, "decay", 0, d)
        k0 = C["g_qk2"].last
        put(k0, "qk_products")
        put(k0 + 2, "qk_sums")
        for l in range(LEVELS):
            put(k0 + 1 + l, "decayed", 0, l)
        s0 = k0 + LEVELS + 1
        for h in (0, 1):
            put(s0 + 2 * h, "gla_scores", h, 0)
            put(s0 + 2 * h + 1, "gla_scores", h, 1)
            o0 = max(s0 + 2 * h + 2, C[f"g_v{(384 * h + 383) // 512}"].last + 1)
            put(o0, "gla_out", h)
        s1 = max(s0 + 4, o0 + 1)
        for d in range(12):
            put(s1 + d, "decay", 1, d)
        for l in range(LEVELS):
            put(s1 + 6 + l + (1 if l >= 4 else 0), "decayed", 1, l)
        s2 = s1 + 15
        for h in (2, 3):
            put(s2 + 2 * (h - 2), "gla_scores", h, 0)
            put(s2 + 2 * (h - 2) + 1, "gla_scores", h, 1)
            o0 = max(s2 + 2 * (h - 2) + 2, C[f"g_v{(384 * h + 383) // 512}"].last + 1)
            put(o0, "gla_out", h)
        put(o0 + 1, "gla_root")
        for h in range(GLA_HEADS):
            put(o0 + 2 + h, "gla_norm", h)
        ax = o0 + 2
        t_unit = 0
        s_uses = []
        tables = dict(units=[], attn=[])
        for h in range(X_HEADS):
            put(ax + h, "scores", ("x", 0, h), len(tables["attn"]))
            s_uses.append(("attn", len(tables["attn"])))
            put(ax + h + 2, "probs_t", ("x", 0, h), t_unit, len(tables["attn"]))
            put(ax + h + 3, "pv", ("x", 0, h), t_unit, len(tables["attn"]))
            tables["attn"].append(t_unit)
            t_unit += 1
        def gated_to_b(stage, l, after_mem, after_r0):
            for k in range(4):
                put(after_mem + 3 + k // 2, "transpose", stage, 12 + k)
                put(after_r0 + 5 + k // 2, "transpose", stage, k)
                put(C[f"{l}_r2"].first + 4 + k // 2, "transpose", stage, 4 + k)
                put(C[f"{l}_out0"].first + 2 + k // 2, "transpose", stage, 8 + k)

        gated_to_b("y0", "g", C["g_r1"].first, C["g_r1"].first)
        for kt in range(KT):
            put(C["g_out0"].first + 6 + kt // 2, "transpose", "mem1", kt)
        m0 = C["mem_v1"].first
        put(m0, "residual_root", 0)
        for k in range(4 * TT):
            put(m0 + 1 + k // 2, "residual", 0, k)
            put(m0 + 2 + k // 2, "stream_square", k)
        put(m0 + 5, "stream_root")
        for q in range(4):
            put(m0 + 6 + q // 2, "stream_scale", q)
        for kt in range(KT):
            put(m0 + 7 + kt // 2, "transpose", "x1", kt)
        put(C["mem_k1"].last - 3, "diagonal", 1)
        put(C["mem_k1"].last - 2, "transpose", "row1", 0)
        put(C["n_gl"].last + 2, "nsa_gates")
        put(C["n_gl"].last, "pe_t")
        put(C["n_gl"].last + 3, "blocks", 0)
        put(C["n_gl"].last + 6, "blocks", 1)
        for g, name in enumerate(("n_wk1", "n_wv1")):
            put(C[name].last + 1, "hidden", g)
            put(C[name].last + 4, "cmp_kv", g)
        for j in range(3):
            u0 = C[f"n_q{j}"].last + 1
            put(u0, "cmp_scores", j)
            s_uses.append(("cmp", j))
            u = u0
            for h in range(4 * j, 4 * j + 4):
                for br in (0, 1, 2):
                    unit = ("cmp", 1, h) if br == 0 else ("nsa", br - 1, h)
                    at_i = len(tables["attn"])
                    if br:
                        put(u, "scores", unit, at_i)
                        s_uses.append(("attn", at_i))
                        tables["attn"].append(t_unit)
                        put(u + 2, "probs_t", unit, t_unit, at_i)
                        put(u + 3, "pv", unit, t_unit, at_i)
                        u += 1
                    else:
                        put(u + 2, "probs_t", unit, t_unit, None)
                        put(u + 3, "pv", unit, t_unit, None)
                    t_unit += 1
        ux = max(u + 1, C["n_xq"].last + 1)
        for h in range(X_HEADS):
            at_i = len(tables["attn"])
            put(ux + h, "scores", ("x", 1, h), at_i)
            s_uses.append(("attn", at_i))
            tables["attn"].append(t_unit)
            put(ux + h + 2, "probs_t", ("x", 1, h), t_unit, at_i)
            put(ux + h + 3, "pv", ("x", 1, h), t_unit, at_i)
            t_unit += 1
        gated_to_b("y1", "n", C["n_r0"].first, C["n_r1"].first - 2)
        put(C["n_out3"].last, "residual_root", 1)
        for k in range(4 * TT):
            put(C["n_out3"].last, "residual", 1, k)

        def last_slot(kind, test):
            return max(s for s, l in steps.items() for st in l if st[0] == kind and test(st))

        ready0 = last_slot("pv", lambda st: st[1][0] == "x" and st[1][1] == 0)
        ready1 = last_slot("pv", lambda st: st[1][1] == 1 and st[1][0] == "x")
        assert ready0 <= C["g_xg"].last and ready1 <= C["n_xg"].last, (ready0, C["g_xg"].last, ready1, C["n_xg"].last)

        def rank(st):
            if st[0] == "probs_t":
                return 1 if st[1][0] == "cmp" else 4
            return {"drain": 0, "scores": 2, "cmp_scores": 2, "pv": 3, "gated_drain": 6}.get(st[0], 5)

        for s in steps:
            steps[s].sort(key=rank)
        slots = list(range(-1, pieces))
        seq = [st for s in slots for st in steps.get(s, ())]
        drained_at = {}
        for st in seq:
            if "drain" in st[0] and st[2:] != (0,):
                assert st[1].c == len(drained_at)
                drained_at[st[1].c] = True
        t_order = {}
        for st in seq:
            if st[0] == "transpose":
                t_order[st[1:]] = len(t_order)
        units = [st for st in seq if st[0] == "probs_t"]
        assert [u[2] for u in units] == list(range(t_unit))
        heads = []
        for u in units:
            key = (u[1][0] == "x", u[1][1] if u[1][0] == "x" else 1, u[1][2])
            if key not in heads:
                heads.append(key)

        def head_no(unit):
            return heads.index((unit[0] == "x", unit[1] if unit[0] == "x" else 1, unit[2]))

        def t_source(stage):
            return {"mem0": Y, "x0": H, "y0": Y, "x1": Y, "y1": Y}[stage]

        def t_done(stage):
            return max(n for (st, kt), n in t_order.items() if st == stage) + 1

        def t_dest(stage):
            return {"mem0": (AHI, ALO, 2 * KT), "mem1": (BHI, BLO, 3 * KT), "x0": (BHI, BLO, 0), "y0": (AHI, ALO, None),
                    "x1": (AHI, ALO, KT), "y1": (BHI, BLO, None)}[stage]

        def lhs_ready(ch, j):
            stage = {"mem_k0": "mem0", "mem_v0": "mem0", "mem_k1": "mem1", "mem_v1": "mem1"}.get(
                ch.name, ("y" if "out" in ch.name else "x") + ("0" if ch.name[0] == "g" else "1"))
            return max(t_order[stage, kt] for kt in ch.order[:(j + 1) * ch.tiles]) + 1

        def lhs_free(stage):
            return {"mem0": None, "mem1": "g_r2", "x0": None, "y0": "mem_k0", "x1": "g_out3", "y1": "mem_k1"}.get(stage)

        def piece_view(buf, n):
            ch, j = piece_of[n]
            return buf[:, n % RING, 0:ch.tiles * ch.width].rearrange("p (t w) -> p t w", t=ch.tiles)

        def acc_bank(ch, i):
            return PS[2 * (ch.c % 2) + i]

        def unit_probs(unit):
            return (PX, PT0) if unit[:2] == ("x", 0) else (PN, PT1)

        def decay_unit(p, d):
            g, rest = divmod(d, 6)
            ft, i = divmod(rest, 2)
            return g, ft, i

        def head_rows(h):
            t0 = 3 * (h // 2)
            return [(t0, 0, P), (t0 + 1, 0, 64)] if h % 2 == 0 else [(t0 + 2, 0, P), (t0 + 1, 64, P)]

    
        gated_names = ["g_r0", "g_xg", "g_r1", "g_r2", "n_xg", "n_r0", "n_r1", "n_r2"]

        def gated_no(ch):
            return gated_names.index(ch.name)

        def dve_drains(c):
            return sum(ch.kind != CMP and ch.name not in gated_names for ch in chunks[:c + 1])

        block = ctx.enter_context(nc.Block())

        @block.sync
        def _(sp):
            def piece_in(n):
                ch, j = piece_of[n]
                if n >= RING:
                    sp.wait_ge(lo_ready, n - RING + 1)
                k0 = ch.order[j * ch.tiles]
                rows = weights[ch.w][k0 * P:(k0 + ch.tiles) * P, ch.col:ch.col + ch.width]
                sp.dma_start(piece_view(RAW, n), rows.rearrange("(t p) w -> p t w", p=P)).then_inc(raw_in[n % RING], 16)

            def mem_quarter(q, dst):
                return sp.dma_start(dst, a["mem"][0, :, 512 * q:512 * (q + 1)].rearrange("(i p) w -> p i w", p=P))

            for g, name in enumerate(("ln_pre", "ln_mem")):
                sp.dma_start(G0[2 * KT * g:2 * KT * (g + 1), :],
                             a[name].rearrange("l (t p) -> (l t) p", p=P)).then_inc(gains_in, 16)
            for q in range(4):
                mem_quarter(q, Y[:, :, 512 * q:512 * (q + 1)]).then_inc(mem_in[q], 16)
                piece_in(q)
            for s in range(1, pieces):
                if s + LEAD < pieces:
                    piece_in(s + LEAD)
                if s in (1, 3):
                    i = s // 2
                    sp.dma_start(H[:, i, :], a["x"][0, i * P:(i + 1) * P, :]).then_inc(x_in[i], 16)
                if s == 6:
                    sp.dma_start(GN[:, :], a["gla_norm"][0:1, :].to_broadcast([P, GLA_DV])).then_inc(gn_in, 16)
                if s == C["mem_k0"].first + RING:
                    sp.wait_ge(tr_lo, t_done("mem0"))
                    sp.wait_ge(squared, TT)
                    sp.dma_start(WG[0:RANK, :], a["gla_w_gate_lr"][0]).then_inc(wg_in, 16)
                    sp.dma_start(WG[RANK:RANK + 1, :], a["gla_b_gate"][0:1, :]).then_inc(wg_in, 16)
                if s == C["g_r2"].first:
                    sp.wait_ge(pt_ready, X_HEADS)
                    sp.wait_ge(qk_ready, 2 * LEVELS)
                    for i in range(TT):
                        sp.dma_start(H[:, i, :], a["x"][0, i * P:(i + 1) * P, :]).then_inc(res_in, 16)
                    sp.dma_start(GPOST[0][:, :], a["ln_post"][0:1, :].to_broadcast([P, D_MODEL])).then_inc(post_in[0], 16)
                if s == C["g_out0"].first:
                    sp.wait_ge(o_norm, GLA_HEADS)
                    sp.wait_ge(pv_ready, X_HEADS)
                    for q in range(4):
                        mem_quarter(q, MQ[q][:, :, :]).then_inc(mem_again[q], 16)
                if s == C["n_cmp"].first + RING - 1:
                    sp.wait_ge(piece_used, C["mem_k1"].last + 1)
                    for g, w in enumerate(("nsa_wk2", "nsa_wv2")):
                        sp.dma_start(W2[:, g], a[w][0].rearrange("(t p) d -> p t d", p=P)).then_inc(w2_in, 16)
                    for g, w in enumerate(("nsa_pe_k", "nsa_pe_v")):
                        sp.dma_start(PE0[:, g, :], a[w][0]).then_inc(pe_in, 16)
                if s == C["n_r1"].first:
                    sp.wait_ge(sc_ready, len(tables["attn"]))
                    sp.wait_ge(cs_ready, 3)
                    sp.dma_start(GPOST[1][:, :], a["ln_post"][1:2, :].to_broadcast([P, D_MODEL])).then_inc(post_in[1], 16)
            for k in range(4 * TT):
                i, q = divmod(k, 4)
                sp.wait_ge(res_ready, 4 * TT + k + 1)
                sp.dma_start(out[0, i * P:(i + 1) * P, 512 * q:512 * (q + 1)], H[:, i, 512 * q:512 * (q + 1)])\
                    .then_inc(stored, 16)
            sp.wait_ge(stored, 16 * 4 * TT)

        @block.gpsimd
        def _(pool):
            count = [0]

            def step(ins):
                count[0] += 1
                ins.then_inc(pool_step, 1)
                pool.wait_ge(pool_step, count[0])

            def keep_where(view, value_of, pattern, base_, mult, fill):
                step(nc.gpsimd.affine_select(out=view, in_=view, compare_op=ALU.is_ge, fill=fill, base=base_,
                                             pattern=pattern, channel_multiplier=mult))

            powers = [0]

            def rstd(v):
                pool.wait_ge(mean_ready, powers[0] + 1)
                nc.gpsimd.tensor_tensor(v, v, HALF[:, 0:v.shape[1]], ALU.pow).then_inc(rstd_ready, 1)
                powers[0] += 1

            step(nc.gpsimd.memset(IDENT[:, :], 0.0))
            step(nc.gpsimd.affine_select(out=IDENT[:, :], in_=IDENT[:, :], compare_op=ALU.not_equal, fill=1.0, base=0,
                                         pattern=[[-1, P]], channel_multiplier=1))
            step(nc.gpsimd.memset(HALF, -0.5))
            nc.gpsimd.memset(ONES, 1.0).then_inc(consts, 1)
            for c in range(2 * TT):
                rstd(RSTD[:, c:c + 1])
            pool.wait_ge(piece_used, C["mem_k0"].last + 1)
            step(nc.gpsimd.memset(PAT0[:, :, :], 1.0))
            step(nc.gpsimd.memset(MSK0[:, :, :], 1.0))
            for l in range(7):
                h = 1 << l
                v = PAT0[:, l, :].rearrange("p (b w o) -> p b w o", w=2, o=h)
                nb = P // (2 * h)
                keep_where(v[:, :, 0, :], None, [[-2 * h, nb], [-1, h]], -1, 1, 0.0)
                keep_where(v[:, :, 0, :], None, [[2 * h, nb], [0, h]], h - 1, -1, 0.0)
                keep_where(v[:, :, 1, :], None, [[-2 * h, nb], [0, h]], -h, 1, 0.0)
                keep_where(v[:, :, 1, :], None, [[2 * h, nb], [1, h]], h, -1, 0.0)
                m = MSK0[:, l, :].rearrange("p (b o) -> p b o", o=h)
                keep_where(m, None, [[-2 * h, nb], [0, h]], 0, 1, 0.0)
                keep_where(m, None, [[2 * h, nb], [0, h]], h - 1, -1, 0.0)
            keep_where(PAT0[:, 7, :], None, [[-1, P]], -1, 1, 0.0)
            keep_where(PAT0[:, 8, :], None, [[1, P]], 0, -1, 0.0)
            for d0, s0_, n_ in ((0, 0, 8), (8, 4, 3), (11, 8, 1)):
                step(nc.gpsimd.tensor_copy(PATTERN[:, d0:d0 + n_, :], PAT0[:, s0_:s0_ + n_, :]))
            nc.gpsimd.tensor_copy(LMASK[:, :, :], MSK0[:, :, :]).then_inc(consts, 1)
            nc.gpsimd.memset(AT[:, :, :, :], 0.0).then_inc(consts, 1)
            rstd(RG)
            pool.wait_ge(pv_ready, X_HEADS)
            pool.wait_ge(o_norm, GLA_HEADS)
            step(nc.gpsimd.memset(CB[:, :], 0.0))
            step(nc.gpsimd.memset(IDB[:, :], 0.0))
            step(nc.gpsimd.memset(CMB[:, :, :], 0.0))
            step(nc.gpsimd.memset(ROWOK[:, :], 1.0))
            keep_where(CB[:, :], None, [[-1, P]], 0, 1, MASKED)
            step(nc.gpsimd.affine_select(out=IDB[:, :], in_=IDB[:, :], compare_op=ALU.not_equal, fill=1.0, base=0,
                                         pattern=[[-1, P]], channel_multiplier=1))
            keep_where(CMB[:, :, :], None, [[P, TT], [-CMP_STRIDE, 16]], -(CMP_LEN - 1), 1, MASKED)
            keep_where(ROWOK[:, :], None, [[P, TT]], -(CMP_LEN - 1), 1, 0.0)
            nc.gpsimd.memset(ST[:, 153:154], 1.0).then_inc(consts2, 1)
            for c in (4, 6, 8):
                rstd(RSTD[:, c:c + TT])

        @block.tensor
        def _(pe):
            def transpose(stage, kt, n):
                if n >= 4:
                    pe.wait_ge(tr_lo, n - 3)
                for i in range(TT):
                    o = PS[4 + n % 4][:, i * P:(i + 1) * P]
                    if stage in ("row0", "row1"):
                        last = nc.tensor.matmul(o, ONESQ, DIAG[:, i * P:(i + 1) * P], start=i == 0, stop=True,
                                                skip_group_check=True)
                    elif stage == "mem1":
                        last = nc.tensor.transpose(o, MQ[kt // 4][:, i, kt % 4 * P:(kt % 4 + 1) * P], IDENT[:, :])
                    else:
                        last = nc.tensor.transpose(o, t_source(stage)[:, i, kt * P:(kt + 1) * P], IDENT[:, :])
                last.then_inc(tr_ready, 1)

            def products(n):
                ch, j = piece_of[n]
                if j == 0:
                    if ch.c >= 2:
                        pe.wait_ge(act_drained, ch.c - 1)
                        pe.wait_ge(dve_drained, dve_drains(ch.c - 2))
                    if ch.kind == CMP:
                        pe.wait_ge(blk_ready, 1 if ch.lhs == "K" else 2)
                if ch.kind != CMP and (j == 0 or lhs_ready(ch, j) > lhs_ready(ch, j - 1)):
                    pe.wait_ge(tr_lo, lhs_ready(ch, j))
                pe.wait_ge(lo_ready, n + 1)
                hi, lo = piece_view(WHI, n), piece_view(WLO, n)
                last = None
                for t in range(ch.tiles):
                    kt = ch.order[j * ch.tiles + t]
                    first, end = j == 0 and t == 0, j == ch.n - 1 and t == ch.tiles - 1
                    if ch.kind == CMP:
                        g = "KV".index(ch.lhs)
                        for q, wt in enumerate((hi, lo)):
                            last = nc.tensor.matmul(acc_bank(ch, 0)[:, 0:CMP_HIDDEN], BK[:, g, 2 * NB * kt:2 * NB * kt + P],
                                                    wt[:, t, :], start=first and q == 0, stop=end and q == 1)
                        continue
                    xh, xl = (AHI, ALO) if ch.lhs == "A" else (BHI, BLO)
                    outs = []
                    if ch.kind == TM:
                        outs = [(acc_bank(ch, i)[:, 0:ch.width], True, slice(0, ch.width), i) for i in range(TT)]
                    if ch.kind == NARROW:
                        flat = [b[:, n % RING, t * ch.width:t * ch.width + P] for b in (WHI, WLO)]
                        for q, (wt, xt) in enumerate(((flat[0], xh), (flat[1], xh), (flat[0], xl))):
                            last = nc.tensor.matmul(acc_bank(ch, 0)[:, 0:SEQ], wt, xt[:, kt, :], start=first and q == 0,
                                                    stop=end and q == 2)
                    if ch.kind == FM:
                        outs = [(acc_bank(ch, b // 2)[:, b % 2 * SEQ:(b % 2 + 1) * SEQ], b % 2 == 0, slice(b * P, (b + 1) * P), None)
                                for b in range(4)]
                    if ch.kind == MIX:
                        outs = [(acc_bank(ch, 0)[:, b * SEQ:(b + 1) * SEQ], b == 0, slice(b * P, (b + 1) * P), None)
                                for b in range(2)]
                        outs += [(acc_bank(ch, 1)[:, i * KVW:(i + 1) * KVW], i == 0, slice(KVW, 2 * KVW), i) for i in range(TT)]
                    for o, opens, w, i in outs:
                        for q, (wt, xt) in enumerate(((hi, xh), (lo, xh), (hi, xl))):
                            ww = wt[:, t, w]
                            if i is None:
                                args = (ww, xt[:, kt, :])
                            else:
                                args = (xt[:, kt, i * P:(i + 1) * P], ww)
                            last = nc.tensor.matmul(o, *args, start=first and opens and q == 0, stop=end and q == 2,
                                                    skip_group_check=True)
                last.then_inc(piece_used, 1)

            def score_bank_free(s):
                if s >= 2:
                    kind, k = s_uses[s - 2]
                    if kind == "attn":
                        pe.wait_ge(pr_ready, k + 1)
                    else:
                        pe.wait_ge(cs_shift, k + 1)

            pe.wait_ge(consts, 1)
            pe.wait_ge(gains_in, 32)
            nc.tensor.transpose(PS[0][:, 0:4 * KT], G0[:, :], IDENT[0:4 * KT, 0:4 * KT]).then_inc(small_t, 1)
            pe.wait_ge(small_c, 1)
            d_no = s_no = 0
            for s in slots:
                if s >= 0:
                    products(s)
                for st in steps.get(s, ()):
                    what = st[0]
                    if what == "transpose":
                        stage, kt = st[1:]
                        n = t_order[stage, kt]
                        if stage == "mem0" and kt % 4 == 0:
                            pe.wait_ge(mem_in[kt // 4], 16)
                        if stage == "mem1" and kt % 4 == 0:
                            pe.wait_ge(mem_again[kt // 4], 16)
                        if stage in ("row0", "row1"):
                            pe.wait_ge(diag_ready, 1 + int(stage[-1]))
                        if stage == "x0" and kt == 0:
                            pe.wait_ge(normed, TT)
                        if stage in ("y0", "y1") and kt % 4 == 0:
                            gated = C[f"{'g' if stage == 'y0' else 'n'}_{'xg' if kt == 12 else f'r{kt // 4}'}"]
                            pe.wait_ge(mixed_gated, TT * (gated_no(gated) + 1))
                            if kt == 12:
                                pe.wait_ge(pt_kept, X_HEADS if stage == "y0" else t_unit)
                                pe.wait_ge(head_kept, X_HEADS if stage == "y0" else len(heads))
                        if stage == "x1" and kt % 4 == 0:
                            pe.wait_ge(normed, TT + TT * (kt // 4 + 1))
                        transpose(stage, kt, n)
                    elif what == "gate":
                        i, = st[1:]
                        pe.wait_ge(act_drained, C["g_lr"].c + 1)
                        pe.wait_ge(wg_in, 32)
                        if i == 1:
                            pe.wait_ge(lg_ready, 1)
                        for k, (c0, w) in enumerate(((0, 512), (512, KEYW - 512))):
                            last = nc.tensor.matmul(PS[6 + k][:, 0:w], GLT[:, i * P:(i + 1) * P], WG[:, c0:c0 + w],
                                                    start=True, stop=True)
                        last.then_inc(z_ready, 1)
                    elif what == "decay":
                        p, d = st[1:]
                        g, ft, i = decay_unit(p, d)
                        if d_no == 0:
                            pe.wait_ge(lg_ready, TT)
                            pe.wait_ge(consts, 3)
                        if d_no >= 2:
                            pe.wait_ge(e_ready, d_no - 1)
                        if p == 1 and d == 0:
                            pe.wait_ge(o_kept, 2)
                        o = PS[4 + d_no % 2]
                        m = 4 * g * (i + 1)
                        for q, lg in enumerate((LGH, LGL)):
                            last = nc.tensor.matmul(o[:, :], lg[:, i, (3 * p + ft) * P:(3 * p + ft + 1) * P],
                                                    PATTERN[:, m:m + 4, :].rearrange("p l t -> p (l t)"),
                                                    start=q == 0, stop=q == 1)
                        last.then_inc(d_ready, 1)
                        d_no += 1
                    elif what == "qk_sums":
                        pe.wait_ge(qkp_ready, 1)
                        for i in range(TT):
                            for h in range(GLA_HEADS):
                                for k, (ft, r0, r1) in enumerate(head_rows(h)):
                                    last = nc.tensor.matmul(PS[7 - h % 2][:, h + i - h % 2:h + i - h % 2 + 1],
                                                            QKP[r0:r1, ft, i * P:(i + 1) * P], ONES[r0:r1, :],
                                                            start=i == 0 and h < 2 and k == 0, stop=k == 1,
                                                            skip_group_check=True)
                        last.then_inc(dq_ready, 1)
                    elif what == "gla_scores":
                        h, i = st[1:]
                        pe.wait_ge(qk_ready, LEVELS * (h // 2 + 1))
                        if h >= 1:
                            pe.wait_ge(at_ready, 2 * (h - 1) + i + 1)
                        else:
                            pe.wait_ge(dq_kept, 1)
                        o = PS[6 + i]
                        for l in range(LEVELS):
                            hf = 1 << l
                            for k, (ft, r0, r1) in enumerate(head_rows(h)):
                                ft -= 3 * (h // 2)
                                if l < 7:
                                    lhs = E[r0:r1, l, ft, i * P:(i + 1) * P]
                                    rhs = E[r0:r1, l, ft, i * P:(i + 1) * P].rearrange("p (b w o) -> p b w o", w=2, o=hf)[:, :, 1, :]
                                    dst = o[:, 64 * l:64 * (l + 1)].rearrange("p (b o) -> p b o", o=hf)
                                else:
                                    lhs = E[r0:r1, l, ft, 0:P]
                                    rhs = E[r0:r1, l, ft, P + 64 * i:P + 64 * (i + 1)]
                                    dst = o[:, 448:512]
                                last = nc.tensor.matmul(dst, lhs, rhs, start=l == 0 and k == 0, stop=k == 1,
                                                        skip_group_check=True)
                        last.then_inc(s_ready, 1)
                    elif what == "gla_out":
                        h, = st[1:]
                        pe.wait_ge(at_ready, 2 * h + 2)
                        pe.wait_ge(e_ready, 12 * (h // 2 + 1))
                        pe.wait_ge(act_drained, C[f"g_v{(384 * h + 383) // 512}"].c + 1)
                        pe.wait_ge(dve_drained, dve_drains(C[f"g_v{(384 * h + 383) // 512}"].c))
                        if h >= 1:
                            pe.wait_ge(o_kept, h)
                        v = slice(h * GLA_DV, (h + 1) * GLA_DV)
                        nc.tensor.matmul(PS[4][:, 0:GLA_DV], AT[:, h % 2, 0, :], V[:, 0, v], start=True, stop=True)
                        nc.tensor.matmul(PS[5][:, 0:GLA_DV], AT[:, h % 2, 2, :], V[:, 0, v], start=True, stop=False)
                        nc.tensor.matmul(PS[5][:, 0:GLA_DV], AT[:, h % 2, 1, :], V[:, 1, v], start=False, stop=True)\
                            .then_inc(o_ready, 1)
                    elif what == "scores":
                        unit, at_i = st[1:]
                        kind, which, h = unit
                        if at_i == 0:
                            pe.wait_ge(o_kept, GLA_HEADS)
                            pe.wait_ge(at_ready, 2 * GLA_HEADS)
                        score_bank_free(s_no)
                        bank = PS[4 + s_no % 2]
                        if kind == "x":
                            ch = C["g_xq" if which == 0 else "n_xq"]
                            pe.wait_ge(act_drained, ch.c + 1)
                            pe.wait_ge(dve_drained, dve_drains(ch.c))
                            for i in range(TT):
                                last = nc.tensor.matmul(bank[:, i * SEQ:(i + 1) * SEQ], XQT[:, h, i * P:(i + 1) * P],
                                                        KX[which][:, h, :], start=i == 0, stop=True, skip_group_check=True)
                        else:
                            ch = C[f"n_q{h // 4}"]
                            pe.wait_ge(act_drained, ch.c + 1)
                            pe.wait_ge(dve_drained, dve_drains(ch.c))
                            g = h // HPG
                            nc.tensor.matmul(bank[:, 0:P], NQT[:, h, 0:P], NKT[:, which, g, 0:P],
                                             start=True, stop=False, skip_group_check=True)
                            nc.tensor.matmul(bank[:, P:P + SEQ], NQT[:, h, P:SEQ], NKT[:, which, g, :],
                                             start=False, stop=False, skip_group_check=True)
                            nc.tensor.matmul(bank[:, 0:P], IDB[:, :], CB[:, :], start=False, stop=True, skip_group_check=True)
                            last = nc.tensor.matmul(bank[:, SEQ:SEQ + P], IDB[:, :], CB[:, :], start=False, stop=True,
                                                    skip_group_check=True)
                        last.then_inc(sc_ready, 1)
                        s_no += 1
                    elif what == "probs_t":
                        unit, t, at_i = st[1:]
                        kind, which, h = unit
                        if t >= 1:
                            pe.wait_ge(pt_kept, t)
                        if kind == "cmp":
                            pe.wait_ge(cs_done, h // 4 + 1)
                            for i in range(TT):
                                last = nc.tensor.transpose(PS[6][0:16, i * P:(i + 1) * P], PC[:, h // 4, 2 * (h % 4) + i, :],
                                                           IDENT[:, :])
                        else:
                            pe.wait_ge(pn_ready, at_i + 1)
                            pr = unit_probs(unit)[0]
                            for k in range(4 if kind == "x" else 3):
                                last = nc.tensor.transpose(PS[6][:, k * P:(k + 1) * P], pr[:, at_i % 2, k * P:(k + 1) * P],
                                                           IDENT[:, :])
                        last.then_inc(pt_ready, 1)
                    elif what == "pv":
                        unit, t, at_i = st[1:]
                        kind, which, h = unit
                        pe.wait_ge(pt_kept, t + 1)
                        e = head_no(unit)
                        o = [PS[7][:, i * P:(i + 1) * P] for i in range(TT)]
                        if kind in ("x", "cmp"):
                            if e >= 1:
                                pe.wait_ge(head_kept, e)
                        if kind == "x":
                            pt = unit_probs(unit)[1]
                            for i in range(TT):
                                for m in range(TT):
                                    last = nc.tensor.matmul(o[i], pt[:, t % 2, (2 * i + m) * P:(2 * i + m + 1) * P],
                                                            VX[which][:, m, h * HD:(h + 1) * HD], start=i == 0 and m == 0,
                                                            stop=m == 1, skip_group_check=True)
                        elif kind == "cmp":
                            for i in range(TT):
                                last = nc.tensor.matmul(o[i], PTC[0:N_CMP, t % 2, i * P:(i + 1) * P], VC[:, h // HPG, :],
                                                        start=i == 0, stop=False, skip_group_check=True)
                        else:
                            g = slice(h // HPG * HD, (h // HPG + 1) * HD)
                            pt = PT1
                            for i, blk, m in ((0, 0, 0), (1, 1, 0), (1, 2, 1)):
                                last = nc.tensor.matmul(o[i], pt[:, t % 2, blk * P:(blk + 1) * P], NV[:, which, m, g],
                                                        start=False, stop=which == 1 and blk != 1, skip_group_check=True)
                        last.then_inc(pv_ready, 1)
                    elif what == "pe_t":
                        pe.wait_ge(pe_in, 32)
                        for g in range(2):
                            last = nc.tensor.transpose(PS[4][:, g * CMP_LEN:(g + 1) * CMP_LEN], PE0[:, g, :],
                                                       IDENT[0:CMP_LEN, 0:CMP_LEN])
                        last.then_inc(small_t, 1)
                    elif what == "nsa_gates":
                        pe.wait_ge(gates_sig, 1)
                        for i in range(TT):
                            last = nc.tensor.transpose(PS[5][:, 64 * i:64 * i + NSA_HEADS * N_BRANCH], GTR[:, i * P:(i + 1) * P],
                                                       IDENT[0:NSA_HEADS * N_BRANCH, 0:NSA_HEADS * N_BRANCH])
                        last.then_inc(gates_t, 1)
                    elif what == "hidden":
                        g, = st[1:]
                        pe.wait_ge(act_drained, C["n_wk1" if g == 0 else "n_wv1"].c + 1)
                        for t in range(2):
                            last = nc.tensor.transpose(PS[6][:, 64 * t:64 * t + 2 * NB], HT[:, g, t * P:(t + 1) * P],
                                                       IDENT[0:2 * NB, 0:2 * NB])
                        last.then_inc(hid_t, 1)
                    elif what == "cmp_kv":
                        g, = st[1:]
                        pe.wait_ge(hid_ready, g + 1)
                        pe.wait_ge(w2_in, 32)
                        if g == 0:
                            for t in range(2):
                                last = nc.tensor.matmul(PS[6][:, 0:NB], W2[:, 0, t, :], HID[:, 0, t, 0:NB], start=t == 0, stop=t == 1)
                        else:
                            pe.wait_ge(kvc_kept, 1)
                            for gr in range(NSA_GROUPS):
                                for t in range(2):
                                    last = nc.tensor.matmul(PS[6][0:N_CMP, gr * HD:(gr + 1) * HD],
                                                            HID[:, 1, t, gr * N_CMP:(gr + 1) * N_CMP], W2[:, 1, t, :],
                                                            start=gr == 0 and t == 0, stop=t == 1, skip_group_check=True)
                        last.then_inc(kvc_ready, 1)
                    elif what == "cmp_scores":
                        j, = st[1:]
                        if j == 0:
                            pe.wait_ge(kvc_kept, 2)
                            pe.wait_ge(consts2, 1)
                        ch = C[f"n_q{j}"]
                        pe.wait_ge(act_drained, ch.c + 1)
                        pe.wait_ge(dve_drained, dve_drains(ch.c))
                        score_bank_free(s_no)
                        bank = PS[4 + s_no % 2]
                        for hh in range(4):
                            h = 4 * j + hh
                            for i in range(TT):
                                o = bank[:, (2 * hh + i) * 16:(2 * hh + i) * 16 + N_CMP]
                                g = h // HPG
                                nc.tensor.matmul(o, NQT[:, h, i * P:(i + 1) * P], KC[:, g * N_CMP:(g + 1) * N_CMP],
                                                 start=hh == 0 and i == 0, stop=False, skip_group_check=True)
                                last = nc.tensor.matmul(o, IDB[:, :], CMB[:, i, 0:N_CMP], start=False, stop=True,
                                                        skip_group_check=True)
                        last.then_inc(cs_ready, 1)
                        s_no += 1

        @block.scalar
        def _(act):
            count = [0]

            def step(ins):
                count[0] += 1
                ins.then_inc(act_step, 1)
                act.wait_ge(act_step, count[0])

            def split_high(n):
                act.wait_ge(raw_in[n % RING], 16 * (n // RING + 1))
                if n >= RING:
                    act.wait_ge(piece_used, n - RING + 1)
                ch, j = piece_of[n]
                w = slice(0, ch.tiles * ch.width)
                nc.scalar.activation(WHI[:, n % RING, w], RAW[:, n % RING, w], ACT.Copy).then_inc(hi_ready, 1)

            def transposed_high(stage, kt, n):
                act.wait_ge(tr_ready, n + 1)
                if kt in (0, 12) and lhs_free(stage):
                    act.wait_ge(piece_used, C[lhs_free(stage)].last + 1)
                src = PS[4 + n % 4][:, 0:SEQ]
                if stage in ("row0", "row1"):
                    nc.scalar.activation(ROW[:, 0:P], src[:, 0:P], ACT.Copy).then_inc(tr_hi, 1)
                    return
                hi, lo, gain = t_dest(stage)
                nc.scalar.activation(hi[:, kt, :], src, ACT.Copy, scale=1.0 if gain is None else GT[:, gain + kt:gain + kt + 1])\
                    .then_inc(tr_hi, 1)

            def square(stage, i, src):
                nc.scalar.activation(JUNK[:, 0:D_MODEL], src, ACT.Square, accum_out=SS[:, 2 * stage + i:2 * stage + i + 1])\
                    .then_inc(squared, 1)

            act.wait_ge(small_c, 1)
            s_no = d_no = 0
            for s in slots:
                if s > 0 and s + LEAD < pieces:
                    split_high(s + LEAD)
                if s == 0:
                    for n in range(LEAD + 1):
                        split_high(n)
                for st in steps.get(s, ()):
                    what = st[0]
                    if what == "square":
                        stage, i = st[1:]
                        if stage:
                            act.wait_ge(x_in[i], 16)
                        elif i == 0:
                            for q in range(4):
                                act.wait_ge(mem_in[q], 16)
                        if stage or i:
                            act.wait_ge(squared, TT * stage + i)
                        square(stage, i, (H if stage else Y)[:, i, :])
                    elif what == "transpose":
                        transposed_high(*st[1:], t_order[st[1:]])
                    elif what == "drain":
                        ch, = st[1:]
                        act.wait_ge(piece_used, ch.last + 1)
                        src, scale = acc_bank(ch, 0), 1.0
                        if ch.name.startswith("mem_k"):
                            dst = KX[int(ch.name[-1])][:, 0:2, :].rearrange("p b t -> p (b t)")
                        elif ch.name.startswith("mem_v"):
                            dst, scale = VX[int(ch.name[-1])][:, 0, :], RSTD[:, 0:1]
                            act.wait_ge(rstd_ready, TT)
                        elif ch.name == "g_lr":
                            act.wait_ge(dve_drained, dve_drains(ch.c))
                            dst, src = GLT[0:RANK, :], src[0:RANK, 0:SEQ]
                        elif ch.name.startswith("g_qk"):
                            j = int(ch.name[-1])
                            dst = QK[:, 4 * j:4 * j + 2, :].rearrange("p b t -> p (b t)")
                            scale = GLA_SCALE if 4 * j < FT else 1.0
                        elif ch.name.startswith("g_v"):
                            j = int(ch.name[-1])
                            dst = V[:, 0, 512 * j:512 * (j + 1)]
                        elif ch.name in ("g_xq", "n_xq"):
                            if ch.name == "n_xq":
                                act.wait_ge(sc_ready, X_HEADS)
                            dst = XQT[:, 0:2, :].rearrange("p b t -> p (b t)")
                        elif "out" in ch.name:
                            j = int(ch.name[-1])
                            k = 4 * (ch.name[0] == "n") + j
                            if j == 0:
                                act.wait_ge(mixed_gated, TT * 4 * (1 + (ch.name[0] == "n")))
                            if k:
                                act.wait_ge(y_sq, k)
                                act.wait_ge(act_drained, ch.c)
                            for i in range(TT):
                                nc.scalar.activation(SG[:, i, :], acc_bank(ch, i)[:, :], ACT.Square,
                                                     accum_out=YSS[k // 4][:, i, j:j + 1]).then_inc(act_drained if i else y_sq, 1)
                            continue
                        elif ch.name == "n_gl":
                            nc.scalar.activation(GTR[:, :], src[0:NSA_HEADS * N_BRANCH, 0:SEQ], ACT.Exp, scale=-1.0)\
                                .then_inc(act_drained, 1)
                            continue
                        elif ch.name == "n_cmp":
                            dst = KVC[:, 0].rearrange("p g t -> p (g t)")
                        elif ch.name in ("n_slc", "n_win"):
                            dst = NKT[:, 0 if ch.name == "n_slc" else 1].rearrange("p g t -> p (g t)")
                        elif ch.name.startswith("n_q"):
                            j = int(ch.name[-1])
                            dst = NQT[:, 4 * j:4 * j + 2, :].rearrange("p b t -> p (b t)")
                        nc.scalar.activation(dst, src if ch.kind == NARROW else src[:, 0:512], ACT.Copy, scale=scale)\
                            .then_inc(act_drained, 1)
                    elif what == "gated_drain":
                        ch, i = st[1:]
                        act.wait_ge(piece_used, ch.last + 1)
                        if gated_no(ch):
                            act.wait_ge(mixed_gated, TT * (gated_no(ch) - 1) + i + 1)
                        nc.scalar.activation(SG[:, i, :], acc_bank(ch, i)[:, :], ACT.Silu)\
                            .then_inc(act_drained if i else sg_exp, 1)
                    elif what == "hidden_drain":
                        ch, = st[1:]
                        g = "KV".index(ch.lhs)
                        act.wait_ge(piece_used, ch.last + 1)
                        nc.scalar.activation(HT[:, g, :], acc_bank(ch, 0)[0:2 * NB, 0:CMP_HIDDEN], ACT.Copy).then_inc(act_drained, 1)
                    elif what == "hidden":
                        g, = st[1:]
                        act.wait_ge(hid_t, g + 1)
                        nc.scalar.activation(HB[:, g, :, 0:2 * NB],
                                             PS[6][:, 0:128].rearrange("p (t n) -> p t n", t=2)[:, :, 0:2 * NB], ACT.Copy)\
                            .then_inc(hid_parts, 1)
                        act.wait_ge(hid_sum, g + 1)
                        nc.scalar.activation(HSG[:, g, :, 0:NB], HB[:, g, :, 0:NB], ACT.Exp, scale=-1.0).then_inc(hid_exp, 1)
                    elif what == "gate":
                        i, = st[1:]
                        act.wait_ge(z_ready, i + 1)
                        step(nc.scalar.activation(ZA[:, 0:512], PS[6][:, :], ACT.Abs))
                        step(nc.scalar.activation(ZA[:, 512:KEYW], PS[7][:, 0:KEYW - 512], ACT.Abs))
                        step(nc.scalar.activation(ZA[:, :], ZA[:, :], ACT.Exp, scale=-1.0))
                        nc.scalar.activation(ZL[:, :], ZA[:, :], ACT.Ln, bias=1.0).then_inc(z_exp, 1)
                    elif what == "decay":
                        p, d = st[1:]
                        g, ft, i = decay_unit(p, d)
                        act.wait_ge(d_ready, d_no + 1)
                        if d == 0 and p == 1:
                            act.wait_ge(s_ready, 4)
                        nc.scalar.activation(E[:, 4 * g:4 * g + 4, ft, i * P:(i + 1) * P],
                                             PS[4 + d_no % 2][:, :].rearrange("p (l t) -> p l t", l=4), ACT.Exp,
                                             scale=1.0 / GATE_TEMP).then_inc(e_ready, 1)
                        d_no += 1
                    elif what == "gla_out":
                        h, = st[1:]
                        act.wait_ge(o_kept, h + 1)
                        for i in range(TT):
                            nc.scalar.activation(SG[:, i, 0:GLA_DV], V[:, i, h * GLA_DV:(h + 1) * GLA_DV], ACT.Square,
                                                 accum_out=SSG[:, 2 * h + i:2 * h + i + 1]).then_inc(o_sq, 1)
                            act.wait_ge(o_sq, 2 * h + i + 1)
                    elif what == "scores":
                        unit, at_i = st[1:]
                        kind, which, h = unit
                        act.wait_ge(mx_ready, at_i + 1)
                        if at_i >= 2:
                            act.wait_ge(pt_ready, tables["attn"][at_i - 2] + 1)
                        pr = unit_probs(unit)[0]
                        bank, b = PS[4 + s_no % 2], at_i % 2
                        spans = ((0, SEQ), (SEQ, 2 * SEQ)) if kind == "x" else ((0, P), (P, P + SEQ))
                        if kind == "nsa" and at_i == X_HEADS:
                            act.wait_ge(consts2, 1)
                        for i, (c0, c1) in enumerate(spans):
                            ins = nc.scalar.activation(pr[:, b, c0:c1], bank[:, c0:c1], ACT.Exp, scale=ATT_SCALE,
                                                       bias=NM[:, 2 * b + i:2 * b + i + 1], accum_out=RS[:, 2 * b + i:2 * b + i + 1])
                        ins.then_inc(pr_ready, 1)
                        s_no += 1
                    elif what == "probs_t":
                        unit, t, at_i = st[1:]
                        act.wait_ge(pt_ready, t + 1)
                        if t >= 2:
                            act.wait_ge(pv_ready, t - 1)
                        if unit[0] == "cmp":
                            nc.scalar.activation(PTC[:, t % 2, :], PS[6][0:16, 0:SEQ], ACT.Copy).then_inc(pt_kept, 1)
                        else:
                            w = 512 if unit[0] == "x" else 384
                            nc.scalar.activation(unit_probs(unit)[1][:, t % 2, 0:w], PS[6][:, 0:w], ACT.Copy).then_inc(pt_kept, 1)
                    elif what == "pv":
                        unit, t, at_i = st[1:]
                        kind, which, h = unit
                        if kind == "x":
                            act.wait_ge(pv_ready, t + 1)
                            act.wait_ge(pn_ready, at_i + 1)
                            for i in range(TT):
                                ins = nc.scalar.activation(Y[:, i, BW + h * HD:BW + (h + 1) * HD], PS[7][:, i * P:(i + 1) * P],
                                                           ACT.Copy, scale=RI[:, 2 * (at_i % 2) + i:2 * (at_i % 2) + i + 1])
                            ins.then_inc(head_kept, 1)
                        elif kind == "nsa" and which == 1:
                            act.wait_ge(pv_ready, t + 1)
                            nc.scalar.activation(Y[:, :, h * HD:(h + 1) * HD], PS[7][:, 0:SEQ].rearrange("p (i d) -> p i d", i=TT),
                                                 ACT.Copy).then_inc(head_kept, 1)
                    elif what == "cmp_scores":
                        j, = st[1:]
                        act.wait_ge(cs_shift, j + 1)
                        nc.scalar.activation(PC[:, j, :, 0:N_CMP], PC[:, j, :, 0:N_CMP], ACT.Exp, scale=ATT_SCALE).then_inc(cs_exp, 1)
                        s_no += 1
                    elif what == "stream_square":
                        k, = st[1:]
                        i, q = divmod(k, 4)
                        act.wait_ge(res_ready, k + 1)
                        if k >= 2:
                            act.wait_ge(squared, 2 * TT + k - 1)
                        nc.scalar.activation(SG[:, k % 2, :], H[:, i, 512 * q:512 * (q + 1)], ACT.Square,
                                             accum_out=HSS[:, i, q:q + 1]).then_inc(squared, 1)

        @block.vector
        def _(dve):
            count = [0]

            def step(ins):
                count[0] += 1
                ins.then_inc(dve_step, 1)
                dve.wait_ge(dve_step, count[0])

            def split_low(n):
                dve.wait_ge(hi_ready, n + 1)
                ch, j = piece_of[n]
                w = slice(0, ch.tiles * ch.width)
                nc.vector.tensor_tensor(WLO[:, n % RING, w], RAW[:, n % RING, w], WHI[:, n % RING, w].bitcast(f32), ALU.subtract)\
                    .then_inc(lo_ready, 1)

            rstds = [0]

            def mean(dst, src, n):
                nc.vector.tensor_scalar(dst, src, 1.0 / n, EPS, ALU.mult, ALU.add).then_inc(mean_ready, 1)
                rstds[0] += 1

            def root():
                dve.wait_ge(rstd_ready, rstds[0])

            def transposed_low(stage, kt, n):
                dve.wait_ge(tr_hi, n + 1)
                src = PS[4 + n % 4][:, 0:SEQ]
                if stage in ("row0", "row1"):
                    nc.vector.tensor_copy(ROW[:, P:SEQ], src[:, P:SEQ]).then_inc(tr_lo, 1)
                    return
                hi, lo, gain = t_dest(stage)
                if gain is None:
                    last = nc.vector.tensor_tensor(lo[:, kt, :], src, hi[:, kt, :].bitcast(f32), ALU.subtract)
                else:
                    last = nc.vector.scalar_tensor_tensor(lo[:, kt, :], src, GT[:, gain + kt:gain + kt + 1],
                                                          hi[:, kt, :].bitcast(f32), ALU.mult, ALU.subtract)
                last.then_inc(tr_lo, 1)

            dve.wait_ge(small_t, 1)
            nc.vector.tensor_copy(GT[:, :], PS[0][:, 0:4 * KT]).then_inc(small_c, 1)
            s_no = 0
            for s in slots:
                here = steps.get(s, ())
                early = [st for st in here if st[0] == "probs_t"]
                for st in early + [("split",)] + [st for st in here if st not in early]:
                    what = st[0]
                    if what == "split":
                        for n in range(LEAD + 1) if s == 0 else range(s + LEAD, min(s + LEAD + 1, pieces)) if s > 0 else ():
                            split_low(n)
                    elif what == "square":
                        stage, i = st[1:]
                        c = TT * stage + i
                        dve.wait_ge(squared, c + 1)
                        mean(RSTD[:, c:c + 1], SS[:, c:c + 1], D_MODEL)
                    elif what == "scale":
                        i, = st[1:]
                        root()
                        nc.vector.tensor_scalar(H[:, i, :], H[:, i, :], RSTD[:, 2 + i:3 + i], None, ALU.mult).then_inc(normed, 1)
                    elif what == "transpose":
                        transposed_low(*st[1:], t_order[st[1:]])
                    elif what == "diagonal":
                        dve.wait_ge(rstd_ready, TT)
                        nc.vector.memset(ONESQ, 1.0)
                        for i in range(TT):
                            ins = nc.vector.tensor_scalar(DIAG[:, i * P:(i + 1) * P], IDENT[:, :], RSTD[:, i:i + 1], None,
                                                          ALU.mult)
                        ins.then_inc(diag_ready, 1)
                    elif what == "drain":
                        ch, = st[1:]
                        src, scale = acc_bank(ch, 1), None
                        if ch.kind == NARROW:
                            if ch.name == "n_gl":
                                dve.wait_ge(act_drained, ch.c + 1)
                                nc.vector.tensor_scalar(GTR[:, :], GTR[:, :], 1.0, None, ALU.add).then_inc(dve_drained, 1)
                                dve.wait_ge(dve_drained, dve_drains(ch.c))
                                nc.vector.reciprocal(GTR[:, :], GTR[:, :]).then_inc(gates_sig, 1)
                            else:
                                dve.wait_ge(squared, TT)
                                dve.wait_ge(tr_lo, t_done("mem0"))
                                nc.vector.memset(GLT[:, :], 1.0).then_inc(dve_drained, 1)
                            continue
                        dve.wait_ge(piece_used, ch.last + 1)
                        if ch.name.startswith("mem_k"):
                            kx = KX[int(ch.name[-1])]
                            row = ROW.unsqueeze(1).to_broadcast([P, 2, SEQ])
                            dve.wait_ge(tr_hi, t_done("row" + ch.name[-1]))
                            dve.wait_ge(tr_lo, t_done("row" + ch.name[-1]))
                            nc.vector.tensor_tensor(kx[:, 2:4, :], src[:, 0:512].rearrange("p (b t) -> p b t", b=2), row, ALU.mult)\
                                .then_inc(dve_drained, 1)
                            dve.wait_ge(act_drained, ch.c + 1)
                            step(nc.vector.tensor_tensor(kx[:, 0:2, :], kx[:, 0:2, :], row, ALU.mult))
                            continue
                        elif ch.name.startswith("mem_v"):
                            dst, scale = VX[int(ch.name[-1])][:, 1, :], RSTD[:, 1:2]
                            dve.wait_ge(rstd_ready, TT)
                        elif ch.name.startswith("g_qk"):
                            j = int(ch.name[-1])
                            dst = QK[:, 4 * j + 2:4 * j + 4, :].rearrange("p b t -> p (b t)")
                            scale = GLA_SCALE if 4 * j + 2 < FT else None
                        elif ch.name.startswith("g_v"):
                            j = int(ch.name[-1])
                            dst = V[:, 1, 512 * j:512 * (j + 1)]
                        elif ch.name in ("g_xq", "n_xq"):
                            if ch.name == "n_xq":
                                dve.wait_ge(sc_ready, X_HEADS)
                            dst = XQT[:, 2:4, :].rearrange("p b t -> p (b t)")
                        elif "out" in ch.name:
                            j = int(ch.name[-1])
                            l = int(ch.name[0] == "n")
                            dve.wait_ge(post_in[l], 16)
                            c0 = slice(512 * j, 512 * (j + 1))
                            dve.wait_ge(y_sq, 4 * l + j + 1)
                            if j == 0:
                                dve.wait_ge(tr_ready, t_done(f"y{l}"))
                            nc.vector.tensor_tensor(Y[:, 0, c0], acc_bank(ch, 0)[:, :], GPOST[l][:, c0], ALU.mult)
                            dve.wait_ge(act_drained, ch.c + 1)
                            nc.vector.tensor_tensor(Y[:, 1, c0], acc_bank(ch, 1)[:, :], GPOST[l][:, c0], ALU.mult)\
                                .then_inc(dve_drained, 1)
                            continue
                        elif ch.name == "n_cmp":
                            dst = KVC[:, 1].rearrange("p g t -> p (g t)")
                        elif ch.name in ("n_slc", "n_win"):
                            dst = NV[:, 0 if ch.name == "n_slc" else 1].rearrange("p i w -> p (i w)")
                        elif ch.name.startswith("n_q"):
                            j = int(ch.name[-1])
                            dst = NQT[:, 4 * j + 2:4 * j + 4, :].rearrange("p b t -> p (b t)")
                        if scale is None:
                            nc.vector.tensor_copy(dst, src[:, 0:512]).then_inc(dve_drained, 1)
                        else:
                            nc.vector.tensor_scalar(dst, src[:, 0:512], scale, None, ALU.mult).then_inc(dve_drained, 1)
                    elif what == "gated_drain":
                        ch, i = st[1:]
                        k = gated_no(ch)
                        c0 = BW if "xg" in ch.name else 512 * int(ch.name[-1])
                        if k in (0, 2, 3):
                            dve.wait_ge(o_norm, (c0 + 511) // GLA_DV + 1)
                        if k == 1:
                            dve.wait_ge(head_kept, X_HEADS)
                        if k == 4:
                            dve.wait_ge(head_kept, len(heads))
                        if i == 0:
                            dve.wait_ge(sg_exp, k + 1)
                        else:
                            dve.wait_ge(act_drained, ch.c + 1)
                        nc.vector.tensor_tensor(Y[:, i, c0:c0 + 512], Y[:, i, c0:c0 + 512], SG[:, i, :], ALU.mult)\
                            .then_inc(mixed_gated, 1)
                    elif what == "hidden":
                        g, = st[1:]
                        dve.wait_ge(hid_parts, g + 1)
                        a0, b0 = HB[:, g, :, 0:NB], HB[:, g, :, NB:2 * NB]
                        nc.vector.tensor_tensor(a0, a0, b0, ALU.add).then_inc(hid_sum, 1)
                        dve.wait_ge(hid_exp, g + 1)
                        v = HSG[:, g, :, 0:NB]
                        step(nc.vector.tensor_scalar(v, v, 1.0, None, ALU.add))
                        step(nc.vector.reciprocal(v, v))
                        nc.vector.tensor_tensor(HID[:, g, :, 0:NB], v, a0, ALU.mult).then_inc(hid_ready, 1)
                    elif what == "nsa_gates":
                        dve.wait_ge(gates_t, 1)
                        step(nc.vector.tensor_copy(GATES[:, :, 0:NSA_HEADS * N_BRANCH],
                                                   PS[5][:, 0:128].rearrange("p (i w) -> p i w", i=TT)[:, :, 0:NSA_HEADS * N_BRANCH]))
                    elif what == "gate":
                        i, = st[1:]
                        dve.wait_ge(z_exp, i + 1)
                        nc.vector.scalar_tensor_tensor(ZG[:, 0:512], PS[6][:, :], 0.0, ZL[:, 0:512], ALU.min, ALU.subtract)
                        step(nc.vector.scalar_tensor_tensor(ZG[:, 512:KEYW], PS[7][:, 0:KEYW - 512], 0.0, ZL[:, 512:KEYW],
                                                            ALU.min, ALU.subtract))
                        step(nc.vector.tensor_copy(LGH[:, i, :], ZG[:, :]))
                        nc.vector.tensor_tensor(LGL[:, i, :], ZG[:, :], LGH[:, i, :].bitcast(f32), ALU.subtract).then_inc(lg_ready, 1)
                    elif what == "qk_products":
                        dve.wait_ge(act_drained, C["g_qk2"].c + 1)
                        dve.wait_ge(dve_drained, dve_drains(C["g_qk2"].c))
                        nc.vector.tensor_tensor(QKP[:, :, :], QK[:, 0:FT, :], QK[:, FT:2 * FT, :], ALU.mult).then_inc(qkp_ready, 1)
                    elif what == "qk_sums":
                        dve.wait_ge(dq_ready, 1)
                        for par in range(2):
                            ins = nc.vector.tensor_copy(DQ.rearrange("p (g w i) -> p g w i", w=2, i=TT)[:, :, par, :],
                                                        PS[7 - par][:, 0:4].rearrange("p (g i) -> p g i", i=TT))
                        ins.then_inc(dq_kept, 1)
                    elif what == "decayed":
                        p, l = st[1:]
                        dve.wait_ge(e_ready, 12 * p + 6 * (l // 4 + 1))
                        hf = 1 << l

                        def halves(x, w):
                            return x.rearrange("p f t -> p (f t)").rearrange("p (b w o) -> p b w o", w=2, o=hf)[:, :, w, :]

                        e = E[:, l, :, :]
                        nc.vector.tensor_tensor(halves(e, 1), halves(e, 1), halves(QK[:, 3 * p:3 * p + 3, :], 1), ALU.mult)
                        nc.vector.tensor_tensor(halves(e, 0), halves(e, 0), halves(QK[:, FT + 3 * p:FT + 3 * p + 3, :], 0), ALU.mult)\
                            .then_inc(qk_ready, 1)
                    elif what == "gla_scores":
                        h, i = st[1:]
                        dve.wait_ge(s_ready, 2 * h + i + 1)
                        if h == 0 and i == 0:
                            dve.wait_ge(consts, 3)
                        if h >= 2:
                            dve.wait_ge(o_ready, h - 1)
                        for l in range(7):
                            hf = 1 << l
                            dst = AT[:, h % 2, i, :].rearrange("p (b w o) -> p b w o", w=2, o=hf)[:, :, 1, :]
                            src = PS[6 + i][:, 64 * l:64 * (l + 1)].rearrange("p (b o) -> p b o", o=hf)
                            msk = LMASK[:, l, :].rearrange("p (b o) -> p b o", o=hf)
                            step(nc.vector.copy_predicated(dst, msk, src))
                        nc.vector.tensor_copy(AT[:, h % 2, 2, 64 * i:64 * (i + 1)], PS[6 + i][:, 448:512]).then_inc(at_ready, 1)
                    elif what == "gla_out":
                        h, = st[1:]
                        dve.wait_ge(o_ready, h + 1)
                        v = slice(h * GLA_DV, (h + 1) * GLA_DV)
                        for i in range(TT):
                            ins = nc.vector.scalar_tensor_tensor(V[:, i, v], V[:, i, v], DQ[:, 2 * h + i:2 * h + i + 1],
                                                                 PS[4 + i][:, 0:GLA_DV], ALU.mult, ALU.add)
                        ins.then_inc(o_kept, 1)
                    elif what == "gla_root":
                        dve.wait_ge(o_sq, 2 * GLA_HEADS)
                        mean(RG, SSG, GLA_DV)
                    elif what == "gla_norm":
                        h, = st[1:]
                        if h == 0:
                            dve.wait_ge(gn_in, 16)
                            root()
                        v = slice(h * GLA_DV, (h + 1) * GLA_DV)
                        for i in range(TT):
                            ins = nc.vector.scalar_tensor_tensor(Y[:, i, v], V[:, i, v], RG[:, 2 * h + i:2 * h + i + 1],
                                                                 GN[:, :], ALU.mult, ALU.mult)
                        ins.then_inc(o_norm, 1)
                    elif what == "scores":
                        unit, at_i = st[1:]
                        kind, which, h = unit
                        dve.wait_ge(sc_ready, at_i + 1)
                        bank, b = PS[4 + s_no % 2], at_i % 2
                        m = MX[:, 2 * b:2 * b + 2]
                        if kind == "x":
                            step(nc.vector.tensor_reduce(m, bank[:, :].rearrange("p (i k) -> p i k", i=TT), AX.X, ALU.max))
                        else:
                            nc.vector.tensor_reduce(m[:, 0:1], bank[:, 0:P], AX.X, ALU.max)
                            step(nc.vector.tensor_reduce(m[:, 1:2], bank[:, P:P + SEQ], AX.X, ALU.max))
                        nc.vector.tensor_scalar(NM[:, 2 * b:2 * b + 2], m, -ATT_SCALE, None, ALU.mult).then_inc(mx_ready, 1)
                        s_no += 1
                    elif what == "probs_t":
                        unit, t, at_i = st[1:]
                        kind, which, h = unit
                        if kind == "cmp":
                            continue
                        b = at_i % 2
                        dve.wait_ge(pr_ready, at_i + 1)
                        ri = RI[:, 2 * b:2 * b + 2]
                        if kind == "x":
                            if at_i % X_HEADS >= 2:
                                dve.wait_ge(head_kept, head_no(unit) - 1)
                            nc.vector.reciprocal(ri, RS[:, 2 * b:2 * b + 2]).then_inc(pn_ready, 1)
                        else:
                            step(nc.vector.reciprocal(ri, RS[:, 2 * b:2 * b + 2]))
                            step(nc.vector.tensor_tensor(ri, ri, GATES[:, :, N_BRANCH * h + 1 + which], ALU.mult))
                            nc.vector.tensor_scalar(PN[:, b, 0:P], PN[:, b, 0:P], ri[:, 0:1], None, ALU.mult)
                            nc.vector.tensor_scalar(PN[:, b, P:P + SEQ], PN[:, b, P:P + SEQ], ri[:, 1:2], None, ALU.mult)\
                                .then_inc(pn_ready, 1)
                    elif what == "pe_t":
                        dve.wait_ge(small_t, 2)
                        nc.vector.tensor_copy(PET[:, :, :].rearrange("p g j -> p (g j)"), PS[4][:, 0:2 * CMP_LEN]).then_inc(small_c, 1)
                    elif what == "blocks":
                        g, = st[1:]
                        dve.wait_ge(act_drained, C["n_cmp"].c + 1)
                        dve.wait_ge(dve_drained, dve_drains(C["n_cmp"].c))
                        dve.wait_ge(small_c, 2)
                        if g:
                            dve.wait_ge(blk_ready, g)
                        for half in range(2):
                            for gr in range(NSA_GROUPS):
                                src = KVC[:, g, gr, half * 16:half * 16 + 16 * N_CMP].rearrange("p (n j) -> p j n", j=16)
                                pe_b = PET[:, g, half * 16:(half + 1) * 16].unsqueeze(2).to_broadcast([P, 16, N_CMP])
                                dst = BKT[:, half * 16:(half + 1) * 16, gr * N_CMP:(gr + 1) * N_CMP]
                                last = nc.vector.tensor_tensor(dst, src, pe_b, ALU.add)
                        step(last)
                        parts = BK[:, g, 0:2 * NB * CMP_LEN].rearrange("p (j w n) -> p j w n", w=2, n=NB)
                        nc.vector.memset(BK[:, g, 2 * NB * CMP_LEN:].bitcast(f32), 0.0)
                        step(nc.vector.tensor_copy(parts[:, :, 0, :], BKT[:, :, :]))
                        nc.vector.tensor_tensor(parts[:, :, 1, :], BKT[:, :, :], parts[:, :, 0, :].bitcast(f32), ALU.subtract)\
                            .then_inc(blk_ready, 1)
                    elif what == "cmp_kv":
                        g, = st[1:]
                        dve.wait_ge(kvc_ready, g + 1)
                        if g == 0:
                            nc.vector.tensor_copy(KC[:, 0:NB], PS[6][:, 0:NB]).then_inc(kvc_kept, 1)
                            nc.vector.memset(PC[:, :, :, :], 0.0)
                        else:
                            nc.vector.tensor_copy(VC[:, :, :].rearrange("p g d -> p (g d)"), PS[6][0:N_CMP, 0:SEQ]).then_inc(kvc_kept, 1)
                    elif what == "cmp_scores":
                        j, = st[1:]
                        dve.wait_ge(cs_ready, j + 1)
                        bank = PS[4 + s_no % 2][:, 0:128].rearrange("p (u n) -> p u n", n=16)[:, :, 0:N_CMP]
                        m, sm, fc = MC[:, 8 * j:8 * j + 8], SC[:, 8 * j:8 * j + 8], FC[:, 8 * j:8 * j + 8]
                        pc = PC[:, j, :, 0:N_CMP]
                        step(nc.vector.tensor_reduce(m, bank, AX.X, ALU.max))
                        nc.vector.tensor_tensor(pc, bank, m.unsqueeze(2).to_broadcast([P, 8, N_CMP]), ALU.subtract).then_inc(cs_shift, 1)
                        dve.wait_ge(cs_exp, j + 1)
                        step(nc.vector.tensor_reduce(sm, pc, AX.X, ALU.add))
                        step(nc.vector.reciprocal(fc, sm))
                        fv = fc.rearrange("p (h i) -> p h i", i=TT)
                        step(nc.vector.tensor_tensor(fv, fv, ROWOK[:, :].unsqueeze(1).to_broadcast([P, 4, TT]), ALU.mult))
                        gv = GATES[:, :, 12 * j:12 * j + 12].rearrange("p i (h b) -> p h i b", b=N_BRANCH)[:, :, :, 0]
                        step(nc.vector.tensor_tensor(fv, fv, gv, ALU.mult))
                        nc.vector.tensor_tensor(pc, pc, fc.unsqueeze(2).to_broadcast([P, 8, N_CMP]), ALU.mult).then_inc(cs_done, 1)
                        s_no += 1
                    elif what == "residual_root":
                        l, = st[1:]
                        dve.wait_ge(act_drained, C["g_out3" if l == 0 else "n_out3"].c + 1)
                        dve.wait_ge(dve_drained, dve_drains(C["g_out3" if l == 0 else "n_out3"].c))
                        c = 4 + 4 * l
                        step(nc.vector.tensor_reduce(SS[:, c:c + TT], YSS[l], AX.X, ALU.add))
                        mean(RSTD[:, c:c + TT], SS[:, c:c + TT], D_MODEL)
                    elif what == "residual":
                        l, k = st[1:]
                        i, q = divmod(k, 4)
                        if k == 0:
                            root()
                            if l == 0:
                                dve.wait_ge(res_in, 16 * TT)
                        c0 = slice(512 * q, 512 * (q + 1))
                        r = 4 + 4 * l + i
                        nc.vector.scalar_tensor_tensor(H[:, i, c0], Y[:, i, c0], RSTD[:, r:r + 1], H[:, i, c0], ALU.mult,
                                                       ALU.add).then_inc(res_ready, 1)
                    elif what == "stream_root":
                        dve.wait_ge(squared, 2 * TT + 4 * TT)
                        step(nc.vector.tensor_reduce(SS[:, 6:8], HSS, AX.X, ALU.add))
                        mean(RSTD[:, 6:8], SS[:, 6:8], D_MODEL)
                    elif what == "stream_scale":
                        q, = st[1:]
                        if q == 0:
                            root()
                        for i in range(TT):
                            c0 = slice(512 * q, 512 * (q + 1))
                            nc.vector.tensor_scalar(Y[:, i, c0], H[:, i, c0], RSTD[:, 6 + i:7 + i], None, ALU.mult)\
                                .then_inc(normed, 1)


_INS = ["x", "mem", "ln_pre", "ln_post", "ln_mem", "w_mem_kv", "gla_w_in", "gla_w_gate_lr", "gla_b_gate", "gla_norm",
        "gla_w_out", "nsa_w_in", "nsa_pe_k", "nsa_pe_v", "nsa_wk1", "nsa_wk2", "nsa_wv1", "nsa_wv2", "nsa_w_out"]


def kernel(**inputs):
    import numpy as _np
    import concourse.bacc as _bacc
    from concourse import mybir as _mybir
    from concourse.bass_utils import run_bass_kernel_spmd as _run

    nc = _bacc.Bacc("TRN2", target_bir_lowering=False, num_devices=1)
    arrays, args = {}, {}
    for name in _INS:
        v = _np.ascontiguousarray(inputs[name])
        arrays[f"in_{name}_dram"] = v
        args[name] = nc.dram_tensor(f"in_{name}_dram", v.shape, _mybir.dt.from_np(v.dtype), kind="ExternalInput").ap()
    out = nc.dram_tensor("out_0_dram", (1, SEQ, D_MODEL), _mybir.dt.float32, kind="ExternalOutput").ap()
    hybrid_trunk(nc, args, out)
    r = _run(nc, [arrays], core_ids=[0])
    return r.results[0]["out_0_dram"]
```

```python
import concourse.bass as bass
from concourse import mybir
from contextlib import ExitStack

P = 128
D_MODEL, SEQ, N_MEM = 2048, 256, 256
KT = D_MODEL // P
TT = SEQ // P
HD = 128
X_HEADS = 4
XW = X_HEADS * HD
BW = D_MODEL - XW
GLA_HEADS, GLA_DV = 4, BW // 4
GLA_DK = GLA_DV // 2
KEYW = GLA_HEADS * GLA_DK
FT = KEYW // P
RANK = 16
GATE_TEMP = 16.0
NSA_HEADS, NSA_GROUPS = BW // HD, 2
HPG = NSA_HEADS // NSA_GROUPS
KVW = NSA_GROUPS * HD
N_BRANCH = 3
CMP_LEN, CMP_STRIDE, CMP_HIDDEN = 32, 16, 256
N_CMP = (SEQ - CMP_LEN) // CMP_STRIDE + 1
NB = NSA_GROUPS * N_CMP
EPS = 1e-6
LEVELS = 8
MASKED = -1e30
ATT_SCALE = float(HD) ** -0.5
GLA_SCALE = float(GLA_DK) ** -0.5

RING = 4
PIECE = 1024
LEAD = RING - 1

TM, FM, MIX, NARROW, CMP = "token-major", "feature-major", "both", "narrow", "compress"


class Chunk:

    def __init__(self, name, kind, w, col, width, lhs):
        self.name, self.kind, self.w, self.col, self.width, self.lhs = name, kind, w, col, width, lhs
        self.tiles = {NARROW: KT if width <= 24 else KT // 2, CMP: PIECE // CMP_HIDDEN}.get(kind, PIECE // 512)
        self.n = {CMP: CMP_LEN}.get(kind, KT) // self.tiles
        self.order = list(range(BW // P, KT)) + list(range(BW // P)) if "out" in name else list(range(CMP_LEN if kind == CMP else KT))


def chunk_list():
    g, n = "gla_w_in", "nsa_w_in"
    gq, gv, gl = 0, 2 * KEYW, 2 * KEYW + BW
    gr = gl + RANK
    nk = BW
    ng = BW + 6 * KVW
    nr = ng + NSA_HEADS * N_BRANCH
    out = []
    def memory(i, act):
        return [Chunk(f"mem_v{i}", TM, f"kv{i}", XW, XW, act), Chunk(f"mem_k{i}", FM, f"kv{i}", 0, XW, act)]

    out += memory(0, "A")
    out.append(Chunk("g_qk0", FM, g, gq, 512, "B"))
    out.append(Chunk("g_lr", NARROW, g, gl, RANK, "B"))
    out += [Chunk(f"g_qk{j}", FM, g, gq + 512 * j, 512, "B") for j in (1, 2)]
    out += [Chunk(f"g_v{j}", TM, g, gv + 512 * j, 512, "B") for j in range(3)]
    out.append(Chunk("g_xq", FM, g, gr + BW, XW, "B"))
    out.append(Chunk("g_r0", TM, g, gr, 512, "B"))
    out.append(Chunk("g_xg", FM, g, gr + BW + XW, XW, "B"))
    out += [Chunk(f"g_r{j}", TM, g, gr + 512 * j, 512, "B") for j in (1, 2)]
    out += [Chunk(f"g_out{j}", TM, "gla_w_out", 512 * j, 512, "A") for j in range(4)]
    out += memory(1, "B")
    out.append(Chunk("n_cmp", FM, n, nk, 2 * KVW, "A"))
    out.append(Chunk("n_gl", NARROW, n, ng, NSA_HEADS * N_BRANCH, "A"))
    out.append(Chunk("n_wk1", CMP, "nsa_wk1", 0, CMP_HIDDEN, "K"))
    out.append(Chunk("n_wv1", CMP, "nsa_wv1", 0, CMP_HIDDEN, "V"))
    out.append(Chunk("n_slc", MIX, n, nk + 2 * KVW, 2 * KVW, "A"))
    out.append(Chunk("n_win", MIX, n, nk + 4 * KVW, 2 * KVW, "A"))
    out += [Chunk(f"n_q{j}", FM, n, 512 * j, 512, "A") for j in range(3)]
    out.append(Chunk("n_xq", FM, n, nr + BW, XW, "A"))
    out.append(Chunk("n_xg", FM, n, nr + BW + XW, XW, "A"))
    out += [Chunk(f"n_r{j}", FM, n, nr + 512 * j, 512, "A") for j in range(3)]
    out += [Chunk(f"n_out{j}", TM, "nsa_w_out", 512 * j, 512, "B") for j in range(4)]
    stream, between = [], []
    for ch in out:
        if ch.kind == CMP:
            between += [(ch, j) for j in range(ch.n)]
        elif ch.name in ("n_slc", "n_win", "n_q0"):
            skip = 4 if ch.name == "n_slc" else 0
            for j in range(ch.n):
                stream.append((ch, j))
                if j >= skip and between:
                    stream.append(between.pop(0))
        else:
            stream += [(ch, j) for j in range(ch.n)]
    assert not between
    for n, (ch, j) in enumerate(stream):
        if j == 0:
            ch.first = n
        ch.last = n
    out.sort(key=lambda ch: ch.last)
    pair = 0
    for c, ch in enumerate(out):
        ch.c = c
        if ch.kind != CMP:
            ch.pair = pair
            ch.before = next((b for b in out[:c] if b.kind != CMP and b.pair == pair - 2), None)
            pair += 1
    return out, stream


def hybrid_trunk(nc, a, out):
    f32, f32r, bf16, i32 = mybir.dt.float32, mybir.dt.float32r, mybir.dt.bfloat16, mybir.dt.int32
    ALU, ACT, AX = mybir.AluOpType, mybir.ActivationFunctionType, mybir.AxisListType

    chunks, piece_of = chunk_list()
    pieces = len(piece_of)
    C = {ch.name: ch for ch in chunks}
    weights = {"kv0": a["w_mem_kv"][0], "kv1": a["w_mem_kv"][1], "gla_w_in": a["gla_w_in"][0],
               "gla_w_out": a["gla_w_out"][0], "nsa_w_in": a["nsa_w_in"][0], "nsa_w_out": a["nsa_w_out"][0],
               "nsa_wk1": a["nsa_wk1"][0], "nsa_wv1": a["nsa_wv1"][0]}

    base = (nc.sbuf_base + 31) // 32 * 32
    top = [0]

    def at(name, shape, dt, off):
        return nc.alloc_sbuf_tensor_at(name, [shape[0], *shape[1:]], dt, offset=base + off)

    def region(size):
        off = top[0]
        top[0] += (size + 31) // 32 * 32
        assert base + top[0] <= nc.sbuf_usable_end, top[0]
        return off

    def new(name, shape, dt):
        n = 4 if dt != bf16 else 2
        for s in shape[1:]:
            n *= s
        return at(name, shape, dt, region(n))

    RAW = new("weights_raw", [P, RING, PIECE], f32)
    WHI = new("weights_high", [P, RING, PIECE], f32r)
    WLO = new("weights_low", [P, RING, PIECE], f32r)
    a_off = region(2 * KT * SEQ * 4)
    AHI = at("act_a_high", [P, KT, SEQ], f32r, a_off)
    ALO = at("act_a_low", [P, KT, SEQ], f32r, a_off + KT * SEQ * 4)
    b_off = region(2 * KT * SEQ * 4)
    BHI = at("act_b_high", [P, KT, SEQ], f32r, b_off)
    BLO = at("act_b_low", [P, KT, SEQ], f32r, b_off + KT * SEQ * 4)
    h_off = region(TT * D_MODEL * 4)
    H = at("stream", [P, TT, D_MODEL], f32, h_off)
    m_off = region(2 * TT * BW * 4)
    y_off = region(TT * D_MODEL * 4)
    Y = at("mixed", [P, TT, D_MODEL], f32, y_off)
    XQT = new("xattn_q", [P, X_HEADS, SEQ], f32)
    KX = [new(f"xattn_k{i}", [P, X_HEADS, N_MEM], f32) for i in range(2)]
    VX = [new(f"xattn_v{i}", [P, TT, XW], f32) for i in range(2)]
    SG = new("gate_silu", [P, TT, 512], f32)
    IDENT = new("identity", [P, P], f32)
    GT = new("gains_transposed", [P, 4 * KT], f32)
    gla_off = region(12 * P * 4 + 7 * 64 * 4 + 2 * 3 * P * 4 + GLA_DV * 4)
    ST = new("stats", [P, 192], f32)

    ROW = SG[:, 0, 0:SEQ]
    DIAG = SG[:, 1, 0:SEQ]
    ONESQ = SG[:, 1, SEQ:SEQ + P]
    MQ = [at(f"mem_again{q}", [P, TT, 512], f32, m_off + o) for q, o in enumerate((12288, 16384, 20480, 0))]

    LGH = at("log_gate_high", [P, TT, KEYW], f32r, h_off)
    LGL = at("log_gate_low", [P, TT, KEYW], f32r, h_off + TT * KEYW * 4)
    PX = at("xattn_probs", [P, 2, 512], f32, h_off + 2 * TT * KEYW * 4)
    QK = at("gla_qk", [P, 2 * FT, SEQ], f32, m_off)
    V = at("gla_v", [P, TT, BW], f32, m_off + 2 * FT * SEQ * 4)
    E = at("gla_decayed", [P, LEVELS, 3, SEQ], f32, a_off)
    QKP = at("gla_qk_product", [P, FT, SEQ], f32, a_off + LEVELS * 3 * SEQ * 4)
    WG = at("gate_weights", [2 * RANK + 1, KEYW], f32, y_off)
    GLT = at("gate_rank_t", [2 * RANK + 1, SEQ], f32, y_off + KEYW * 4)
    ZA = at("gate_abs", [P, KEYW], f32, y_off + KEYW * 4 + 1536)
    ZL = at("gate_log", [P, KEYW], f32, y_off + 2 * KEYW * 4 + 1536)
    ZG = at("gate_sum", [P, KEYW], f32, y_off + 3 * KEYW * 4 + 1536)
    PATTERN = at("decay_patterns", [P, 12, P], f32r, gla_off)
    LMASK = at("level_masks", [P, 7, 64], i32, gla_off + 12 * P * 4)
    AT = at("gla_attn_t", [P, 2, 3, P], f32, gla_off + 12 * P * 4 + 7 * 64 * 4)
    GN = at("gla_norm_rows", [P, GLA_DV], f32, gla_off + 12 * P * 4 + 7 * 64 * 4 + 2 * 3 * P * 4)
    PT0 = at("xattn_probs_t", [P, 2, 512], f32, m_off)
    PAT0 = at("pattern_scratch", [P, 9, P], f32, a_off)
    MSK0 = at("mask_scratch", [P, 7, 64], f32, a_off + 9 * P * 4)

    NQT = at("nsa_q", [P, NSA_HEADS, SEQ], f32, m_off)
    NKT = at("nsa_k", [P, 2, NSA_GROUPS, SEQ], f32, m_off + NSA_HEADS * SEQ * 4)
    NV = at("nsa_v", [P, 2, TT, KVW], f32, m_off + NSA_HEADS * SEQ * 4 + 4096)
    KVC = at("nsa_cmp_kv", [P, 2, NSA_GROUPS, SEQ], f32, m_off + NSA_HEADS * SEQ * 4 + 8192)
    BK = at("cmp_blocks_split", [P, 2, CMP_LEN * 2 * NB + P], f32r, b_off)
    BKT = at("cmp_blocks", [P, CMP_LEN, NB], f32, b_off + 16384)
    W2 = at("cmp_w2", [P, 2, 2, HD], f32, b_off + 20224)
    HT = at("cmp_hidden_rows", [2 * NB, 2, CMP_HIDDEN], f32, b_off + 22272)
    HB = at("cmp_hidden_parts", [P, 2, 2, 64], f32, b_off + 24320)
    HID = at("cmp_hidden", [P, 2, 2, 32], f32, b_off + 25344)
    HSG = at("cmp_hidden_sigmoid", [P, 2, 2, 32], f32, b_off + 25856)
    KC = at("cmp_k", [P, 32], f32, b_off + 26368)
    VC = at("cmp_v", [N_CMP, NSA_GROUPS, HD], f32, b_off + 26496)
    PC = at("cmp_probs", [P, 3, 8, 16], f32, b_off + 27520)
    PTC = at("cmp_probs_t", [16, 2, 256], f32, b_off + 29056)
    GATES = at("nsa_gates", [P, TT, 64], f32, b_off + 31104)
    NG = NSA_HEADS * N_BRANCH
    PE0 = at("cmp_pe", [CMP_LEN, 2, HD], f32, b_off + 31616)
    PET = at("cmp_pe_t", [P, 2, CMP_LEN], f32, y_off)
    GTR = at("nsa_gates_t", [2 * NSA_HEADS * N_BRANCH, SEQ], f32, y_off + 1024)
    CB = at("causal_bias", [P, P], bf16, gla_off)
    IDB = at("identity_bf16", [P, P], bf16, gla_off + 256)
    CMB = at("cmp_bias", [P, TT, 16], bf16, gla_off + 512)
    ROWOK = at("cmp_row_visible", [P, TT], f32, gla_off + 576)
    PN = at("nsa_probs", [P, 2, 512], f32, gla_off + 608)
    PT1 = at("nsa_probs_t", [P, 2, 512], f32, gla_off + 608 + 4096)
    GPOST = [at(f"post_gain{i}", [P, D_MODEL], f32, m_off + 4096) for i in range(2)]
    YSS = [ST[:, 168 + 8 * l:176 + 8 * l].rearrange("p (i j) -> p i j", i=TT) for l in range(2)]
    HSS = ST[:, 184:192].rearrange("p (i j) -> p i j", i=TT)
    G0 = at("gains_raw", [4 * KT, P], f32, m_off)
    SQUARES = at("squares", [P, D_MODEL], f32, m_off + 12288 + 2048)

    SS = ST[:, 0:16]
    RSTD = ST[:, 16:32]
    NM = ST[:, 32:36]
    RS = ST[:, 36:40]
    RI = ST[:, 40:44]
    MX = ST[:, 44:48]
    SSG = ST[:, 48:56]
    RG = ST[:, 56:64]
    DQ = ST[:, 64:72]
    MC = ST[:, 72:96]
    SC = ST[:, 96:120]
    FC = ST[:, 120:144]
    ONES = ST[:, 144:145]
    HALF = ST[:, 160:168]

    ctx = ExitStack()
    with ctx:
        PS = [ctx.enter_context(nc.psum_tensor(f"bank{i}", [P, 512], f32)) for i in range(8)]

        def sem(name):
            return ctx.enter_context(nc.semaphore(name))

        raw_in = [sem(f"raw_piece_in{i}") for i in range(RING)]
        hi_ready, lo_ready, piece_used = sem("high_ready"), sem("low_ready"), sem("piece_used")
        act_drained, dve_drained = sem("drained_by_scalar"), sem("drained_by_vector")
        mem_in = [sem(f"mem_in{q}") for q in range(4)]
        mem_again = [sem(f"mem_again_in{q}") for q in range(4)]
        diag_ready = sem("diagonal_ready")
        x_in = [sem(f"x_in{i}") for i in range(2)]
        gains_in, wg_in, gn_in, res_in = sem("gains_in"), sem("gate_weights_in"), sem("gla_norm_in"), sem("residual_in")
        w2_in, pe_in = sem("cmp_w2_in"), sem("cmp_pe_in")
        post_in = [sem(f"post_gain_in{i}") for i in range(2)]
        stored = sem("stored")
        consts, consts2 = sem("constants_ready"), sem("nsa_constants_ready")
        pool_step, dve_step, act_step = sem("pool_step"), sem("vector_step"), sem("scalar_step")
        squared, normed = sem("squared"), sem("normed")
        mean_ready, rstd_ready = sem("mean_square"), sem("reciprocal_root")
        small_t, small_c = sem("small_transposed"), sem("small_copied")
        tr_ready, tr_hi, tr_lo = sem("transposed"), sem("transposed_high"), sem("transposed_low")
        z_ready, za_exp, z_exp, lg_ready = sem("gate_logits"), sem("gate_exp"), sem("gate_ln"), sem("log_gates")
        d_ready, e_ready, qk_ready = sem("decay_logs"), sem("decays"), sem("decayed")
        qkp_ready, dq_ready, dq_kept = sem("qk_products"), sem("qk_sums"), sem("qk_sums_kept")
        s_ready, at_ready = sem("gla_scores"), sem("gla_attn")
        o_ready, o_kept, o_sq, o_norm = sem("gla_out"), sem("gla_out_kept"), sem("gla_out_squared"), sem("gla_out_normed")
        sc_ready, mx_ready, pr_ready, pn_ready = sem("scores"), sem("maxima"), sem("probs"), sem("probs_scaled")
        pt_ready, pt_kept, pv_ready, head_kept = sem("probs_t"), sem("probs_t_kept"), sem("pv_done"), sem("head_kept")
        cs_ready, cs_shift, cs_exp, cs_done = sem("cmp_scores"), sem("cmp_shifted"), sem("cmp_exps"), sem("cmp_probs_done")
        blk_ready, hid_exp, hid_ready = sem("cmp_blocks_ready"), sem("hidden_exps"), sem("hidden_ready")
        kvc_ready, kvc_kept = sem("cmp_kv_ready"), sem("cmp_kv_kept")
        mixed_gated = sem("mixed_gated")
        sg_exp = sem("sigmoid_exps")
        tile0_done = sem("last_chunk_tile0_done")
        y_hi, y_lo = sem("gated_high"), sem("gated_low")
        y_sq, res_ready = sem("projected_squared"), sem("residual_ready")
        hid_t, hid_parts, hid_sum = sem("hidden_transposed"), sem("hidden_parts"), sem("hidden_sums")
        gates_sum, gates_sig, gates_t = sem("gates_summed"), sem("gates_sigmoid"), sem("gates_transposed")

        steps = {}

        def put(slot, *step):
            steps.setdefault(slot, []).append(step)

        for ch in chunks:
            if ch.name[2:4] in ("r0", "r1", "r2", "xg"):
                late = 4 if ch.name == "g_r0" else 0
                put(ch.last + late, "gated_drain", ch, 0)
                put(ch.last + late + 1, "gated_drain", ch, 1)
                if ch.kind == FM:
                    put(ch.last + 1, "gated_split", ch, 0)
                    put(ch.last + 2, "gated_split", ch, 1)
            elif ch.kind == CMP:
                put(ch.last, "hidden_drain", ch)
            else:
                put(ch.last, "drain", ch)
        for kt in range(4):
            put(-1, "transpose", "mem0", kt)
            if kt == 1:
                put(-1, "first_split")
        for kt in range(4, KT):
            put((kt - 4) // 2, "transpose", "mem0", kt)
        put(2, "square", 0, 0)
        put(3, "square", 0, 1)
        put(4, "diagonal", 0)
        put(6, "transpose", "row0", 0)
        for i in range(TT):
            put(6 + i, "square", 1, i)
            put(8 + i, "scale", i)
        for kt in range(KT):
            put(11 + kt // 2, "transpose", "x0", kt)
        q0 = C["g_lr"].last
        put(q0 + 1, "gate", 0)
        put(q0 + 2, "gate_ln", 0)
        put(q0 + 5, "gate_ln", 1)
        put(q0 + 4, "gate", 1)
        for d in range(12):
            put(q0 + 8 + d, "decay", 0, d)
        k0 = C["g_qk2"].last
        put(k0, "qk_products")
        put(k0 + 2, "qk_sums")
        for l in range(LEVELS):
            put(k0 + 1 + l, "decayed", 0, l)
        s0 = k0 + LEVELS + 1
        for h in (0, 1):
            put(s0 + 2 * h, "gla_scores", h, 0)
            put(s0 + 2 * h + 1, "gla_scores", h, 1)
            o0 = max(s0 + 2 * h + 2, C[f"g_v{(384 * h + 383) // 512}"].last + 1)
            put(o0, "gla_out", h)
        s1 = max(s0 + 4, o0 + 1)
        for d in range(12):
            put(s1 + d, "decay", 1, d)
        for l in range(LEVELS):
            put(s1 + 6 + l + (1 if l >= 4 else 0), "decayed", 1, l)
        s2 = s1 + 15
        for h in (2, 3):
            put(s2 + 2 * (h - 2), "gla_scores", h, 0)
            put(s2 + 2 * (h - 2) + 1, "gla_scores", h, 1)
            o0 = max(s2 + 2 * (h - 2) + 2, C[f"g_v{(384 * h + 383) // 512}"].last + 1)
            put(o0, "gla_out", h)
        put(o0 + 1, "gla_root")
        for h in range(GLA_HEADS):
            put(o0 + 2 + h, "gla_norm", h)
        ax = o0 + 2
        t_unit = 0
        s_uses = []
        attn_units = []
        for h in range(X_HEADS):
            put(ax + h, "scores", ("x", 0, h), len(attn_units))
            s_uses.append(("attn", len(attn_units)))
            put(ax + h + 2, "probs_t", ("x", 0, h), t_unit, len(attn_units))
            put(ax + h + 3, "pv", ("x", 0, h), t_unit, len(attn_units))
            attn_units.append(t_unit)
            t_unit += 1
        for k in range(4):
            put(C["g_r1"].first + 5 + k // 2, "transpose", "y0", k)
            put(C["g_r2"].first + 4 + k // 2, "transpose", "y0", 4 + k)
            put(C["g_out0"].first + 2 + k // 2, "transpose", "y0", 8 + k)
        for kt in range(KT):
            put(C["g_out0"].first + 6 + kt // 2, "transpose", "mem1", kt)
        m0 = C["mem_v1"].first
        for k in range(4 * TT):
            put(m0 + 1 + k // 2, "residual", 0, k)
            put(m0 + 2 + k // 2, "stream_square", k)
        put(m0 + 5, "stream_root")
        for q in range(4):
            put(m0 + 6 + q // 2, "stream_scale", q)
        for kt in range(KT):
            put(m0 + 7 + kt // 2, "transpose", "x1", kt)
        put(C["mem_k1"].last - 3, "diagonal", 1)
        put(C["mem_k1"].last - 2, "transpose", "row1", 0)
        put(C["n_gl"].last + 2, "nsa_gates")
        put(C["n_gl"].last, "pe_t")
        put(C["n_gl"].last + 3, "blocks", 0)
        put(C["n_gl"].last + 6, "blocks", 1)
        for g, name in enumerate(("n_wk1", "n_wv1")):
            put(C[name].last + 1, "hidden", g)
            put(C[name].last + 4, "cmp_kv", g)
        for j in range(3):
            u0 = C[f"n_q{j}"].last + 1
            put(u0, "cmp_scores", j)
            s_uses.append(("cmp", j))
            u = u0
            for h in range(4 * j, 4 * j + 4):
                for br in (0, 1, 2):
                    unit = ("cmp", 1, h) if br == 0 else ("nsa", br - 1, h)
                    at_i = len(attn_units)
                    if br:
                        put(u, "scores", unit, at_i)
                        s_uses.append(("attn", at_i))
                        attn_units.append(t_unit)
                        put(u + 2, "probs_t", unit, t_unit, at_i)
                        put(u + 3, "pv", unit, t_unit, at_i)
                        u += 1
                    else:
                        put(u + 2, "probs_t", unit, t_unit, None)
                        put(u + 3, "pv", unit, t_unit, None)
                    t_unit += 1
        ux = max(u + 1, C["n_xq"].last + 1)
        for h in range(X_HEADS):
            at_i = len(attn_units)
            put(ux + h, "scores", ("x", 1, h), at_i)
            s_uses.append(("attn", at_i))
            attn_units.append(t_unit)
            put(ux + h + 2, "probs_t", ("x", 1, h), t_unit, at_i)
            put(ux + h + 3, "pv", ("x", 1, h), t_unit, at_i)
            t_unit += 1
        for k in range(4 * TT):
            put(C["n_out3"].last, "residual", 1, k)

        def last_slot(kind, test):
            return max(s for s, l in steps.items() for st in l if st[0] == kind and test(st))

        ready0 = last_slot("pv", lambda st: st[1][0] == "x" and st[1][1] == 0)
        ready1 = last_slot("pv", lambda st: st[1][1] == 1 and st[1][0] == "x")
        assert ready0 <= C["g_xg"].last and ready1 <= C["n_xg"].last, (ready0, C["g_xg"].last, ready1, C["n_xg"].last)

        def rank(st):
            if st[0] == "probs_t":
                return 1 if st[1][0] == "cmp" else 4
            return {"drain": 0, "scores": 2, "cmp_scores": 2, "pv": 3, "gated_drain": 6, "gated_split": 7}.get(st[0], 5)

        for s in steps:
            steps[s].sort(key=rank)
        slots = list(range(-1, pieces))
        seq = [st for s in slots for st in steps.get(s, ())]
        assert [st[1].c for st in seq if "drain" in st[0] and st[2:] != (0,)] == list(range(len(chunks)))
        t_order = {}
        for st in seq:
            if st[0] == "transpose":
                t_order[st[1:]] = len(t_order)
        units = [st for st in seq if st[0] == "probs_t"]
        assert [u[2] for u in units] == list(range(t_unit))
        heads = []
        for u in units:
            key = (u[1][0] == "x", u[1][1] if u[1][0] == "x" else 1, u[1][2])
            if key not in heads:
                heads.append(key)

        def head_no(unit):
            return heads.index((unit[0] == "x", unit[1] if unit[0] == "x" else 1, unit[2]))

        def t_source(stage):
            return {"mem0": Y, "x0": H, "y0": Y, "x1": Y}[stage]

        def t_done(stage):
            return max(n for (st, kt), n in t_order.items() if st == stage) + 1

        def t_dest(stage):
            return {"mem0": (AHI, ALO, 2 * KT), "mem1": (BHI, BLO, 3 * KT), "x0": (BHI, BLO, 0), "y0": (AHI, ALO, None),
                    "x1": (AHI, ALO, KT)}[stage]

        def lhs_ready(ch, j):
            if "out" in ch.name:
                return t_order["y0", ch.order[2 * j + 1]] + 1 if ch.name[0] == "g" and ch.order[2 * j] < 12 else 0
            stage = {"mem_k0": "mem0", "mem_v0": "mem0", "mem_k1": "mem1", "mem_v1": "mem1"}.get(
                ch.name, "x" + ("0" if ch.name[0] == "g" else "1"))
            return max(t_order[stage, kt] for kt in ch.order[:(j + 1) * ch.tiles]) + 1

        def lhs_free(stage):
            return {"mem0": None, "mem1": "g_r2", "x0": None, "y0": "mem_k0", "x1": "g_out3"}.get(stage)

        def piece_view(buf, n):
            ch, j = piece_of[n]
            return buf[:, n % RING, 0:ch.tiles * ch.width].rearrange("p (t w) -> p t w", t=ch.tiles)

        def narrow_parts(n, part):
            ch = piece_of[n][0]
            return WHI[:, n % RING, 0:2 * ch.tiles * ch.width].rearrange("p (t q w) -> p t q w", q=2, w=ch.width)[:, :, part, :]

        def splits_before(s):
            return [[1], [3], [5]][s] if 0 <= s <= 2 else [s + LEAD] if 2 < s < pieces - LEAD else []

        def splits_after(s):
            return [[2], [4]][s] if 0 <= s <= 1 else []

        def acc_bank(ch, i):
            if ch.kind == CMP:
                return PS[7 if ch.lhs == "K" else 5]
            return PS[2 * (ch.pair % 2) + i]

        def unit_probs(unit):
            return (PX, PT0) if unit[:2] == ("x", 0) else (PN, PT1)

        def decay_unit(p, d):
            g, rest = divmod(d, 6)
            ft, i = divmod(rest, 2)
            return g, ft, i

        def head_rows(h):
            t0 = 3 * (h // 2)
            return [(t0, 0, P), (t0 + 1, 0, 64)] if h % 2 == 0 else [(t0 + 2, 0, P), (t0 + 1, 64, P)]

        gated_names = ["g_r0", "g_xg", "g_r1", "g_r2", "n_xg", "n_r0", "n_r1", "n_r2"]

        def gated_no(ch):
            return gated_names.index(ch.name)

        def dve_drains(c):
            return sum(ch.kind != CMP and ch.name not in ("n_gl", *gated_names) for ch in chunks[:c + 1])

        def gated_pair(ch, i):
            return (BW // P if "xg" in ch.name else 4 * int(ch.name[-1])) // 2 + i

        def mixed_pair(layer, pair):
            if layer == 0:
                return Y[:, pair - BW // (2 * P), BW:D_MODEL]
            return Y[:, :, :].rearrange("p i w -> p (i w)")[:, 512 * pair:512 * (pair + 1)]

        def mixed_head(layer, tile):
            return mixed_pair(layer, tile // 2)[:, tile % 2 * SEQ:(tile % 2 + 1) * SEQ]

        y_order = [(0, 6), (0, 7), (1, 6), (1, 7)] + [(1, p_) for p_ in range(6)]
        assert [(int(st[1].name[0] == "n"), gated_pair(*st[1:])) for st in seq if st[0] == "gated_split"] == y_order

        block = ctx.enter_context(nc.Block())

        @block.sync
        def _(sp):
            def piece_in(n):
                ch, j = piece_of[n]
                if n >= RING:
                    sp.wait_ge(lo_ready, n - RING + 1)
                k0 = ch.order[j * ch.tiles]
                rows = weights[ch.w][k0 * P:(k0 + ch.tiles) * P, ch.col:ch.col + ch.width]
                sp.dma_start(piece_view(RAW, n), rows.rearrange("(t p) w -> p t w", p=P)).then_inc(raw_in[n % RING], 16)

            def mem_quarter(q, dst):
                return sp.dma_start(dst, a["mem"][0, :, 512 * q:512 * (q + 1)].rearrange("(i p) w -> p i w", p=P))

            for q in range(4):
                mem_quarter(q, Y[:, :, 512 * q:512 * (q + 1)]).then_inc(mem_in[q], 16)
                if q == 0:
                    for g, name in enumerate(("ln_pre", "ln_mem")):
                        sp.dma_start(G0[2 * KT * g:2 * KT * (g + 1), :],
                                     a[name].rearrange("l (t p) -> (l t) p", p=P)).then_inc(gains_in, 16)
                piece_in(q)
            for s in range(1, pieces):
                if s + LEAD < pieces:
                    piece_in(s + LEAD)
                if 2 <= s < 2 + 2 * TT:
                    i, half = divmod(s - 2, 2)
                    cols = slice(half * D_MODEL // 2, (half + 1) * D_MODEL // 2)
                    sp.dma_start(H[:, i, cols], a["x"][0, i * P:(i + 1) * P, cols]).then_inc(x_in[i], 16)
                if s == 6:
                    sp.dma_start(GN[:, :], a["gla_norm"][0:1, :].to_broadcast([P, GLA_DV])).then_inc(gn_in, 16)
                if s == C["mem_k0"].first + RING:
                    sp.wait_ge(tr_lo, t_done("mem0"))
                    sp.wait_ge(squared, TT)
                    for k in range(2):
                        sp.dma_start(WG[k * RANK:(k + 1) * RANK, :], a["gla_w_gate_lr"][0]).then_inc(wg_in, 16)
                    sp.dma_start(WG[2 * RANK:2 * RANK + 1, :], a["gla_b_gate"][0:1, :]).then_inc(wg_in, 16)
                if s == C["g_r2"].first:
                    sp.wait_ge(pt_ready, X_HEADS)
                    sp.wait_ge(qk_ready, 2 * LEVELS)
                    for i in range(TT):
                        sp.dma_start(H[:, i, :], a["x"][0, i * P:(i + 1) * P, :]).then_inc(res_in, 16)
                    sp.dma_start(GPOST[0][:, :], a["ln_post"][0:1, :].to_broadcast([P, D_MODEL])).then_inc(post_in[0], 16)
                if s == C["g_out0"].first:
                    sp.wait_ge(o_norm, GLA_HEADS)
                    sp.wait_ge(pv_ready, X_HEADS)
                    for q in range(4):
                        mem_quarter(q, MQ[q][:, :, :]).then_inc(mem_again[q], 16)
                if s == C["n_cmp"].first + RING - 1:
                    sp.wait_ge(piece_used, C["mem_k1"].last + 1)
                    for g, w in enumerate(("nsa_wk2", "nsa_wv2")):
                        sp.dma_start(W2[:, g], a[w][0].rearrange("(t p) d -> p t d", p=P)).then_inc(w2_in, 16)
                    for g, w in enumerate(("nsa_pe_k", "nsa_pe_v")):
                        sp.dma_start(PE0[:, g, :], a[w][0]).then_inc(pe_in, 16)
                if s == C["n_r1"].first:
                    sp.wait_ge(sc_ready, len(attn_units))
                    sp.wait_ge(cs_ready, 3)
                    sp.dma_start(GPOST[1][:, :], a["ln_post"][1:2, :].to_broadcast([P, D_MODEL])).then_inc(post_in[1], 16)
            for k in range(4 * TT):
                i, q = divmod(k, 4)
                sp.wait_ge(res_ready, 4 * TT + k + 1)
                sp.dma_start(out[0, i * P:(i + 1) * P, 512 * q:512 * (q + 1)], H[:, i, 512 * q:512 * (q + 1)])\
                    .then_inc(stored, 16)
            sp.wait_ge(stored, 16 * 4 * TT)

        @block.gpsimd
        def _(pool):
            count = [0]

            def step(ins):
                count[0] += 1
                ins.then_inc(pool_step, 1)
                pool.wait_ge(pool_step, count[0])

            def keep_where(view, pattern, base_, mult, fill):
                step(nc.gpsimd.affine_select(out=view, in_=view, compare_op=ALU.is_ge, fill=fill, base=base_,
                                             pattern=pattern, channel_multiplier=mult))

            powers = [0]

            def rstd(v):
                pool.wait_ge(mean_ready, powers[0] + 1)
                nc.gpsimd.tensor_tensor(v, v, HALF[:, 0:v.shape[1]], ALU.pow).then_inc(rstd_ready, 1)
                powers[0] += 1

            step(nc.gpsimd.memset(IDENT[:, :], 0.0))
            step(nc.gpsimd.affine_select(out=IDENT[:, :], in_=IDENT[:, :], compare_op=ALU.not_equal, fill=1.0, base=0,
                                         pattern=[[-1, P]], channel_multiplier=1))
            step(nc.gpsimd.memset(HALF, -0.5))
            nc.gpsimd.memset(ONES, 1.0).then_inc(consts, 1)
            for c in range(2 * TT):
                rstd(RSTD[:, c:c + 1])
            pool.wait_ge(piece_used, C["mem_k0"].last + 1)
            step(nc.gpsimd.memset(PAT0[:, :, :], 1.0))
            step(nc.gpsimd.memset(MSK0[:, :, :], 1.0))
            for l in range(7):
                h = 1 << l
                v = PAT0[:, l, :].rearrange("p (b w o) -> p b w o", w=2, o=h)
                nb = P // (2 * h)
                keep_where(v[:, :, 0, :], [[-2 * h, nb], [-1, h]], -1, 1, 0.0)
                keep_where(v[:, :, 0, :], [[2 * h, nb], [0, h]], h - 1, -1, 0.0)
                keep_where(v[:, :, 1, :], [[-2 * h, nb], [0, h]], -h, 1, 0.0)
                keep_where(v[:, :, 1, :], [[2 * h, nb], [1, h]], h, -1, 0.0)
                m = MSK0[:, l, :].rearrange("p (b o) -> p b o", o=h)
                keep_where(m, [[-2 * h, nb], [0, h]], 0, 1, 0.0)
                keep_where(m, [[2 * h, nb], [0, h]], h - 1, -1, 0.0)
            keep_where(PAT0[:, 7, :], [[-1, P]], -1, 1, 0.0)
            keep_where(PAT0[:, 8, :], [[1, P]], 0, -1, 0.0)
            for d0, s0_, n_ in ((0, 0, 8), (8, 4, 3), (11, 8, 1)):
                step(nc.gpsimd.tensor_copy(PATTERN[:, d0:d0 + n_, :], PAT0[:, s0_:s0_ + n_, :]))
            nc.gpsimd.tensor_copy(LMASK[:, :, :], MSK0[:, :, :]).then_inc(consts, 1)
            nc.gpsimd.memset(AT[:, :, :, :], 0.0).then_inc(consts, 1)
            rstd(RG)
            pool.wait_ge(pv_ready, X_HEADS)
            pool.wait_ge(o_norm, GLA_HEADS)
            step(nc.gpsimd.memset(CB[:, :], 0.0))
            step(nc.gpsimd.memset(IDB[:, :], 0.0))
            step(nc.gpsimd.memset(CMB[:, :, :], 0.0))
            step(nc.gpsimd.memset(ROWOK[:, :], 1.0))
            keep_where(CB[:, :], [[-1, P]], 0, 1, MASKED)
            step(nc.gpsimd.affine_select(out=IDB[:, :], in_=IDB[:, :], compare_op=ALU.not_equal, fill=1.0, base=0,
                                         pattern=[[-1, P]], channel_multiplier=1))
            keep_where(CMB[:, :, :], [[P, TT], [-CMP_STRIDE, 16]], -(CMP_LEN - 1), 1, MASKED)
            nc.gpsimd.affine_select(out=ROWOK[:, :], in_=ROWOK[:, :], compare_op=ALU.is_ge, fill=0.0, base=-(CMP_LEN - 1),
                                    pattern=[[P, TT]], channel_multiplier=1).then_inc(consts2, 1)
            for c, w in ((4, 1), (5, 1), (6, TT), (8, 1), (9, 1)):
                rstd(RSTD[:, c:c + w])

        @block.tensor
        def _(pe):
            def transpose(stage, kt, n):
                if n >= 4:
                    pe.wait_ge(tr_lo, n - 3)
                for i in range(TT):
                    o = PS[4 + n % 4][:, i * P:(i + 1) * P]
                    if stage in ("row0", "row1"):
                        last = nc.tensor.matmul(o, ONESQ, DIAG[:, i * P:(i + 1) * P], start=i == 0, stop=True,
                                                skip_group_check=True)
                    elif stage == "mem1":
                        last = nc.tensor.transpose(o, MQ[kt // 4][:, i, kt % 4 * P:(kt % 4 + 1) * P], IDENT[:, :])
                    else:
                        last = nc.tensor.transpose(o, t_source(stage)[:, i, kt * P:(kt + 1) * P], IDENT[:, :])
                last.then_inc(tr_ready, 1)

            def products(n):
                ch, j = piece_of[n]
                if j == 0:
                    if ch.kind != CMP and ch.before:
                        pe.wait_ge(act_drained, ch.before.c + 1)
                        pe.wait_ge(dve_drained, dve_drains(ch.before.c))
                    if ch.kind == CMP:
                        pe.wait_ge(blk_ready, 1 if ch.lhs == "K" else 2)
                if "out" in ch.name:
                    key = (int(ch.name[0] == "n"), ch.order[2 * j] // 2)
                    if key in y_order:
                        pe.wait_ge(y_lo, y_order.index(key) + 1)
                    else:
                        pe.wait_ge(tr_lo, lhs_ready(ch, j))
                elif ch.kind != CMP and (j == 0 or lhs_ready(ch, j) > lhs_ready(ch, j - 1)):
                    pe.wait_ge(tr_lo, lhs_ready(ch, j))
                pe.wait_ge(lo_ready, n + 1)
                hi, lo = piece_view(WHI, n), piece_view(WLO, n)
                last = None
                xh, xl = (AHI, ALO) if ch.lhs == "A" else (BHI, BLO)
                for i, t in [(i, t) for i in range(TT) for t in range(ch.tiles)] if ch.kind == TM else ():
                    kt = ch.order[j * ch.tiles + t]
                    for q, (wt, xt) in enumerate(((hi, xh), (lo, xh), (hi, xl))):
                        last = nc.tensor.matmul(acc_bank(ch, i)[:, 0:ch.width], xt[:, kt, i * P:(i + 1) * P], wt[:, t, :],
                                                start=j == 0 and t == 0 and q == 0,
                                                stop=j == ch.n - 1 and t == ch.tiles - 1 and q == 2, skip_group_check=True)
                    if ch is chunks[-1] and j == ch.n - 1 and i == 0 and t == ch.tiles - 1:
                        last.then_inc(tile0_done, 1)
                for t in range(ch.tiles) if ch.kind != TM else ():
                    kt = ch.order[j * ch.tiles + t]
                    first, end = j == 0 and t == 0, j == ch.n - 1 and t == ch.tiles - 1
                    if ch.kind == CMP:
                        g = "KV".index(ch.lhs)
                        for q, wt in enumerate((hi, lo)):
                            last = nc.tensor.matmul(acc_bank(ch, 0)[:, 0:CMP_HIDDEN], BK[:, g, 2 * NB * kt:2 * NB * kt + P],
                                                    wt[:, t, :], start=first and q == 0, stop=end and q == 1)
                        continue
                    outs = []
                    if ch.kind == NARROW:
                        stand = WHI[:, n % RING, 2 * t * ch.width:2 * t * ch.width + P]
                        for q, xt in enumerate((xh, xl)):
                            last = nc.tensor.matmul(acc_bank(ch, 0)[:, 0:SEQ], stand, xt[:, kt, :], start=first and q == 0,
                                                    stop=end and q == 1)
                    if ch.kind == FM:
                        outs = [(acc_bank(ch, b // 2)[:, b % 2 * SEQ:(b % 2 + 1) * SEQ], b % 2 == 0, slice(b * P, (b + 1) * P), None)
                                for b in range(4)]
                    if ch.kind == MIX:
                        outs = [(acc_bank(ch, 0)[:, b * SEQ:(b + 1) * SEQ], b == 0, slice(b * P, (b + 1) * P), None)
                                for b in range(2)]
                        outs += [(acc_bank(ch, 1)[:, i * KVW:(i + 1) * KVW], i == 0, slice(KVW, 2 * KVW), i) for i in range(TT)]
                    for o, opens, w, i in outs:
                        for q, (wt, xt) in enumerate(((hi, xh), (lo, xh), (hi, xl))):
                            ww = wt[:, t, w]
                            if i is None:
                                args = (ww, xt[:, kt, :])
                            else:
                                args = (xt[:, kt, i * P:(i + 1) * P], ww)
                            last = nc.tensor.matmul(o, *args, start=first and opens and q == 0, stop=end and q == 2,
                                                    skip_group_check=True)
                last.then_inc(piece_used, 1)

            def score_bank_free(s):
                if s >= 2:
                    kind, k = s_uses[s - 2]
                    if kind == "attn":
                        pe.wait_ge(pr_ready, k + 1)
                    else:
                        pe.wait_ge(cs_shift, k + 1)

            def keep_warm(count):
                for _ in range(count):
                    nc.tensor.matmul(PS[3][:, 0:P], IDENT[:, :], IDENT[:, :], start=True, stop=True)

            pe.wait_ge(consts, 1)
            keep_warm(6)
            pe.wait_ge(gains_in, 32)
            nc.tensor.transpose(PS[0][:, 0:4 * KT], G0[:, :], IDENT[0:4 * KT, 0:4 * KT]).then_inc(small_t, 1)
            pe.wait_ge(small_c, 1)
            d_no = s_no = 0
            for s in slots:
                if s == 0:
                    keep_warm(8)
                if s >= 0:
                    products(s)
                for st in steps.get(s, ()):
                    what = st[0]
                    if what == "transpose":
                        stage, kt = st[1:]
                        n = t_order[stage, kt]
                        if stage == "mem0" and kt % 4 == 0:
                            pe.wait_ge(mem_in[kt // 4], 16)
                        if stage == "mem1" and kt % 4 == 0:
                            pe.wait_ge(mem_again[kt // 4], 16)
                        if stage in ("row0", "row1"):
                            pe.wait_ge(diag_ready, 1 + int(stage[-1]))
                        if stage == "x0" and kt == 0:
                            pe.wait_ge(normed, TT)
                        if stage == "y0" and kt % 4 == 0:
                            pe.wait_ge(mixed_gated, TT * (gated_no(C[f"g_r{kt // 4}"]) + 1))
                            if kt == 0:
                                pe.wait_ge(pt_kept, X_HEADS)
                                pe.wait_ge(head_kept, X_HEADS)
                        if stage == "x1" and kt % 4 == 0:
                            pe.wait_ge(normed, TT + TT * (kt // 4 + 1))
                        transpose(stage, kt, n)
                    elif what == "gate":
                        i, = st[1:]
                        pe.wait_ge(act_drained, C["g_lr"].c + 1)
                        pe.wait_ge(wg_in, 48)
                        if i == 1:
                            pe.wait_ge(lg_ready, 1)
                        for k, (c0, w) in enumerate(((0, 512), (512, KEYW - 512))):
                            last = nc.tensor.matmul(PS[6 + k][:, 0:w], GLT[:, i * P:(i + 1) * P], WG[:, c0:c0 + w],
                                                    start=True, stop=True)
                        last.then_inc(z_ready, 1)
                    elif what == "decay":
                        p, d = st[1:]
                        g, ft, i = decay_unit(p, d)
                        if d_no == 0:
                            pe.wait_ge(lg_ready, TT)
                            pe.wait_ge(consts, 3)
                        if d_no >= 2:
                            pe.wait_ge(e_ready, d_no - 1)
                        if p == 1 and d == 0:
                            pe.wait_ge(o_kept, 2)
                        o = PS[4 + d_no % 2]
                        m = 4 * g * (i + 1)
                        for q, lg in enumerate((LGH, LGL)):
                            last = nc.tensor.matmul(o[:, :], lg[:, i, (3 * p + ft) * P:(3 * p + ft + 1) * P],
                                                    PATTERN[:, m:m + 4, :].rearrange("p l t -> p (l t)"),
                                                    start=q == 0, stop=q == 1)
                        last.then_inc(d_ready, 1)
                        d_no += 1
                    elif what == "qk_sums":
                        pe.wait_ge(qkp_ready, 1)
                        for i in range(TT):
                            for h in range(GLA_HEADS):
                                for k, (ft, r0, r1) in enumerate(head_rows(h)):
                                    last = nc.tensor.matmul(PS[7 - h % 2][:, h + i - h % 2:h + i - h % 2 + 1],
                                                            QKP[r0:r1, ft, i * P:(i + 1) * P], ONES[r0:r1, :],
                                                            start=i == 0 and h < 2 and k == 0, stop=k == 1,
                                                            skip_group_check=True)
                        last.then_inc(dq_ready, 1)
                    elif what == "gla_scores":
                        h, i = st[1:]
                        pe.wait_ge(qk_ready, LEVELS * (h // 2 + 1))
                        if h >= 1:
                            pe.wait_ge(at_ready, 2 * (h - 1) + i + 1)
                        else:
                            pe.wait_ge(dq_kept, 1)
                        o = PS[6 + i]
                        for l in range(LEVELS):
                            hf = 1 << l
                            for k, (ft, r0, r1) in enumerate(head_rows(h)):
                                ft -= 3 * (h // 2)
                                if l < 7:
                                    lhs = E[r0:r1, l, ft, i * P:(i + 1) * P]
                                    rhs = E[r0:r1, l, ft, i * P:(i + 1) * P].rearrange("p (b w o) -> p b w o", w=2, o=hf)[:, :, 1, :]
                                    dst = o[:, 64 * l:64 * (l + 1)].rearrange("p (b o) -> p b o", o=hf)
                                else:
                                    lhs = E[r0:r1, l, ft, 0:P]
                                    rhs = E[r0:r1, l, ft, P + 64 * i:P + 64 * (i + 1)]
                                    dst = o[:, 448:512]
                                last = nc.tensor.matmul(dst, lhs, rhs, start=l == 0 and k == 0, stop=k == 1,
                                                        skip_group_check=True)
                        last.then_inc(s_ready, 1)
                    elif what == "gla_out":
                        h, = st[1:]
                        pe.wait_ge(at_ready, 2 * h + 2)
                        pe.wait_ge(e_ready, 12 * (h // 2 + 1))
                        pe.wait_ge(act_drained, C[f"g_v{(384 * h + 383) // 512}"].c + 1)
                        pe.wait_ge(dve_drained, dve_drains(C[f"g_v{(384 * h + 383) // 512}"].c))
                        if h >= 1:
                            pe.wait_ge(o_kept, h)
                        v = slice(h * GLA_DV, (h + 1) * GLA_DV)
                        nc.tensor.matmul(PS[4][:, 0:GLA_DV], AT[:, h % 2, 0, :], V[:, 0, v], start=True, stop=True)
                        nc.tensor.matmul(PS[5][:, 0:GLA_DV], AT[:, h % 2, 2, :], V[:, 0, v], start=True, stop=False)
                        nc.tensor.matmul(PS[5][:, 0:GLA_DV], AT[:, h % 2, 1, :], V[:, 1, v], start=False, stop=True)\
                            .then_inc(o_ready, 1)
                    elif what == "scores":
                        unit, at_i = st[1:]
                        kind, which, h = unit
                        if at_i == 0:
                            pe.wait_ge(o_kept, GLA_HEADS)
                            pe.wait_ge(at_ready, 2 * GLA_HEADS)
                        score_bank_free(s_no)
                        bank = PS[4 + s_no % 2]
                        if kind == "x":
                            ch = C["g_xq" if which == 0 else "n_xq"]
                            pe.wait_ge(act_drained, ch.c + 1)
                            pe.wait_ge(dve_drained, dve_drains(ch.c))
                            for i in range(TT):
                                last = nc.tensor.matmul(bank[:, i * SEQ:(i + 1) * SEQ], XQT[:, h, i * P:(i + 1) * P],
                                                        KX[which][:, h, :], start=i == 0, stop=True, skip_group_check=True)
                        else:
                            ch = C[f"n_q{h // 4}"]
                            pe.wait_ge(act_drained, ch.c + 1)
                            pe.wait_ge(dve_drained, dve_drains(ch.c))
                            g = h // HPG
                            nc.tensor.matmul(bank[:, 0:P], NQT[:, h, 0:P], NKT[:, which, g, 0:P],
                                             start=True, stop=False, skip_group_check=True)
                            nc.tensor.matmul(bank[:, P:P + SEQ], NQT[:, h, P:SEQ], NKT[:, which, g, :],
                                             start=False, stop=False, skip_group_check=True)
                            nc.tensor.matmul(bank[:, 0:P], IDB[:, :], CB[:, :], start=False, stop=True, skip_group_check=True)
                            last = nc.tensor.matmul(bank[:, SEQ:SEQ + P], IDB[:, :], CB[:, :], start=False, stop=True,
                                                    skip_group_check=True)
                        last.then_inc(sc_ready, 1)
                        s_no += 1
                    elif what == "probs_t":
                        unit, t, at_i = st[1:]
                        kind, which, h = unit
                        if t >= 1:
                            pe.wait_ge(pt_kept, t)
                        if kind == "cmp":
                            pe.wait_ge(cs_done, h // 4 + 1)
                            for i in range(TT):
                                last = nc.tensor.transpose(PS[6][0:16, i * P:(i + 1) * P], PC[:, h // 4, 2 * (h % 4) + i, :],
                                                           IDENT[:, :])
                        else:
                            pe.wait_ge(pn_ready, at_i + 1)
                            pr = unit_probs(unit)[0]
                            for k in range(4 if kind == "x" else 3):
                                last = nc.tensor.transpose(PS[6][:, k * P:(k + 1) * P], pr[:, at_i % 2, k * P:(k + 1) * P],
                                                           IDENT[:, :])
                        last.then_inc(pt_ready, 1)
                    elif what == "pv":
                        unit, t, at_i = st[1:]
                        kind, which, h = unit
                        pe.wait_ge(pt_kept, t + 1)
                        e = head_no(unit)
                        if kind in ("x", "cmp"):
                            if e >= 1:
                                pe.wait_ge(head_kept, e)
                        if kind == "x":
                            pt = unit_probs(unit)[1][:, t % 2, :].rearrange("p (i m q) -> p i m q", i=TT, m=TT)
                            for m in range(TT):
                                last = nc.tensor.matmul(PS[7][:, 0:SEQ], VX[which][:, m, h * HD:(h + 1) * HD], pt[:, :, m, :],
                                                        start=m == 0, stop=m == 1)
                        elif kind == "cmp":
                            last = nc.tensor.matmul(PS[7][:, 0:SEQ], VC[:, h // HPG, :], PTC[0:N_CMP, t % 2, :],
                                                    start=True, stop=False, skip_group_check=True)
                        else:
                            g = slice(h // HPG * HD, (h // HPG + 1) * HD)
                            for m in range(TT):
                                last = nc.tensor.matmul(PS[7][:, m * P:SEQ], NV[:, which, m, g],
                                                        PT1[:, t % 2, m * SEQ:m * P + SEQ], start=False,
                                                        stop=which == 1 and m == 1, skip_group_check=True)
                        last.then_inc(pv_ready, 1)
                    elif what == "pe_t":
                        pe.wait_ge(pe_in, 32)
                        for g in range(2):
                            last = nc.tensor.transpose(PS[4][:, g * CMP_LEN:(g + 1) * CMP_LEN], PE0[:, g, :],
                                                       IDENT[0:CMP_LEN, 0:CMP_LEN])
                        last.then_inc(small_t, 1)
                    elif what == "nsa_gates":
                        pe.wait_ge(act_drained, C["n_gl"].c + 1)
                        for i in range(TT):
                            last = nc.tensor.transpose(PS[5][:, P * i:P * i + 2 * NG], GTR[:, i * P:(i + 1) * P],
                                                       IDENT[0:2 * NG, 0:2 * NG])
                        last.then_inc(gates_t, 1)
                    elif what == "hidden":
                        g, = st[1:]
                        pe.wait_ge(act_drained, C["n_wk1" if g == 0 else "n_wv1"].c + 1)
                        for t in range(2):
                            last = nc.tensor.transpose(PS[6][:, 64 * t:64 * t + 2 * NB], HT[:, g, t * P:(t + 1) * P],
                                                       IDENT[0:2 * NB, 0:2 * NB])
                        last.then_inc(hid_t, 1)
                    elif what == "cmp_kv":
                        g, = st[1:]
                        pe.wait_ge(hid_ready, g + 1)
                        pe.wait_ge(w2_in, 32)
                        if g == 0:
                            for t in range(2):
                                last = nc.tensor.matmul(PS[6][:, 0:NB], W2[:, 0, t, :], HID[:, 0, t, 0:NB], start=t == 0, stop=t == 1)
                        else:
                            pe.wait_ge(kvc_kept, 1)
                            for gr in range(NSA_GROUPS):
                                for t in range(2):
                                    last = nc.tensor.matmul(PS[6][0:N_CMP, gr * HD:(gr + 1) * HD],
                                                            HID[:, 1, t, gr * N_CMP:(gr + 1) * N_CMP], W2[:, 1, t, :],
                                                            start=gr == 0 and t == 0, stop=t == 1, skip_group_check=True)
                        last.then_inc(kvc_ready, 1)
                    elif what == "cmp_scores":
                        j, = st[1:]
                        if j == 0:
                            pe.wait_ge(kvc_kept, 2)
                            pe.wait_ge(consts2, 1)
                        ch = C[f"n_q{j}"]
                        pe.wait_ge(act_drained, ch.c + 1)
                        pe.wait_ge(dve_drained, dve_drains(ch.c))
                        score_bank_free(s_no)
                        bank = PS[4 + s_no % 2]
                        for hh in range(4):
                            h = 4 * j + hh
                            for i in range(TT):
                                o = bank[:, (2 * hh + i) * 16:(2 * hh + i) * 16 + N_CMP]
                                g = h // HPG
                                last = nc.tensor.matmul(o, NQT[:, h, i * P:(i + 1) * P], KC[:, g * N_CMP:(g + 1) * N_CMP],
                                                        start=hh == 0 and i == 0, stop=True, skip_group_check=True)
                        last.then_inc(cs_ready, 1)
                        s_no += 1

        @block.scalar
        def _(act):
            count = [0]

            def step(ins):
                count[0] += 1
                ins.then_inc(act_step, 1)
                act.wait_ge(act_step, count[0])

            def split_high(n):
                act.wait_ge(raw_in[n % RING], 16 * (n // RING + 1))
                if n >= RING:
                    act.wait_ge(piece_used, n - RING + 1)
                ch, j = piece_of[n]
                if ch.kind == NARROW:
                    nc.scalar.activation(narrow_parts(n, 0), piece_view(RAW, n), ACT.Copy).then_inc(hi_ready, 1)
                    return
                w = slice(0, ch.tiles * ch.width)
                nc.scalar.activation(WHI[:, n % RING, w], RAW[:, n % RING, w], ACT.Copy).then_inc(hi_ready, 1)

            def transposed_high(stage, kt, n):
                act.wait_ge(tr_ready, n + 1)
                if kt in (0, 12) and lhs_free(stage):
                    act.wait_ge(piece_used, C[lhs_free(stage)].last + 1)
                src = PS[4 + n % 4][:, 0:SEQ]
                if stage in ("row0", "row1"):
                    nc.scalar.activation(ROW[:, 0:P], src[:, 0:P], ACT.Copy).then_inc(tr_hi, 1)
                    return
                hi, lo, gain = t_dest(stage)
                nc.scalar.activation(hi[:, kt, :], src, ACT.Copy, scale=1.0 if gain is None else GT[:, gain + kt:gain + kt + 1])\
                    .then_inc(tr_hi, 1)

            def square(stage, i, src):
                nc.scalar.activation(SQUARES[:, 0:D_MODEL], src, ACT.Square, accum_out=SS[:, 2 * stage + i:2 * stage + i + 1])\
                    .then_inc(squared, 1)

            act.wait_ge(consts, 1)
            nc.scalar.activation(ST[:, 145:146], ONES, ACT.Copy)
            act.wait_ge(small_t, 1)
            nc.scalar.activation(GT[:, :], PS[0][:, 0:4 * KT], ACT.Copy).then_inc(small_c, 1)
            act.wait_ge(small_c, 1)
            s_no = d_no = 0
            for s in slots:
                for n in splits_before(s):
                    split_high(n)
                here = sorted(steps.get(s, ()), key=lambda st: 4.5 if "scores" in st[0] and "gla" not in st[0] else rank(st))
                for st in here + [("late_split",)]:
                    what = st[0]
                    if what == "first_split":
                        split_high(0)
                    elif what == "late_split":
                        for n in splits_after(s):
                            split_high(n)
                    elif what == "square":
                        stage, i = st[1:]
                        if stage:
                            act.wait_ge(x_in[i], 32)
                        elif i == 0:
                            for q in range(4):
                                act.wait_ge(mem_in[q], 16)
                        if stage or i:
                            act.wait_ge(squared, TT * stage + i)
                        square(stage, i, (H if stage else Y)[:, i, :])
                    elif what == "transpose":
                        transposed_high(*st[1:], t_order[st[1:]])
                    elif what == "drain":
                        ch, = st[1:]
                        if ch is chunks[-1]:
                            act.wait_ge(tile0_done, 1)
                        else:
                            act.wait_ge(piece_used, ch.last + 1)
                        src, scale = acc_bank(ch, 0), 1.0
                        if ch.name.startswith("mem_k"):
                            dst = KX[int(ch.name[-1])][:, 0:2, :].rearrange("p b t -> p (b t)")
                        elif ch.name.startswith("mem_v"):
                            dst, scale = VX[int(ch.name[-1])][:, 0, :], RSTD[:, 0:1]
                            act.wait_ge(rstd_ready, TT)
                        elif ch.name == "g_lr":
                            act.wait_ge(dve_drained, dve_drains(ch.c))
                            dst, src = GLT[0:2 * RANK, :], src[0:2 * RANK, 0:SEQ]
                        elif ch.name.startswith("g_qk"):
                            j = int(ch.name[-1])
                            dst = QK[:, 4 * j:4 * j + 2, :].rearrange("p b t -> p (b t)")
                            scale = GLA_SCALE if 4 * j < FT else 1.0
                        elif ch.name.startswith("g_v"):
                            j = int(ch.name[-1])
                            dst = V[:, 0, 512 * j:512 * (j + 1)]
                        elif ch.name in ("g_xq", "n_xq"):
                            if ch.name == "n_xq":
                                act.wait_ge(sc_ready, X_HEADS)
                            dst = XQT[:, 0:2, :].rearrange("p b t -> p (b t)")
                        elif "out" in ch.name:
                            j = int(ch.name[-1])
                            k = 4 * (ch.name[0] == "n") + j
                            if j == 0:
                                act.wait_ge(mixed_gated, TT * 4 * (1 + (ch.name[0] == "n")))
                            if k:
                                act.wait_ge(y_sq, k)
                                act.wait_ge(act_drained, ch.c)
                            for i in range(TT):
                                if ch is chunks[-1] and i:
                                    act.wait_ge(piece_used, ch.last + 1)
                                nc.scalar.activation(SG[:, i, :], acc_bank(ch, i)[:, :], ACT.Square,
                                                     accum_out=YSS[k // 4][:, i, j:j + 1]).then_inc(act_drained if i else y_sq, 1)
                            continue
                        elif ch.name == "n_gl":
                            nc.scalar.activation(GTR[:, :], src[0:2 * NG, 0:SEQ], ACT.Copy).then_inc(act_drained, 1)
                            continue
                        elif ch.name == "n_cmp":
                            dst = KVC[:, 0].rearrange("p g t -> p (g t)")
                        elif ch.name in ("n_slc", "n_win"):
                            dst = NKT[:, 0 if ch.name == "n_slc" else 1].rearrange("p g t -> p (g t)")
                        elif ch.name.startswith("n_q"):
                            j = int(ch.name[-1])
                            dst = NQT[:, 4 * j:4 * j + 2, :].rearrange("p b t -> p (b t)")
                        nc.scalar.activation(dst, src if ch.kind == NARROW else src[:, 0:512], ACT.Copy, scale=scale)\
                            .then_inc(act_drained, 1)
                    elif what == "gated_drain":
                        ch, i = st[1:]
                        act.wait_ge(piece_used, ch.last + 1)
                        if gated_no(ch):
                            act.wait_ge(mixed_gated, TT * (gated_no(ch) - 1) + i + 1)
                        nc.scalar.activation(SG[:, i, :], acc_bank(ch, i)[:, :], ACT.Silu)\
                            .then_inc(act_drained if i else sg_exp, 1)
                    elif what == "hidden_drain":
                        ch, = st[1:]
                        g = "KV".index(ch.lhs)
                        act.wait_ge(piece_used, ch.last + 1)
                        nc.scalar.activation(HT[:, g, :], acc_bank(ch, 0)[0:2 * NB, 0:CMP_HIDDEN], ACT.Copy).then_inc(act_drained, 1)
                    elif what == "nsa_gates":
                        act.wait_ge(gates_sum, 1)
                        nc.scalar.activation(GATES[:, :, 0:NG], GATES[:, :, 0:NG], ACT.Sigmoid).then_inc(gates_sig, 1)
                    elif what == "hidden":
                        g, = st[1:]
                        act.wait_ge(hid_t, g + 1)
                        nc.scalar.activation(HB[:, g, :, 0:2 * NB],
                                             PS[6][:, 0:128].rearrange("p (t n) -> p t n", t=2)[:, :, 0:2 * NB], ACT.Copy)\
                            .then_inc(hid_parts, 1)
                        act.wait_ge(hid_sum, g + 1)
                        nc.scalar.activation(HSG[:, g, :, 0:NB], HB[:, g, :, 0:NB], ACT.Exp, scale=-1.0).then_inc(hid_exp, 1)
                    elif what == "gate":
                        i, = st[1:]
                        act.wait_ge(z_ready, i + 1)
                        step(nc.scalar.activation(ZA[:, 0:512], PS[6][:, :], ACT.Abs))
                        step(nc.scalar.activation(ZA[:, 512:KEYW], PS[7][:, 0:KEYW - 512], ACT.Abs))
                        nc.scalar.activation(ZA[:, :], ZA[:, :], ACT.Exp, scale=-1.0).then_inc(za_exp, 1)
                    elif what == "gate_ln":
                        i, = st[1:]
                        act.wait_ge(za_exp, i + 1)
                        nc.scalar.activation(ZL[:, :], ZA[:, :], ACT.Ln, bias=1.0).then_inc(z_exp, 1)
                    elif what == "decay":
                        p, d = st[1:]
                        g, ft, i = decay_unit(p, d)
                        act.wait_ge(d_ready, d_no + 1)
                        if d == 0 and p == 1:
                            act.wait_ge(s_ready, 4)
                        nc.scalar.activation(E[:, 4 * g:4 * g + 4, ft, i * P:(i + 1) * P],
                                             PS[4 + d_no % 2][:, :].rearrange("p (l t) -> p l t", l=4), ACT.Exp,
                                             scale=1.0 / GATE_TEMP).then_inc(e_ready, 1)
                        d_no += 1
                    elif what == "gla_out":
                        h, = st[1:]
                        act.wait_ge(o_kept, h + 1)
                        for i in range(TT):
                            nc.scalar.activation(SG[:, i, 0:GLA_DV], V[:, i, h * GLA_DV:(h + 1) * GLA_DV], ACT.Square,
                                                 accum_out=SSG[:, 2 * h + i:2 * h + i + 1]).then_inc(o_sq, 1)
                            act.wait_ge(o_sq, 2 * h + i + 1)
                    elif what == "scores":
                        unit, at_i = st[1:]
                        kind, which, h = unit
                        act.wait_ge(mx_ready, at_i + 1)
                        if at_i >= 2:
                            act.wait_ge(pt_ready, attn_units[at_i - 2] + 1)
                        pr = unit_probs(unit)[0]
                        bank, b = PS[4 + s_no % 2], at_i % 2
                        spans = ((0, SEQ), (SEQ, 2 * SEQ)) if kind == "x" else ((0, P), (P, P + SEQ))
                        if kind == "nsa" and at_i == X_HEADS:
                            act.wait_ge(consts2, 1)
                        for i, (c0, c1) in enumerate(spans):
                            ins = nc.scalar.activation(pr[:, b, c0:c1], bank[:, c0:c1], ACT.Exp, scale=ATT_SCALE,
                                                       bias=NM[:, 2 * b + i:2 * b + i + 1], accum_out=RS[:, 2 * b + i:2 * b + i + 1])
                        ins.then_inc(pr_ready, 1)
                        s_no += 1
                    elif what == "probs_t":
                        unit, t, at_i = st[1:]
                        act.wait_ge(pt_ready, t + 1)
                        if t >= 2:
                            act.wait_ge(pv_ready, t - 1)
                        if unit[0] == "cmp":
                            nc.scalar.activation(PTC[:, t % 2, :], PS[6][0:16, 0:SEQ], ACT.Copy).then_inc(pt_kept, 1)
                        else:
                            w = 512 if unit[0] == "x" else 384
                            nc.scalar.activation(unit_probs(unit)[1][:, t % 2, 0:w], PS[6][:, 0:w], ACT.Copy).then_inc(pt_kept, 1)
                    elif what == "pv":
                        unit, t, at_i = st[1:]
                        kind, which, h = unit
                        if kind == "x" or (kind == "nsa" and which == 1):
                            act.wait_ge(pv_ready, t + 1)
                            layer = which if kind == "x" else 1
                            tile = h + (BW // P if kind == "x" else 0)
                            nc.scalar.activation(mixed_head(layer, tile), PS[7][:, 0:SEQ], ACT.Copy).then_inc(head_kept, 1)
                    elif what == "gated_split":
                        ch, i = st[1:]
                        layer, pair = int(ch.name[0] == "n"), gated_pair(ch, i)
                        act.wait_ge(mixed_gated, TT * gated_no(ch) + i + 1)
                        if "xg" in ch.name and i == 0:
                            act.wait_ge(pv_ready, X_HEADS if layer == 0 else t_unit)
                            act.wait_ge(piece_used, C["mem_k0" if layer == 0 else "mem_k1"].last + 1)
                        dst = (AHI, BHI)[layer][:, 2 * pair:2 * pair + 2, :].rearrange("p t q -> p (t q)")
                        nc.scalar.activation(dst, mixed_pair(layer, pair), ACT.Copy).then_inc(y_hi, 1)
                    elif what == "cmp_scores":
                        j, = st[1:]
                        act.wait_ge(cs_shift, j + 1)
                        nc.scalar.activation(PC[:, j, :, 0:N_CMP], PC[:, j, :, 0:N_CMP], ACT.Exp, scale=ATT_SCALE).then_inc(cs_exp, 1)
                        s_no += 1
                    elif what == "stream_square":
                        k, = st[1:]
                        i, q = divmod(k, 4)
                        act.wait_ge(res_ready, k + 1)
                        if k >= 2:
                            act.wait_ge(squared, 2 * TT + k - 1)
                        nc.scalar.activation(SG[:, k % 2, :], H[:, i, 512 * q:512 * (q + 1)], ACT.Square,
                                             accum_out=HSS[:, i, q:q + 1]).then_inc(squared, 1)

        @block.vector
        def _(dve):
            count = [0]

            def step(ins):
                count[0] += 1
                ins.then_inc(dve_step, 1)
                dve.wait_ge(dve_step, count[0])

            def split_low(n):
                dve.wait_ge(hi_ready, n + 1)
                ch, j = piece_of[n]
                if ch.kind == NARROW:
                    nc.vector.tensor_tensor(narrow_parts(n, 1), piece_view(RAW, n), narrow_parts(n, 0).bitcast(f32), ALU.subtract)\
                        .then_inc(lo_ready, 1)
                    return
                w = slice(0, ch.tiles * ch.width)
                nc.vector.tensor_tensor(WLO[:, n % RING, w], RAW[:, n % RING, w], WHI[:, n % RING, w].bitcast(f32), ALU.subtract)\
                    .then_inc(lo_ready, 1)

            rstds = [0]

            def mean(dst, src, n):
                nc.vector.tensor_scalar(dst, src, 1.0 / n, EPS, ALU.mult, ALU.add).then_inc(mean_ready, 1)
                rstds[0] += 1

            def root():
                dve.wait_ge(rstd_ready, rstds[0])

            def row_root(l, i):
                c = 4 + 4 * l + i
                step(nc.vector.tensor_reduce(SS[:, c:c + 1], YSS[l][:, i, :], AX.X, ALU.add))
                mean(RSTD[:, c:c + 1], SS[:, c:c + 1], D_MODEL)

            def transposed_low(stage, kt, n):
                dve.wait_ge(tr_hi, n + 1)
                src = PS[4 + n % 4][:, 0:SEQ]
                if stage in ("row0", "row1"):
                    nc.vector.tensor_copy(ROW[:, P:SEQ], src[:, P:SEQ]).then_inc(tr_lo, 1)
                    return
                hi, lo, gain = t_dest(stage)
                if gain is None:
                    last = nc.vector.tensor_tensor(lo[:, kt, :], src, hi[:, kt, :].bitcast(f32), ALU.subtract)
                else:
                    last = nc.vector.scalar_tensor_tensor(lo[:, kt, :], src, GT[:, gain + kt:gain + kt + 1],
                                                          hi[:, kt, :].bitcast(f32), ALU.mult, ALU.subtract)
                last.then_inc(tr_lo, 1)

            dve.wait_ge(small_c, 1)
            s_no = 0
            for s in slots:
                here = steps.get(s, ())
                early = [st for st in here if st[0] == "probs_t"]
                for st in early + [("split",)] + [st for st in here if st not in early] + [("late_split",)]:
                    what = st[0]
                    if what == "first_split":
                        split_low(0)
                    elif what == "split":
                        for n in splits_before(s):
                            split_low(n)
                    elif what == "late_split":
                        for n in splits_after(s):
                            split_low(n)
                    elif what == "square":
                        stage, i = st[1:]
                        c = TT * stage + i
                        dve.wait_ge(squared, c + 1)
                        mean(RSTD[:, c:c + 1], SS[:, c:c + 1], D_MODEL)
                    elif what == "scale":
                        i, = st[1:]
                        root()
                        nc.vector.tensor_scalar(H[:, i, :], H[:, i, :], RSTD[:, 2 + i:3 + i], None, ALU.mult).then_inc(normed, 1)
                    elif what == "transpose":
                        transposed_low(*st[1:], t_order[st[1:]])
                    elif what == "diagonal":
                        dve.wait_ge(rstd_ready, TT)
                        nc.vector.memset(ONESQ, 1.0)
                        for i in range(TT):
                            ins = nc.vector.tensor_scalar(DIAG[:, i * P:(i + 1) * P], IDENT[:, :], RSTD[:, i:i + 1], None,
                                                          ALU.mult)
                        ins.then_inc(diag_ready, 1)
                    elif what == "drain":
                        ch, = st[1:]
                        src, scale = acc_bank(ch, 1), None
                        if ch.kind == NARROW:
                            if ch.name == "g_lr":
                                dve.wait_ge(squared, TT)
                                dve.wait_ge(tr_lo, t_done("mem0"))
                                nc.vector.memset(GLT[:, :], 1.0).then_inc(dve_drained, 1)
                            continue
                        if ch is chunks[-1]:
                            dve.wait_ge(tile0_done, 1)
                        else:
                            dve.wait_ge(piece_used, ch.last + 1)
                        if ch.name.startswith("mem_k"):
                            kx = KX[int(ch.name[-1])]
                            row = ROW.unsqueeze(1).to_broadcast([P, 2, SEQ])
                            dve.wait_ge(tr_hi, t_done("row" + ch.name[-1]))
                            dve.wait_ge(tr_lo, t_done("row" + ch.name[-1]))
                            nc.vector.tensor_tensor(kx[:, 2:4, :], src[:, 0:512].rearrange("p (b t) -> p b t", b=2), row, ALU.mult)\
                                .then_inc(dve_drained, 1)
                            dve.wait_ge(act_drained, ch.c + 1)
                            step(nc.vector.tensor_tensor(kx[:, 0:2, :], kx[:, 0:2, :], row, ALU.mult))
                            continue
                        elif ch.name.startswith("mem_v"):
                            dst, scale = VX[int(ch.name[-1])][:, 1, :], RSTD[:, 1:2]
                            dve.wait_ge(rstd_ready, TT)
                        elif ch.name.startswith("g_qk"):
                            j = int(ch.name[-1])
                            dst = QK[:, 4 * j + 2:4 * j + 4, :].rearrange("p b t -> p (b t)")
                            scale = GLA_SCALE if 4 * j + 2 < FT else None
                        elif ch.name.startswith("g_v"):
                            j = int(ch.name[-1])
                            dst = V[:, 1, 512 * j:512 * (j + 1)]
                        elif ch.name in ("g_xq", "n_xq"):
                            if ch.name == "n_xq":
                                dve.wait_ge(sc_ready, X_HEADS)
                            dst = XQT[:, 2:4, :].rearrange("p b t -> p (b t)")
                        elif "out" in ch.name:
                            j = int(ch.name[-1])
                            l = int(ch.name[0] == "n")
                            dve.wait_ge(post_in[l], 16)
                            c0 = slice(512 * j, 512 * (j + 1))
                            dve.wait_ge(y_sq, 4 * l + j + 1)
                            if j == 0:
                                dve.wait_ge(tr_ready, t_done("y0"))
                                dve.wait_ge(y_hi, len(y_order) if l else 2)
                            nc.vector.tensor_tensor(Y[:, 0, c0], acc_bank(ch, 0)[:, :], GPOST[l][:, c0], ALU.mult)
                            if j == 3:
                                row_root(l, 0)
                            dve.wait_ge(act_drained, ch.c + 1)
                            if j == 3:
                                row_root(l, 1)
                            if ch is chunks[-1]:
                                continue
                            nc.vector.tensor_tensor(Y[:, 1, c0], acc_bank(ch, 1)[:, :], GPOST[l][:, c0], ALU.mult)\
                                .then_inc(dve_drained, 1)
                            continue
                        elif ch.name == "n_cmp":
                            dst = KVC[:, 1].rearrange("p g t -> p (g t)")
                        elif ch.name in ("n_slc", "n_win"):
                            dst = NV[:, 0 if ch.name == "n_slc" else 1].rearrange("p i w -> p (i w)")
                        elif ch.name.startswith("n_q"):
                            j = int(ch.name[-1])
                            dst = NQT[:, 4 * j + 2:4 * j + 4, :].rearrange("p b t -> p (b t)")
                        if scale is None:
                            nc.vector.tensor_copy(dst, src[:, 0:512]).then_inc(dve_drained, 1)
                        else:
                            nc.vector.tensor_scalar(dst, src[:, 0:512], scale, None, ALU.mult).then_inc(dve_drained, 1)
                    elif what == "gated_drain":
                        ch, i = st[1:]
                        k = gated_no(ch)
                        if k in (0, 2, 3):
                            dve.wait_ge(o_norm, (512 * int(ch.name[-1]) + 511) // GLA_DV + 1)
                        if k == 1:
                            dve.wait_ge(head_kept, X_HEADS)
                        if k == 4:
                            dve.wait_ge(head_kept, len(heads))
                        if i == 0:
                            dve.wait_ge(sg_exp, k + 1)
                        else:
                            dve.wait_ge(act_drained, ch.c + 1)
                        if ch.kind == TM:
                            v = Y[:, i, 512 * int(ch.name[-1]):512 * (int(ch.name[-1]) + 1)]
                        else:
                            v = mixed_pair(int(ch.name[0] == "n"), gated_pair(ch, i))
                        nc.vector.tensor_tensor(v, v, SG[:, i, :], ALU.mult).then_inc(mixed_gated, 1)
                    elif what == "gated_split":
                        ch, i = st[1:]
                        layer, pair = int(ch.name[0] == "n"), gated_pair(ch, i)
                        dve.wait_ge(y_hi, y_order.index((layer, pair)) + 1)
                        dve.wait_ge(mixed_gated, TT * gated_no(ch) + i + 1)
                        hi, lo = [b[:, 2 * pair:2 * pair + 2, :].rearrange("p t q -> p (t q)")
                                  for b in ((AHI, ALO), (BHI, BLO))[layer]]
                        nc.vector.tensor_tensor(lo, mixed_pair(layer, pair), hi.bitcast(f32), ALU.subtract).then_inc(y_lo, 1)
                    elif what == "hidden":
                        g, = st[1:]
                        dve.wait_ge(hid_parts, g + 1)
                        a0, b0 = HB[:, g, :, 0:NB], HB[:, g, :, NB:2 * NB]
                        nc.vector.tensor_tensor(a0, a0, b0, ALU.add).then_inc(hid_sum, 1)
                        dve.wait_ge(hid_exp, g + 1)
                        v = HSG[:, g, :, 0:NB]
                        step(nc.vector.tensor_scalar(v, v, 1.0, None, ALU.add))
                        step(nc.vector.reciprocal(v, v))
                        nc.vector.tensor_tensor(HID[:, g, :, 0:NB], v, a0, ALU.mult).then_inc(hid_ready, 1)
                    elif what == "nsa_gates":
                        dve.wait_ge(gates_t, 1)
                        parts = PS[5][:, 0:SEQ].rearrange("p (i w) -> p i w", i=TT)
                        step(nc.vector.tensor_copy(GATES[:, :, 0:NG], parts[:, :, 0:NG]))
                        nc.vector.tensor_tensor(GATES[:, :, 0:NG], GATES[:, :, 0:NG], parts[:, :, NG:2 * NG], ALU.add)\
                            .then_inc(gates_sum, 1)
                    elif what == "gate_ln":
                        i, = st[1:]
                        dve.wait_ge(z_exp, i + 1)
                        nc.vector.scalar_tensor_tensor(ZG[:, 0:512], PS[6][:, :], 0.0, ZL[:, 0:512], ALU.min, ALU.subtract)
                        step(nc.vector.scalar_tensor_tensor(ZG[:, 512:KEYW], PS[7][:, 0:KEYW - 512], 0.0, ZL[:, 512:KEYW],
                                                            ALU.min, ALU.subtract))
                        step(nc.vector.tensor_copy(LGH[:, i, :], ZG[:, :]))
                        nc.vector.tensor_tensor(LGL[:, i, :], ZG[:, :], LGH[:, i, :].bitcast(f32), ALU.subtract).then_inc(lg_ready, 1)
                    elif what == "qk_products":
                        dve.wait_ge(act_drained, C["g_qk2"].c + 1)
                        dve.wait_ge(dve_drained, dve_drains(C["g_qk2"].c))
                        nc.vector.tensor_tensor(QKP[:, :, :], QK[:, 0:FT, :], QK[:, FT:2 * FT, :], ALU.mult).then_inc(qkp_ready, 1)
                    elif what == "qk_sums":
                        dve.wait_ge(dq_ready, 1)
                        for par in range(2):
                            ins = nc.vector.tensor_copy(DQ.rearrange("p (g w i) -> p g w i", w=2, i=TT)[:, :, par, :],
                                                        PS[7 - par][:, 0:4].rearrange("p (g i) -> p g i", i=TT))
                        ins.then_inc(dq_kept, 1)
                    elif what == "decayed":
                        p, l = st[1:]
                        dve.wait_ge(e_ready, 12 * p + 6 * (l // 4 + 1))
                        hf = 1 << l

                        def halves(x, w):
                            return x.rearrange("p f t -> p (f t)").rearrange("p (b w o) -> p b w o", w=2, o=hf)[:, :, w, :]

                        e = E[:, l, :, :]
                        nc.vector.tensor_tensor(halves(e, 1), halves(e, 1), halves(QK[:, 3 * p:3 * p + 3, :], 1), ALU.mult)
                        nc.vector.tensor_tensor(halves(e, 0), halves(e, 0), halves(QK[:, FT + 3 * p:FT + 3 * p + 3, :], 0), ALU.mult)\
                            .then_inc(qk_ready, 1)
                    elif what == "gla_scores":
                        h, i = st[1:]
                        dve.wait_ge(s_ready, 2 * h + i + 1)
                        if h == 0 and i == 0:
                            dve.wait_ge(consts, 3)
                        if h >= 2:
                            dve.wait_ge(o_ready, h - 1)
                        for l in range(7):
                            hf = 1 << l
                            dst = AT[:, h % 2, i, :].rearrange("p (b w o) -> p b w o", w=2, o=hf)[:, :, 1, :]
                            src = PS[6 + i][:, 64 * l:64 * (l + 1)].rearrange("p (b o) -> p b o", o=hf)
                            msk = LMASK[:, l, :].rearrange("p (b o) -> p b o", o=hf)
                            step(nc.vector.copy_predicated(dst, msk, src))
                        nc.vector.tensor_copy(AT[:, h % 2, 2, 64 * i:64 * (i + 1)], PS[6 + i][:, 448:512]).then_inc(at_ready, 1)
                    elif what == "gla_out":
                        h, = st[1:]
                        dve.wait_ge(o_ready, h + 1)
                        v = slice(h * GLA_DV, (h + 1) * GLA_DV)
                        for i in range(TT):
                            ins = nc.vector.scalar_tensor_tensor(V[:, i, v], V[:, i, v], DQ[:, 2 * h + i:2 * h + i + 1],
                                                                 PS[4 + i][:, 0:GLA_DV], ALU.mult, ALU.add)
                        ins.then_inc(o_kept, 1)
                    elif what == "gla_root":
                        dve.wait_ge(o_sq, 2 * GLA_HEADS)
                        mean(RG, SSG, GLA_DV)
                    elif what == "gla_norm":
                        h, = st[1:]
                        if h == 0:
                            dve.wait_ge(gn_in, 16)
                            root()
                        v = slice(h * GLA_DV, (h + 1) * GLA_DV)
                        for i in range(TT):
                            ins = nc.vector.scalar_tensor_tensor(Y[:, i, v], V[:, i, v], RG[:, 2 * h + i:2 * h + i + 1],
                                                                 GN[:, :], ALU.mult, ALU.mult)
                        ins.then_inc(o_norm, 1)
                    elif what == "scores":
                        unit, at_i = st[1:]
                        kind, which, h = unit
                        dve.wait_ge(sc_ready, at_i + 1)
                        bank, b = PS[4 + s_no % 2], at_i % 2
                        m = MX[:, 2 * b:2 * b + 2]
                        if kind == "x":
                            step(nc.vector.tensor_reduce(m, bank[:, :].rearrange("p (i k) -> p i k", i=TT), AX.X, ALU.max))
                        else:
                            nc.vector.tensor_reduce(m[:, 0:1], bank[:, 0:P], AX.X, ALU.max)
                            step(nc.vector.tensor_reduce(m[:, 1:2], bank[:, P:P + SEQ], AX.X, ALU.max))
                        nc.vector.tensor_scalar(NM[:, 2 * b:2 * b + 2], m, -ATT_SCALE, None, ALU.mult).then_inc(mx_ready, 1)
                        s_no += 1
                    elif what == "probs_t":
                        unit, t, at_i = st[1:]
                        kind, which, h = unit
                        if kind == "cmp":
                            continue
                        b = at_i % 2
                        dve.wait_ge(pr_ready, at_i + 1)
                        ri = RI[:, 2 * b:2 * b + 2]
                        step(nc.vector.reciprocal(ri, RS[:, 2 * b:2 * b + 2]))
                        if kind == "nsa":
                            dve.wait_ge(gates_sig, 1)
                            step(nc.vector.tensor_tensor(ri, ri, GATES[:, :, N_BRANCH * h + 1 + which], ALU.mult))
                        pr = unit_probs(unit)[0]
                        for i, (c0, c1) in enumerate(((0, SEQ), (SEQ, 2 * SEQ)) if kind == "x" else ((0, P), (P, P + SEQ))):
                            ins = nc.vector.tensor_scalar(pr[:, b, c0:c1], pr[:, b, c0:c1], ri[:, i:i + 1], None, ALU.mult)
                        ins.then_inc(pn_ready, 1)
                    elif what == "pe_t":
                        dve.wait_ge(small_t, 2)
                        nc.vector.tensor_copy(PET[:, :, :].rearrange("p g j -> p (g j)"), PS[4][:, 0:2 * CMP_LEN]).then_inc(small_c, 1)
                    elif what == "blocks":
                        g, = st[1:]
                        dve.wait_ge(act_drained, C["n_cmp"].c + 1)
                        dve.wait_ge(dve_drained, dve_drains(C["n_cmp"].c))
                        dve.wait_ge(small_c, 2)
                        if g:
                            dve.wait_ge(blk_ready, g)
                        for half in range(2):
                            for gr in range(NSA_GROUPS):
                                src = KVC[:, g, gr, half * 16:half * 16 + 16 * N_CMP].rearrange("p (n j) -> p j n", j=16)
                                pe_b = PET[:, g, half * 16:(half + 1) * 16].unsqueeze(2).to_broadcast([P, 16, N_CMP])
                                dst = BKT[:, half * 16:(half + 1) * 16, gr * N_CMP:(gr + 1) * N_CMP]
                                last = nc.vector.tensor_tensor(dst, src, pe_b, ALU.add)
                        step(last)
                        parts = BK[:, g, 0:2 * NB * CMP_LEN].rearrange("p (j w n) -> p j w n", w=2, n=NB)
                        nc.vector.memset(BK[:, g, 2 * NB * CMP_LEN:].bitcast(f32), 0.0)
                        step(nc.vector.tensor_copy(parts[:, :, 0, :], BKT[:, :, :]))
                        nc.vector.tensor_tensor(parts[:, :, 1, :], BKT[:, :, :], parts[:, :, 0, :].bitcast(f32), ALU.subtract)\
                            .then_inc(blk_ready, 1)
                    elif what == "cmp_kv":
                        g, = st[1:]
                        dve.wait_ge(kvc_ready, g + 1)
                        if g == 0:
                            nc.vector.tensor_copy(KC[:, 0:NB], PS[6][:, 0:NB]).then_inc(kvc_kept, 1)
                            nc.vector.memset(PC[:, :, :, :], 0.0)
                        else:
                            nc.vector.tensor_copy(VC[:, :, :].rearrange("p g d -> p (g d)"), PS[6][0:N_CMP, 0:SEQ]).then_inc(kvc_kept, 1)
                    elif what == "cmp_scores":
                        j, = st[1:]
                        dve.wait_ge(cs_ready, j + 1)
                        bank = PS[4 + s_no % 2][:, 0:128].rearrange("p (h i n) -> p h i n", i=TT, n=16)
                        m, sm, fc = MC[:, 8 * j:8 * j + 8], SC[:, 8 * j:8 * j + 8], FC[:, 8 * j:8 * j + 8]
                        pc = PC[:, j, :, 0:N_CMP]
                        for i in range(TT):
                            ins = nc.vector.tensor_tensor(PC[:, j, :, 0:N_CMP].rearrange("p (h i) n -> p h i n", i=TT)[:, :, i, :],
                                                          bank[:, :, i, 0:N_CMP],
                                                          CMB[:, i, 0:N_CMP].unsqueeze(1).to_broadcast([P, 4, N_CMP]), ALU.add)
                        step(ins)
                        step(nc.vector.tensor_reduce(m, pc, AX.X, ALU.max))
                        nc.vector.tensor_tensor(pc, pc, m.unsqueeze(2).to_broadcast([P, 8, N_CMP]), ALU.subtract).then_inc(cs_shift, 1)
                        dve.wait_ge(cs_exp, j + 1)
                        step(nc.vector.tensor_reduce(sm, pc, AX.X, ALU.add))
                        step(nc.vector.reciprocal(fc, sm))
                        fv = fc.rearrange("p (h i) -> p h i", i=TT)
                        step(nc.vector.tensor_tensor(fv, fv, ROWOK[:, :].unsqueeze(1).to_broadcast([P, 4, TT]), ALU.mult))
                        dve.wait_ge(gates_sig, 1)
                        gv = GATES[:, :, 12 * j:12 * j + 12].rearrange("p i (h b) -> p h i b", b=N_BRANCH)[:, :, :, 0]
                        step(nc.vector.tensor_tensor(fv, fv, gv, ALU.mult))
                        nc.vector.tensor_tensor(pc, pc, fc.unsqueeze(2).to_broadcast([P, 8, N_CMP]), ALU.mult).then_inc(cs_done, 1)
                        s_no += 1
                    elif what == "residual":
                        l, k = st[1:]
                        i, q = divmod(k, 4)
                        if q == 0:
                            dve.wait_ge(rstd_ready, rstds[0] - 1 + i)
                        if k == 0 and l == 0:
                            dve.wait_ge(dve_drained, dve_drains(C["g_out3"].c))
                            dve.wait_ge(res_in, 16 * TT)
                        if k == 4 and l == 1:
                            ch = chunks[-1]
                            v = Y[:, 1, D_MODEL - ch.width:D_MODEL]
                            nc.vector.tensor_tensor(v, acc_bank(ch, 1)[:, :], GPOST[1][:, D_MODEL - ch.width:], ALU.mult)\
                                .then_inc(dve_drained, 1)
                            dve.wait_ge(dve_drained, dve_drains(ch.c))
                        c0 = slice(512 * q, 512 * (q + 1))
                        r = 4 + 4 * l + i
                        nc.vector.scalar_tensor_tensor(H[:, i, c0], Y[:, i, c0], RSTD[:, r:r + 1], H[:, i, c0], ALU.mult,
                                                       ALU.add).then_inc(res_ready, 1)
                    elif what == "stream_root":
                        dve.wait_ge(squared, 2 * TT + 4 * TT)
                        step(nc.vector.tensor_reduce(SS[:, 6:8], HSS, AX.X, ALU.add))
                        mean(RSTD[:, 6:8], SS[:, 6:8], D_MODEL)
                    elif what == "stream_scale":
                        q, = st[1:]
                        if q == 0:
                            root()
                        for i in range(TT):
                            c0 = slice(512 * q, 512 * (q + 1))
                            nc.vector.tensor_scalar(Y[:, i, c0], H[:, i, c0], RSTD[:, 6 + i:7 + i], None, ALU.mult)\
                                .then_inc(normed, 1)


_INS = ["x", "mem", "ln_pre", "ln_post", "ln_mem", "w_mem_kv", "gla_w_in", "gla_w_gate_lr", "gla_b_gate", "gla_norm",
        "gla_w_out", "nsa_w_in", "nsa_pe_k", "nsa_pe_v", "nsa_wk1", "nsa_wk2", "nsa_wv1", "nsa_wv2", "nsa_w_out"]


def kernel(**inputs):
    import numpy as _np
    import concourse.bacc as _bacc
    from concourse import mybir as _mybir
    from concourse.bass_utils import run_bass_kernel_spmd as _run

    nc = _bacc.Bacc("TRN2", target_bir_lowering=False, num_devices=1)
    arrays, args = {}, {}
    for name in _INS:
        v = _np.ascontiguousarray(inputs[name])
        arrays[f"in_{name}_dram"] = v
        args[name] = nc.dram_tensor(f"in_{name}_dram", v.shape, _mybir.dt.from_np(v.dtype), kind="ExternalInput").ap()
    out = nc.dram_tensor("out_0_dram", (1, SEQ, D_MODEL), _mybir.dt.float32, kind="ExternalOutput").ap()
    hybrid_trunk(nc, args, out)
    r = _run(nc, [arrays], core_ids=[0])
    return r.results[0]["out_0_dram"]
```
